# Optimizing a Trainium2 kernel written in Bass

```python
import math
import jax, jax.numpy as jnp
from jax import lax
import numpy as np

D_MODEL = 1024
BATCH = 1
SEQ = 512
DEPTH = 2

MEM_LEN = 256
N_MIXERS = 2
X_HEADS = 4
X_HEAD_DIM = 64
X_WIDTH = X_HEADS * X_HEAD_DIM
MIX_WIDTH = D_MODEL - X_WIDTH
M_HEADS = 4
M_HEAD_DIM = MIX_WIDTH // M_HEADS
M_CHUNK = 64
CONV_W = 4
D_HEADS = 6
D_HEAD_DIM = MIX_WIDTH // (2 * D_HEADS)
Q_BLOCK = 128
ROPE_THETA = 10000.0
FFN_HIDDEN = ((-(-8 * D_MODEL // 3)) + 255) // 256 * 256
A_IN = 4 * MIX_WIDTH + 2 * M_HEADS + X_WIDTH
B_IN = 3 * MIX_WIDTH + X_WIDTH
N_A = (DEPTH + 1) // 2
N_B = DEPTH // 2

kernel_name = "hybrid_mlstm_diffattn_memxattn"

def rmsnorm(x, g, eps=1e-6):
    xf = x.astype(jnp.float32)
    y = xf * lax.rsqrt(jnp.mean(xf * xf, axis=-1, keepdims=True) + eps)
    return (y * g.astype(jnp.float32)).astype(x.dtype)

def rope(x, pos):
    d = x.shape[-1]
    half = d // 2
    inv = jnp.power(ROPE_THETA, -jnp.arange(half, dtype=jnp.float32) * 2.0 / d)
    ang = pos.astype(jnp.float32)[..., None] * inv
    cos = jnp.cos(ang)[:, :, None, :]
    sin = jnp.sin(ang)[:, :, None, :]
    xf = x.astype(jnp.float32)
    x1, x2 = xf[..., :half], xf[..., half:]
    return jnp.concatenate([x1 * cos - x2 * sin, x2 * cos + x1 * sin], axis=-1).astype(x.dtype)

def causal_depthwise_conv(x, w, b):
    C = x.shape[-1]
    y = lax.conv_general_dilated(x, w[:, None, :].astype(x.dtype), window_strides=(1,),
                                 padding=[(CONV_W - 1, 0)],
                                 dimension_numbers=('NWC', 'WIO', 'NWC'),
                                 feature_group_count=C)
    return y + b.astype(x.dtype)

def mlstm_chunkwise(q, k, v, i_pre, f_pre):
    B, S, H, d = q.shape
    L = M_CHUNK
    NC = S // L
    to_chunks = lambda t: t.astype(jnp.float32).reshape(B, NC, L, H, d).transpose(1, 0, 3, 2, 4)
    qc, kc, vc = to_chunks(q), to_chunks(k), to_chunks(v)
    ic = i_pre.astype(jnp.float32).reshape(B, NC, L, H).transpose(1, 0, 3, 2)
    log_f = jax.nn.log_sigmoid(f_pre.astype(jnp.float32)).reshape(B, NC, L, H).transpose(1, 0, 3, 2)
    bc = jnp.cumsum(log_f, axis=-1)
    causal = jnp.tril(jnp.ones((L, L), dtype=bool))

    def step(carry, inp):
        C, n, m = carry
        qj, kj, vj, ij, bj = inp
        Dm = bj[..., :, None] - bj[..., None, :] + ij[..., None, :]
        Dm = jnp.where(causal, Dm, -jnp.inf)
        inter = bj + m[..., None]
        m_row = jnp.maximum(inter, jnp.max(Dm, axis=-1))
        Wt = jnp.exp(Dm - m_row[..., None])
        sc = jnp.exp(inter - m_row)
        Sw = jnp.einsum('bhld,bhsd->bhls', qj, kj) * Wt
        num = sc[..., None] * jnp.einsum('bhld,bhde->bhle', qj, C) + jnp.einsum('bhls,bhse->bhle', Sw, vj)
        den = sc * jnp.einsum('bhld,bhd->bhl', qj, n) + jnp.sum(Sw, axis=-1)
        h = num / jnp.maximum(jnp.abs(den), jnp.exp(-m_row))[..., None]
        m_new = m_row[..., -1]
        g = bj[..., -1:] - bj + ij
        wk = jnp.exp(g - m_new[..., None])
        decay = jnp.exp(bj[..., -1] + m - m_new)
        C_new = decay[..., None, None] * C + jnp.einsum('bhs,bhsd,bhse->bhde', wk, kj, vj)
        n_new = decay[..., None] * n + jnp.einsum('bhs,bhsd->bhd', wk, kj)
        return (C_new, n_new, m_new), h

    init = (jnp.zeros((B, H, d, d), jnp.float32), jnp.zeros((B, H, d), jnp.float32),
            jnp.zeros((B, H), jnp.float32))
    _, hs = lax.scan(step, init, (qc, kc, vc, ic, bc))
    return hs.transpose(1, 0, 3, 2, 4).reshape(B, S, H, d)

def mlstm_mixer(h, w_in, conv_w, conv_b, gate_b, head_norm):
    B, S, _ = h.shape
    p = h @ w_in
    qk_raw = p[..., :2 * MIX_WIDTH]
    v = p[..., 2 * MIX_WIDTH:3 * MIX_WIDTH]
    o = p[..., 3 * MIX_WIDTH:4 * MIX_WIDTH]
    gates = p[..., 4 * MIX_WIDTH:4 * MIX_WIDTH + 2 * M_HEADS] + gate_b.astype(p.dtype)
    xq = p[..., 4 * MIX_WIDTH + 2 * M_HEADS:]
    qk = jax.nn.silu(causal_depthwise_conv(qk_raw, conv_w, conv_b))
    q = qk[..., :MIX_WIDTH].reshape(B, S, M_HEADS, M_HEAD_DIM)
    k = qk[..., MIX_WIDTH:].reshape(B, S, M_HEADS, M_HEAD_DIM) * (M_HEAD_DIM ** -0.5)
    v = v.reshape(B, S, M_HEADS, M_HEAD_DIM)
    i_pre, f_pre = gates[..., :M_HEADS], gates[..., M_HEADS:]
    hs = mlstm_chunkwise(q, k, v, i_pre, f_pre)
    hs = rmsnorm(hs, head_norm).reshape(B, S, MIX_WIDTH).astype(h.dtype)
    return hs * jax.nn.sigmoid(o), xq

def diff_attention(h, positions, w_in, q_norm, k_norm, lam_vecs, subln, lambda_init):
    B, S, _ = h.shape
    p = h @ w_in
    q = p[..., :MIX_WIDTH].reshape(B, S, 2 * D_HEADS, D_HEAD_DIM)
    k = p[..., MIX_WIDTH:2 * MIX_WIDTH].reshape(B, S, 2 * D_HEADS, D_HEAD_DIM)
    v = p[..., 2 * MIX_WIDTH:3 * MIX_WIDTH].reshape(B, S, D_HEADS, 2 * D_HEAD_DIM)
    xq = p[..., 3 * MIX_WIDTH:]
    q = rope(rmsnorm(q, q_norm), positions)
    k = rope(rmsnorm(k, k_norm), positions)
    lv = lam_vecs.astype(jnp.float32)
    lam = jnp.exp(jnp.sum(lv[0] * lv[1])) - jnp.exp(jnp.sum(lv[2] * lv[3])) + lambda_init
    qh = q.transpose(0, 2, 1, 3)
    kh = k.transpose(0, 2, 1, 3)
    vh = v.transpose(0, 2, 1, 3)
    NB = S // Q_BLOCK
    qb = qh.reshape(B, 2 * D_HEADS, NB, Q_BLOCK, D_HEAD_DIM).transpose(2, 0, 1, 3, 4)
    key_idx = jnp.arange(S)
    scale = D_HEAD_DIM ** -0.5

    def block(args):
        qblk, bi = args
        s = jnp.einsum('bhqd,bhkd->bhqk', qblk, kh).astype(jnp.float32) * scale
        q_idx = bi * Q_BLOCK + jnp.arange(Q_BLOCK)
        s = jnp.where(key_idx[None, :] <= q_idx[:, None], s, -jnp.inf)
        pr = jax.nn.softmax(s, axis=-1).reshape(B, D_HEADS, 2, Q_BLOCK, S)
        a = (pr[:, :, 0] - lam * pr[:, :, 1]).astype(vh.dtype)
        return jnp.einsum('bhqk,bhke->bhqe', a, vh)

    o = lax.map(block, (qb, jnp.arange(NB)))
    o = o.transpose(1, 0, 3, 2, 4).reshape(B, S, D_HEADS, 2 * D_HEAD_DIM)
    o = rmsnorm(o, subln) * (1.0 - lambda_init)
    return o.reshape(B, S, MIX_WIDTH), xq

def memory_cross_attention(xq, mem, mem_norm, w_mem_kv, q_norm, k_norm):
    B, S, _ = xq.shape
    q = rmsnorm(xq.reshape(B, S, X_HEADS, X_HEAD_DIM), q_norm)
    kv = rmsnorm(mem, mem_norm) @ w_mem_kv
    M = kv.shape[1]
    k = rmsnorm(kv[..., :X_WIDTH].reshape(B, M, X_HEADS, X_HEAD_DIM), k_norm)
    v = kv[..., X_WIDTH:].reshape(B, M, X_HEADS, X_HEAD_DIM)
    s = jnp.einsum('bshd,bmhd->bhsm', q, k).astype(jnp.float32) * (X_HEAD_DIM ** -0.5)
    pr = jax.nn.softmax(s, axis=-1).astype(v.dtype)
    return jnp.einsum('bhsm,bmhd->bshd', pr, v).reshape(B, S, X_WIDTH)

def setup_inputs(seed: int = 0) -> dict:
    key = jax.random.key(seed)
    ks = jax.random.split(key, 32)
    f32 = jnp.float32
    nrm = lambda k, shape, s: jax.random.normal(k, shape, f32) * s
    gain = lambda k, shape: 1.0 + 0.02 * jax.random.normal(k, shape, f32)
    x = jax.random.normal(ks[0], (BATCH, SEQ, D_MODEL), f32)
    mem = jax.random.normal(ks[1], (BATCH, MEM_LEN, D_MODEL), f32)
    offset = jax.random.randint(ks[2], (BATCH, 1), 0, 1024, dtype=jnp.int32)
    positions = offset + jnp.arange(SEQ, dtype=jnp.int32)[None, :]
    i_bias = 0.1 * jax.random.normal(ks[22], (N_A, M_HEADS), f32)
    f_bias = jnp.linspace(3.0, 6.0, M_HEADS, dtype=f32)[None, :] + 0.1 * jax.random.normal(ks[23], (N_A, M_HEADS), f32)
    return {
        "x": x,
        "mem": mem,
        "positions": positions,
        "norm1": gain(ks[3], (DEPTH, D_MODEL)),
        "w_out": nrm(ks[4], (DEPTH, D_MODEL, D_MODEL), D_MODEL ** -0.5),
        "xq_norm": gain(ks[5], (DEPTH, X_HEAD_DIM)),
        "xk_norm": gain(ks[6], (DEPTH, X_HEAD_DIM)),
        "mem_norm": gain(ks[7], (DEPTH, D_MODEL)),
        "w_mem_kv": nrm(ks[8], (DEPTH, D_MODEL, 2 * X_WIDTH), D_MODEL ** -0.5),
        "norm2": gain(ks[9], (DEPTH, D_MODEL)),
        "w_gate_up": nrm(ks[10], (DEPTH, D_MODEL, 2 * FFN_HIDDEN), D_MODEL ** -0.5),
        "w_down": nrm(ks[11], (DEPTH, FFN_HIDDEN, D_MODEL), FFN_HIDDEN ** -0.5),
        "a_w_in": nrm(ks[12], (N_A, D_MODEL, A_IN), D_MODEL ** -0.5),
        "a_conv_w": nrm(ks[13], (N_A, CONV_W, 2 * MIX_WIDTH), CONV_W ** -0.5),
        "a_conv_b": nrm(ks[14], (N_A, 2 * MIX_WIDTH), 0.02),
        "a_gate_b": jnp.concatenate([i_bias, f_bias], axis=-1),
        "a_head_norm": gain(ks[15], (N_A, M_HEADS, M_HEAD_DIM)),
        "b_w_in": nrm(ks[16], (N_B, D_MODEL, B_IN), D_MODEL ** -0.5),
        "b_q_norm": gain(ks[17], (N_B, D_HEAD_DIM)),
        "b_k_norm": gain(ks[18], (N_B, D_HEAD_DIM)),
        "b_lambda": nrm(ks[19], (N_B, 4, D_HEAD_DIM), 0.1),
        "b_subln": gain(ks[20], (N_B, 2 * D_HEAD_DIM)),
    }

def reference(x, mem, positions, norm1, w_out, xq_norm, xk_norm, mem_norm, w_mem_kv, norm2,
              w_gate_up, w_down, a_w_in, a_conv_w, a_conv_b, a_gate_b, a_head_norm,
              b_w_in, b_q_norm, b_k_norm, b_lambda, b_subln):
    for i in range(DEPTH):
        j = i // N_MIXERS
        h = rmsnorm(x, norm1[i])
        if i % N_MIXERS == 0:
            mix, xq = mlstm_mixer(h, a_w_in[j], a_conv_w[j], a_conv_b[j], a_gate_b[j], a_head_norm[j])
        else:
            lambda_init = 0.8 - 0.6 * math.exp(-0.3 * i)
            mix, xq = diff_attention(h, positions, b_w_in[j], b_q_norm[j], b_k_norm[j],
                                     b_lambda[j], b_subln[j], lambda_init)
        xo = memory_cross_attention(xq, mem, mem_norm[i], w_mem_kv[i], xq_norm[i], xk_norm[i])
        x = x + jnp.concatenate([mix, xo], axis=-1) @ w_out[i]
        h = rmsnorm(x, norm2[i])
        gu = h @ w_gate_up[i]
        x = x + (jax.nn.silu(gu[..., :FFN_HIDDEN]) * gu[..., FFN_HIDDEN:]) @ w_down[i]
    return x


_drawn_inputs = setup_inputs


def setup_inputs(seed=0):
    import zlib

    import numpy as np

    out = dict(_drawn_inputs(seed))
    spreads = {}
    factors = {'xq_norm': 8.0,
     'xk_norm': 8.0,
     'mem_norm': 8.0,
     'norm2': 2.951,
     'a_conv_b': 7.073,
     'a_head_norm': 4.744,
     'b_q_norm': 8.0,
     'b_k_norm': 8.0,
     'b_subln': 6.802}
    for name, (base, spread) in spreads.items():
        noise = np.random.default_rng([zlib.crc32(name.encode()), seed]).standard_normal(out[name].shape)
        drawn = base * np.exp(spread * noise) if base else spread * noise
        out[name] = __import__('jax').numpy.asarray(drawn.astype(out[name].dtype))
    for name, factor in factors.items():
        out[name] = (out[name] * factor).astype(out[name].dtype)
    return out
```

```python
import math
from contextlib import ExitStack

import concourse.bass as bass
import numpy as np
from concourse import mybir

F32 = mybir.dt.float32
F32R = mybir.dt.float32r
I32 = mybir.dt.int32
ALU = mybir.AluOpType
ACT = mybir.ActivationFunctionType
AX = mybir.AxisListType

P = 128
D = 1024
SEQ = 512
MEM = 256
KD = D // P
NT = SEQ // P
MT_TILES = MEM // P
MIX = 768
XW = 256
XH_DIM = 64
MH = 4
MHD = MIX // MH
CONV = 4
QKC = 2 * MIX // P
MC = MIX // P
FFN = 2816
HC = FFN // P
A_IN = 4 * MIX + 2 * MH + XW
B_IN = 3 * MIX + XW
GATE_COL = 4 * MIX
XQ_COL_A = 4 * MIX + 2 * MH
LAMBDA_INIT = 0.8 - 0.6 * math.exp(-0.3 * 1)
EPS = 1e-6
RAW = 4
SPLIT = 2

R_N1, R_N2, R_MN, R_CW, R_CB, R_HN, R_SL, R_XQ, R_XK, R_BQ, R_BK = 0, 16, 32, 48, 96, 108, 114, 115, 117, 119, 120
N_PRM = 121

C_ID, C_BD, C_ROT, C_NEG, C_BIG, C_SEL, C_GSEL, C_INV = 0, 128, 256, 384, 512, 640, 640 + MH * P, 640 + MH * P + 8
N_CON = C_INV + 1


def constants():
    c = np.zeros((P, N_CON), np.float32)
    r = np.arange(P)
    c[:, C_ID:C_ID + P] = np.eye(P)
    c[:, C_BD:C_BD + P] = r[:, None] // 64 == r[None, :] // 64
    rot = np.zeros((P, P), np.float32)
    for j in range(P):
        rot[j + 32 if j % 64 < 32 else j - 32, j] = -1.0 if j % 64 < 32 else 1.0
    c[:, C_ROT:C_ROT + P] = rot
    c[:, C_NEG:C_NEG + P] = np.where(r[None, :] > r[:, None], -1e30, 0.0)
    c[:, C_BIG:C_BIG + P] = np.where(r[None, :] < r[:, None], 1e30, 0.0)
    for h in range(MH):
        c[h, C_SEL + h * P:C_SEL + (h + 1) * P] = 1.0
    for j in range(8):
        c[j, C_GSEL + j] = 1.0
    inv = np.power(np.float32(10000.0), -np.arange(32, dtype=np.float32) * np.float32(2.0) / np.float32(64))
    c[:, C_INV] = inv[r % 32]
    return c


T_MEM = 0
T_GATE = T_MEM + 8
T_QK = T_GATE + 1
T_O = T_QK + QKC
T_V = T_O + MC
T_XA = T_V + MC
T_OUT = [T_XA + 2, 0]
SEG = [(0, 8), (8, 8), (16, 6)]
N_FFN = 2 * HC + KD * len(SEG)
T_FFN = [T_OUT[0] + KD, 0]
T_B = T_FFN[0] + N_FFN
T_XB = T_B + 3 * MC
T_OUT[1] = T_XB + 2
T_FFN[1] = T_OUT[1] + KD
N_TILES = T_FFN[1] + N_FFN


def seg_base(layer, s):
    return T_FFN[layer] + sum(2 * n + KD for _, n in SEG[:s])


def tile_k(n):
    for layer in range(2):
        for s, (_, nh) in enumerate(SEG):
            down = seg_base(layer, s) + 2 * nh
            if down <= n < down + KD:
                return nh
    return 8


def hybrid_trunk(nc, x, mem, positions, norm1, w_out, xq_norm, xk_norm, mem_norm, w_mem_kv, norm2,
                 w_gate_up, w_down, a_w_in, a_conv_w, a_conv_b, a_gate_b, a_head_norm,
                 b_w_in, b_q_norm, b_k_norm, b_lambda, b_subln, con, out):
    ctx = ExitStack()
    with ctx:
        def sb(name, shape, dt=F32, scope=ctx):
            return scope.enter_context(nc.sbuf_tensor(name, shape, dt))

        def sem(name):
            return ctx.enter_context(nc.semaphore(name))

        PS = ctx.enter_context(nc.psum_tensor("PS", [P, 8, 512], F32))

        xT = sb("xT", [P, KD, SEQ])
        Hh = sb("Hh", [P, KD, SEQ], F32R)
        Hl = sb("Hl", [P, KD, SEQ], F32R)
        Ah = sb("Ah", [P, 8, SEQ], F32R)
        Al = sb("Al", [P, 8, SEQ], F32R)
        w_raw = sb("w_raw", [P, RAW, 8, P])
        w_hi = sb("w_hi", [P, SPLIT, 8, P], F32R)
        w_lo = sb("w_lo", [P, SPLIT, 8, P], F32R)
        cn = sb("cn", [P, N_CON])
        ones = sb("ones", [P, P])
        gcol = sb("gcol", [P, N_PRM])
        gx = sb("gx", [P, 4])
        epsc = sb("epsc", [P, 1])
        hpi = sb("hpi", [P, 1])
        rinv = sb("rinv", [P, SEQ])
        acc = sb("acc", [P, SEQ])
        xk = sb("xk", [P, 2, 2, MEM])
        xv = sb("xv", [P, 2, MT_TILES, XW])
        lam = sb("lam", [P, 1])
        lame = sb("lame", [1, 4])
        ident = cn[:, C_ID:C_ID + P]
        bdiag = cn[:, C_BD:C_BD + P]
        rotm = cn[:, C_ROT:C_ROT + P]
        neg_mask = cn[:, C_NEG:C_NEG + P]
        big_mask = cn[:, C_BIG:C_BIG + P]

        tmp = [sb(f"tmp{i}", [P, 516]) for i in range(8)]

        s0 = ExitStack()
        x_st = sb("x_st", [P, NT, D], scope=s0)
        m_st = sb("m_st", [P, MT_TILES, D], scope=s0)
        prm = sb("prm", [P, P], scope=s0)
        mT = sb("mT", [P, KD, MEM], scope=s0)
        msq = sb("msq", [P, KD, MEM], scope=s0)
        macc = sb("macc", [P, MEM], scope=s0)
        rm = sb("rm", [P, MEM], scope=s0)
        kv = sb("kv", [P, 2, 4, MEM], scope=s0)
        kvs = sb("kvs", [P, 512], scope=s0)
        lamv = sb("lamv", [1, 4, 64], scope=s0)
        lamw = sb("lamw", [1, 2, 64], scope=s0)
        s0.close()
        sA = ExitStack()
        QK = sb("QK", [P, QKC, SEQ], scope=sA)
        V = sb("V", [P, NT, MIX], scope=sA)
        SO = sb("SO", [P, MC, SEQ], scope=sA)
        xqA = sb("xqA", [P, 2, SEQ], scope=sA)
        WT = sb("WT", [P, 1280], scope=sA)
        Mrow = sb("Mrow", [MH, SEQ], scope=sA)
        mrow = sb("mrow", [MH, SEQ], scope=sA)
        aT = sb("aT", [P, NT, MH], scope=sA)
        gb = sb("gb", [MH, 2], scope=sA)
        nmA = sb("nmA", [P, 16], scope=sA)
        rsA = sb("rsA", [P, 16], scope=sA)
        sA.close()
        sB = ExitStack()
        QKP = sb("QKP", [P, 2, 2, SEQ], scope=sB)
        VB = sb("VB", [P, 2, NT, P], scope=sB)
        PB = sb("PB", [P, 2, 1280], scope=sB)
        ATB = sb("ATB", [P, NT, SEQ], scope=sB)
        QS = sb("QS", [P, 2, SEQ], scope=sB)
        QT = sb("QT", [P, 2, SEQ], scope=sB)
        QR = sb("QR", [P, 2, SEQ], scope=sB)
        cosT = sb("cosT", [P, SEQ], scope=sB)
        sinT = sb("sinT", [P, SEQ], scope=sB)
        xqB = sb("xqB", [P, 2, SEQ], scope=sB)
        nmB = sb("nmB", [P, 64], scope=sB)
        rsB = sb("rsB", [P, 64], scope=sB)
        posi = sb("posi", [P, SEQ], I32, scope=sB)
        nmX = sb("nmX", [P, 16], scope=sB)
        rsX = sb("rsX", [P, 16], scope=sB)
        sB.close()
        sC = ExitStack()
        o_st = sb("o_st", [P, 2, NT, P], scope=sC)
        sC.close()

        w_in = [sem(f"w_in{i}") for i in range(RAW)]
        w_round = sem("w_round")
        w_split = sem("w_split")
        dense_done = sem("dense_done")
        dense_free = sem("dense_free")
        con_in = sem("con_in")
        prm_in = sem("prm_in")
        mem_in = sem("mem_in")
        x_in = sem("x_in")
        set_done = sem("set_done")
        prm_t = sem("prm_t")
        g_ready = sem("g_ready")
        tr_done = sem("tr_done")
        tr_free = sem("tr_free")
        msq_done = sem("msq_done")
        macc_done = sem("macc_done")
        mss_done = sem("mss_done")
        mstd_done = sem("mstd_done")
        mhi = sem("mhi")
        mg_ready = sem("mg_ready")
        ksq = sem("ksq")
        kss = sem("kss")
        kstd = sem("kstd")
        kn_ready = sem("kn_ready")
        vtr = sem("vtr")
        vtr_out = sem("vtr_out")
        vch = sem("vch")
        ach = sem("ach")
        xsq = sem("xsq")
        xsq_used = sem("xsq_used")
        h_hi = sem("h_hi")
        h_ready = sem("h_ready")
        ss_done = sem("ss_done")
        std_done = sem("std_done")
        gt_ready = sem("gt_ready")
        gsel_done = sem("gsel_done")
        lnf_done = sem("lnf_done")
        a_ready = sem("a_ready")
        at_done = sem("at_done")
        at_ready = sem("at_ready")
        conv_done = sem("conv_done")
        conv_step = sem("conv_step")
        qk_ready = sem("qk_ready")
        o_gate = sem("o_gate")
        vT_done = sem("vT_done")
        v_ready = sem("v_ready")
        mbc_done = sem("mbc_done")
        s_done = sem("s_done")
        dg_ready = sem("dg_ready")
        em_done = sem("em_done")
        wt_ready = sem("wt_ready")
        p_ready = sem("p_ready")
        num_done = sem("num_done")
        den_abs = sem("den_abs")
        hn_ready = sem("hn_ready")
        hsq = sem("hsq")
        hss = sem("hss")
        hstd = sem("hstd")
        mix_t = sem("mix_t")
        mix_hi = sem("mix_hi")
        mix_lo = sem("mix_lo")
        xq_sq = sem("xq_sq")
        xq_ss = sem("xq_ss")
        xq_std = sem("xq_std")
        xqn = sem("xqn")
        xs_done = sem("xs_done")
        xmax = sem("xmax")
        xexp = sem("xexp")
        xp_ready = sem("xp_ready")
        xpt_done = sem("xpt_done")
        xpt_ready = sem("xpt_ready")
        xo_done = sem("xo_done")
        xo_hi = sem("xo_hi")
        xo_ready = sem("xo_ready")
        silu_done = sem("silu_done")
        gu_ready = sem("gu_ready")
        f_hi = sem("f_hi")
        f_ready = sem("f_ready")
        pos_in = sem("pos_in")
        lam_in = sem("lam_in")
        lam_s = sem("lam_s")
        lam_e = sem("lam_e")
        lam_d = sem("lam_d")
        lam_b = sem("lam_b")
        ang = sem("ang")
        trig = sem("trig")
        bsq = sem("bsq")
        bss = sem("bss")
        bstd = sem("bstd")
        bn_ready = sem("bn_ready")
        brot = sem("brot")
        bqr = sem("bqr")
        bvt_done = sem("bvt_done")
        bv_ready = sem("bv_ready")
        bs_done = sem("bs_done")
        bmax = sem("bmax")
        bexp = sem("bexp")
        ba_ready = sem("ba_ready")
        bt_done = sem("bt_done")
        bat_ready = sem("bat_ready")
        bpv = sem("bpv")
        bosq = sem("bosq")
        boss = sem("boss")
        bostd = sem("bostd")
        bmix_t = sem("bmix_t")
        bmix_hi = sem("bmix_hi")
        bmix_lo = sem("bmix_lo")
        ot_done = sem("ot_done")
        ot_out = sem("ot_out")
        o_store = [sem("o_store0"), sem("o_store1")]

        def wview(w, r0, nk, col):
            return w[r0:r0 + nk * P, :].rearrange("(k p) n -> p k n", p=P)[:, :, bass.ds(col, P)]

        kvw = [w_mem_kv[l] for l in range(2)]
        aw, bw = a_w_in[0], b_w_in[0]

        FULL = [0, 2, 3, 5]
        HALF = [(1, 0), (1, 64), (4, 0), (4, 64)]
        W_OFF = [0, 512, 896, 1152]

        S_BANK = [2, 3, 6, 7]
        SS_BANK = 7

        block = ctx.enter_context(nc.Block())

        @block.sync
        def _(sp):
            sp.dma_start(m_st[:], mem[0].rearrange("(t p) n -> p t n", p=P)).then_inc(mem_in, 16)

            def load(n, slot, src, nk, first=False):
                if not first:
                    sp.wait_ge(w_split, n - (RAW - 1))
                sp.dma_start(w_raw[:, slot, 0:nk, :], src).then_inc(w_in[slot], 16)

            def run(base, count, w, r0, nk, col, step4=None):
                loops = count // 4 if step4 else 0
                if loops > 1:
                    with sp.Fori(0, loops) as i:
                        for s in range(4):
                            load(i * 4 + (base + s), (base + s) % RAW, wview(w, r0, nk, i * step4 + col(s)), nk)
                    done = loops * 4
                else:
                    done = 0
                for j in range(done, count):
                    load(base + j, (base + j) % RAW, wview(w, r0, nk, col(j)), nk)

            for n in range(RAW):
                load(n, n, wview(kvw[0], 0, 8, n * P), 8, first=True)
            sp.dma_start(x_st[:], x[0].rearrange("(t p) n -> p t n", p=P)).then_inc(x_in, 16)
            for n in range(4, 8):
                load(n, n % RAW, wview(kvw[1], 0, 8, (n - 4) * P), 8)
            run(T_GATE, 1, aw, 0, 8, lambda j: GATE_COL)
            run(T_QK, QKC, aw, 0, 8, lambda j: j * P, 4 * P)
            run(T_O, MC, aw, 0, 8, lambda j: 3 * MIX + j * P)
            run(T_V, MC, aw, 0, 8, lambda j: 2 * MIX + j * P)
            run(T_XA, 2, aw, 0, 8, lambda j: XQ_COL_A + j * P)
            for layer in range(2):
                if layer == 1:
                    for c in range(MC):
                        for j in range(3):
                            n = T_B + 3 * c + j
                            load(n, n % RAW, wview(bw, 0, 8, j * MIX + c * P), 8)
                    run(T_XB, 2, bw, 0, 8, lambda j: 3 * MIX + j * P)
                run(T_OUT[layer], KD, w_out[layer], 0, 8, lambda j: j * P, 4 * P)
                for s, (h0, nh) in enumerate(SEG):
                    base = seg_base(layer, s)
                    run(base, 2 * nh, w_gate_up[layer], 0, 8,
                        lambda j, h0=h0: (h0 + j // 2) * P + (j % 2) * FFN, 2 * P)
                    run(base + 2 * nh, KD, w_down[layer], h0 * P, nh, lambda j: j * P, 4 * P)
            ov = out[0].rearrange("(t p) n -> p t n", p=P)
            for k in range(KD):
                sp.wait_ge(ot_out, k + 1)
                sp.dma_start(ov[:, :, k * P:(k + 1) * P], o_st[:, k % 2]).then_inc(o_store[k % 2], 16)
            for j in range(2):
                sp.wait_ge(o_store[j], 16 * KD // 2)

        @block.gpsimd
        def _(pool):
            nc.gpsimd.memset(ones[:], 1.0).then_inc(set_done, 1)
            nc.gpsimd.memset(epsc[:], EPS).then_inc(set_done, 1)
            nc.gpsimd.memset(hpi[:], math.pi / 2).then_inc(set_done, 1)

            for n in range(N_TILES):
                raw, sl, nk = n % RAW, n % SPLIT, tile_k(n)
                pool.wait_ge(w_in[raw], (n // RAW + 1) * 16)
                if n >= SPLIT:
                    pool.wait_ge(dense_done, n - SPLIT + 1)
                nc.gpsimd.tensor_scalar(w_hi[:, sl, 0:nk], w_raw[:, raw, 0:nk], 0.0, 1.0, ALU.add,
                                        ALU.mult).then_inc(w_round, 1)
                pool.wait_ge(w_round, n + 1)
                nc.gpsimd.tensor_tensor(w_lo[:, sl, 0:nk], w_raw[:, raw, 0:nk],
                                        w_hi[:, sl, 0:nk].bitcast(F32), ALU.subtract).then_inc(w_split, 1)

        @block.scalar
        def _(act):
            link_n = [0]

            def link(ins):
                link_n[0] += 1
                ins.then_inc(ach, 1)
                act.wait_ge(ach, link_n[0])

            act.dma_start(cn[:], con).then_inc(con_in, 16)
            rows = [(R_N1, norm1.rearrange("l (k p) -> (l k) p", p=P)),
                    (R_N2, norm2.rearrange("l (k p) -> (l k) p", p=P)),
                    (R_MN, mem_norm.rearrange("l (k p) -> (l k) p", p=P)),
                    (R_CW, a_conv_w[0].rearrange("w (c p) -> (w c) p", p=P)),
                    (R_CB, a_conv_b.rearrange("a (c p) -> (a c) p", p=P)),
                    (R_HN, a_head_norm.rearrange("a h d -> (a h d)").rearrange("(c p) -> c p", p=P)),
                    (R_SL, b_subln)]
            for r, v in rows:
                act.dma_start(prm[r:r + v.shape[0], :], v).then_inc(prm_in, 16)
            n_in = len(rows)
            for r, v in ((R_XQ, xq_norm), (R_XK, xk_norm), (R_BQ, b_q_norm), (R_BK, b_k_norm)):
                for half in range(2):
                    act.dma_start(prm[r:r + v.shape[0], half * 64:half * 64 + 64], v).then_inc(prm_in, 16)
                    n_in += 1
            assert n_in == 15
            act.dma_start(lamv[:], b_lambda).then_inc(lam_in, 16)
            with nc.allow_non_contiguous_dma(reason="eight gate biases, once"):
                act.dma_start(gb[:], a_gate_b.rearrange("a (g h) -> h (a g)", g=2)).then_inc(prm_in, 16)

            def tr_out(g, dst):
                act.wait_ge(tr_done, g + 1)
                nc.scalar.activation(dst, PS[:, 4 + g % 4], ACT.Copy).then_inc(tr_free, 1)

            for g in range(4):
                tr_out(g, mT[:, 2 * g:2 * g + 2].rearrange("p a n -> p (a n)"))
            act.wait_ge(tr_free, 4)
            nc.scalar.activation(msq[:], mT[:], ACT.Square).then_inc(msq_done, 1)
            act.wait_ge(g_ready, 1)
            for l in range(2):
                for k in range(KD):
                    nc.scalar.activation(Ah[:, 4 * l:4 * l + 4].rearrange("p a n -> p (a n)")[:, k * MEM:(k + 1) * MEM],
                                         mT[:, k], ACT.Copy,
                                         scale=gcol[:, R_MN + 8 * l + k:R_MN + 8 * l + k + 1]).then_inc(mhi, 1)
            for g in range(4, 8):
                tr_out(g, xT[:, g - 4])
            act.wait_ge(lam_s, 1)
            nc.scalar.activation(lame[0:1, 2:4], lame[0:1, 0:2], ACT.Exp).then_inc(lam_e, 1)
            act.wait_ge(mss_done, 1)
            act.wait_ge(set_done, 3)
            nc.scalar.activation(rm[:], PS[:, 3, 0:MEM], ACT.Sqrt, scale=1.0 / D, bias=epsc[:]).then_inc(mstd_done, 1)

            xn = [0]

            def x_chunk(k, grow):
                n = xn[0]
                xn[0] += 1
                if n >= 2:
                    act.wait_ge(xsq_used, n - 1)
                nc.scalar.activation(tmp[6 + n % 2][:, 0:SEQ], xT[:, k], ACT.Square).then_inc(xsq, 1)
                nc.scalar.activation(Hh[:, k], xT[:, k], ACT.Copy,
                                     scale=gcol[:, grow + k:grow + k + 1]).then_inc(h_hi, 1)

            def x_std(i):
                act.wait_ge(ss_done, i + 1)
                nc.scalar.activation(rinv[:], PS[:, SS_BANK], ACT.Sqrt, scale=1.0 / D, bias=epsc[:]).then_inc(std_done, 1)

            for k in range(4):
                act.wait_ge(tr_free, 5 + k)
                x_chunk(k, R_N1)
            for g in range(8, 12):
                tr_out(g, xT[:, g - 4])
            for k in range(4, 8):
                act.wait_ge(tr_free, 5 + k)
                x_chunk(k, R_N1)

            for l in range(2):
                act.wait_ge(dense_free, 4 * l + 2)
                nc.scalar.activation(kvs[:], kv[:, l, 0:2].rearrange("p a n -> p (a n)"), ACT.Square).then_inc(ksq, 1)
                act.wait_ge(kss, l + 1)
                nc.scalar.activation(kvs[:], PS[:, 4 + l], ACT.Sqrt, scale=1.0 / XH_DIM, bias=epsc[:]).then_inc(kstd, 1)
                act.wait_ge(vtr, l + 1)
                nc.scalar.activation(xv[:, l].rearrange("p a n -> p (a n)"), PS[:, 6], ACT.Copy).then_inc(vtr_out, 1)
                if l == 0:
                    act.wait_ge(kn_ready, 1)
            x_std(0)

            act.wait_ge(gsel_done, 1)
            nc.scalar.activation(tmp[0][0:MH, 0:SEQ], PS[0:MH, 3], ACT.Identity, bias=gb[:, 1:2]).then_inc(ach, 1)
            link_n[0] += 1
            act.wait_ge(ach, link_n[0])
            link(nc.scalar.activation(tmp[1][0:MH, 0:SEQ], tmp[0][0:MH, 0:SEQ], ACT.Abs))
            link(nc.scalar.activation(tmp[1][0:MH, 0:SEQ], tmp[1][0:MH, 0:SEQ], ACT.Exp, scale=-1.0))
            nc.scalar.activation(tmp[1][0:MH, 0:SEQ], tmp[1][0:MH, 0:SEQ], ACT.Ln, bias=1.0).then_inc(lnf_done, 1)
            with act.Fori(0, QKC) as c:
                act.wait_ge(conv_done, c + 1)
                nc.scalar.activation(QK[:, bass.ds(c, 1)], QK[:, bass.ds(c, 1)], ACT.Silu).then_inc(qk_ready, 1)
            act.wait_ge(dense_free, T_O + MC)
            nc.scalar.activation(SO[:], SO[:], ACT.Sigmoid).then_inc(o_gate, 1)
            for c in range(MC):
                act.wait_ge(vT_done, c + 1)
                nc.scalar.activation(V[:, :, c * P:(c + 1) * P], PS[:, 4 + c % 2].rearrange("p (t n) -> p t n", t=NT),
                                     ACT.Copy).then_inc(v_ready, 1)

            def head_weights(h):
                act.wait_ge(mbc_done, 2 * h + 2)
                if h >= 1:
                    act.wait_ge(hn_ready, h)
                nc.scalar.activation(tmp[0][:, 0:SEQ], PS[:, 5], ACT.Exp, scale=-1.0).then_inc(em_done, 1)
                act.wait_ge(dg_ready, h + 1)
                act.wait_ge(at_ready, 1)
                if h >= 1:
                    act.wait_ge(num_done, h)
                for s in range(NT):
                    a = aT[:, s, h:h + 1]
                    nc.scalar.activation(WT[:, W_OFF[s]:W_OFF[s] + P], tmp[1][:, s * P:(s + 1) * P], ACT.Exp,
                                         scale=-1.0, bias=a).then_inc(wt_ready, 1)
                    if s < NT - 1:
                        nc.scalar.activation(WT[:, W_OFF[s] + P:W_OFF[s] + SEQ - s * P], PS[:, 4, (s + 1) * P:SEQ],
                                             ACT.Exp, scale=-1.0, bias=a).then_inc(wt_ready, 1)
                    else:
                        pass

            def head_den(h):
                act.wait_ge(num_done, h + 1)
                nc.scalar.activation(tmp[2][:, 0:SEQ], PS[:, 5], ACT.Abs).then_inc(den_abs, 1)

            def head_sq(h):
                f, (c, r) = FULL[h], HALF[h]
                act.wait_ge(hn_ready, h + 1)
                if h >= 1:
                    act.wait_ge(hss, h)
                nc.scalar.activation(tmp[3][:, 0:SEQ], QK[:, f], ACT.Square).then_inc(hsq, 1)
                nc.scalar.activation(tmp[4][r:r + 64, 0:SEQ], QK[r:r + 64, c], ACT.Square).then_inc(hsq, 1)

            def head_std(h):
                act.wait_ge(hss, h + 1)
                if h >= 1:
                    act.wait_ge(mix_t, 2 * h)
                nc.scalar.activation(tmp[5][:, 0:SEQ], PS[:, 0], ACT.Sqrt, scale=1.0 / MHD, bias=epsc[:]).then_inc(hstd, 1)

            def head_hi(h):
                f, (c, r) = FULL[h], HALF[h]
                act.wait_ge(mix_t, 2 * h + 1)
                nc.scalar.activation(Ah[:, f], QK[:, f], ACT.Copy).then_inc(mix_hi, 1)
                act.wait_ge(mix_t, 2 * h + 2)
                nc.scalar.activation(Ah[r:r + 64, c], QK[r:r + 64, c], ACT.Copy).then_inc(mix_hi, 1)

            for h in range(MH):
                head_weights(h)
                head_den(h)
                head_sq(h)
                head_std(h)
                head_hi(h)

            def cross(l, xq, sq, Pb, PT, nm, rs):
                act.wait_ge(dense_free, (T_XA, T_XB)[l] + 2)
                nc.scalar.activation(sq, xq, ACT.Square).then_inc(xq_sq, 1)
                act.wait_ge(xq_ss, l + 1)
                nc.scalar.activation(sq, PS[:, 2:4], ACT.Sqrt, scale=1.0 / XH_DIM, bias=epsc[:]).then_inc(xq_std, 1)
                for c in range(2):
                    i = 2 * l + c
                    for hd in range(2):
                        for t in range(NT):
                            act.wait_ge(xmax, 4 * i + 2 * hd + t // 2 + 1)
                            if c == 1 and hd == 0 and t == 0:
                                act.wait_ge(xpt_done, 2 * l + 1)
                            j = 4 * hd + t
                            nc.scalar.activation(Pb[:, j], PS[:, 4 + 2 * hd + t // 2, (t % 2) * MEM:(t % 2 + 1) * MEM],
                                                 ACT.Exp, bias=nm[:, 8 * c + j:8 * c + j + 1],
                                                 accum_out=rs[:, 8 * c + j:8 * c + j + 1]).then_inc(xexp, 1)
                    act.wait_ge(xpt_done, i + 1)
                    if c == 1:
                        act.wait_ge(xo_done, 2 * l + 1)
                    for j in range(4):
                        nc.scalar.activation(PT[:, j], PS[:, 4 + j], ACT.Copy).then_inc(xpt_ready, 1)
                    act.wait_ge(xo_done, i + 1)
                    nc.scalar.activation(Ah[:, MC + c], PS[:, 2 + c], ACT.Copy).then_inc(xo_hi, 1)

            cross(0, xqA[:], SO[:, 0:2], QK[:, 6:10].rearrange("p a (b n) -> p (a b) n", b=2),
                  V[:].rearrange("p a n -> p (a n)")[:, 0:2048].rearrange("p (a n) -> p a n", a=4), nmA, rsA)

            def x_phase(grow, base):
                for k in range(KD):
                    act.wait_ge(dense_free, base + k + 1)
                    x_chunk(k, grow)

            def ffn(l):
                n0 = l * HC
                for s, (h0, nh) in enumerate(SEG):
                    base = seg_base(l, s)
                    with act.Fori(0, nh) as i:
                        act.wait_ge(dense_free, i * 2 + (base + 1))
                        nc.scalar.activation(tmp[0][:, 0:SEQ], tmp[1][:, 0:SEQ], ACT.Silu).then_inc(silu_done, 1)
                        act.wait_ge(gu_ready, i + (n0 + h0 + 1))
                        nc.scalar.activation(Ah[:, bass.ds(i, 1)], tmp[3][:, 0:SEQ].rearrange("p (a n) -> p a n", a=1),
                                             ACT.Copy).then_inc(f_hi, 1)

            x_phase(R_N2, T_OUT[0])
            x_std(1)
            ffn(0)
            act.dma_start(posi[:], positions.broadcast_to([P, SEQ])).then_inc(pos_in, 16)
            x_phase(R_N1 + 8, seg_base(0, 2) + 2 * SEG[2][1])
            x_std(2)
            act.wait_ge(ang, 1)
            nc.scalar.activation(sinT[:], QT[:, 0], ACT.Sin).then_inc(trig, 1)
            link(nc.scalar.activation(cosT[:], QT[:, 0], ACT.Abs))
            nc.scalar.activation(cosT[:], cosT[:], ACT.Sin, scale=-1.0, bias=hpi[:]).then_inc(trig, 1)

            def b_sq(c):
                act.wait_ge(dense_free, T_B + 3 * c + 2)
                if c >= 1:
                    act.wait_ge(bn_ready, c)
                nc.scalar.activation(QS[:], QKP[:, c % 2], ACT.Square).then_inc(bsq, 1)

            def b_std(c):
                act.wait_ge(bss, c + 1)
                nc.scalar.activation(QS[:], PS[:, 2:4], ACT.Sqrt, scale=1.0 / 64, bias=epsc[:]).then_inc(bstd, 1)

            def b_v(c):
                act.wait_ge(bvt_done, c + 1)
                if c >= 2:
                    act.wait_ge(bpv, c - 1)
                nc.scalar.activation(VB[:, c % 2], PS[:, 2].rearrange("p (t n) -> p t n", t=NT), ACT.Copy).then_inc(bv_ready, 1)

            def b_exp(c, u):
                t = NT - 1 - u
                n = 4 * c + u
                act.wait_ge(bmax, n + 1)
                if c >= 1:
                    act.wait_ge(bt_done, 4 * (c - 1) + u + 1)
                for hd in range(2):
                    j = (8 * c + 2 * u + hd) % 64
                    nc.scalar.activation(PB[:, hd, W_OFF[u]:W_OFF[u] + (t + 1) * P], PS[:, 4 + 2 * (u % 2) + hd, 0:(t + 1) * P],
                                         ACT.Exp, bias=nmB[:, j:j + 1], accum_out=rsB[:, j:j + 1]).then_inc(bexp, 1)

            def b_at(c, u):
                t = NT - 1 - u
                act.wait_ge(bt_done, 4 * c + u + 1)
                if c >= 1 and u == 0:
                    act.wait_ge(bpv, c)
                nc.scalar.activation(ATB[:, 0:t + 1, t * P:(t + 1) * P],
                                     PS[:, 2 + u % 2, 0:(t + 1) * P].rearrange("p (a n) -> p a n", n=P),
                                     ACT.Copy).then_inc(bat_ready, 1)

            def b_osq(c):
                act.wait_ge(bpv, c + 1)
                if c >= 1:
                    act.wait_ge(boss, c)
                nc.scalar.activation(tmp[6][:, 0:SEQ], PS[:, 4], ACT.Square).then_inc(bosq, 1)

            def b_ostd(c):
                act.wait_ge(boss, c + 1)
                if c >= 1:
                    act.wait_ge(bmix_t, c)
                nc.scalar.activation(tmp[7][:, 0:SEQ], PS[:, 5], ACT.Sqrt, scale=1.0 / P, bias=epsc[:]).then_inc(bostd, 1)
                act.wait_ge(bmix_t, c + 1)
                nc.scalar.activation(Ah[:, c], tmp[5][:, 0:SEQ], ACT.Copy).then_inc(bmix_hi, 1)

            b_sq(0)
            for c in range(MC):
                b_std(c)
                if c >= 1:
                    b_osq(c - 1)
                    b_ostd(c - 1)
                b_v(c)
                for u in range(NT):
                    b_exp(c, u)
                if c + 1 < MC:
                    b_sq(c + 1)
                for u in range(NT):
                    b_at(c, u)
            b_osq(MC - 1)
            b_ostd(MC - 1)
            act.wait_ge(bn_ready, MC)
            cross(1, xqB[:], QS[:], PB[:].rearrange("p a n -> p (a n)")[:, 0:2048].rearrange("p (a n) -> p a n", a=8), ATB[:], nmX, rsX)
            x_phase(R_N2 + 8, T_OUT[1])
            x_std(3)
            ffn(1)
            for k in range(KD):
                act.wait_ge(ot_done, k + 1)
                if k >= 2:
                    act.wait_ge(o_store[k % 2], 16 * (k // 2))
                nc.scalar.activation(o_st[:, k % 2].rearrange("p t n -> p (t n)"), PS[:, 2 + k % 2], ACT.Copy).then_inc(ot_out, 1)

        @block.vector
        def _(dve):
            link_n = [0]

            def link(ins):
                link_n[0] += 1
                ins.then_inc(vch, 1)
                dve.wait_ge(vch, link_n[0])

            def col(r):
                return gcol[:, r:r + 1]

            nc.vector.memset(tmp[2][:, 0:CONV - 1], 0.0)
            nc.vector.memset(tmp[3][:, 0:CONV - 1], 0.0)
            dve.wait_ge(lam_in, 16)
            link(nc.vector.tensor_tensor(lamw[:], lamv[0:1, 0:4:2], lamv[0:1, 1:4:2], ALU.mult))
            nc.vector.tensor_reduce(lame[0:1, 0:2], lamw[:], AX.X, ALU.add).then_inc(lam_s, 1)
            dve.wait_ge(prm_t, 1)
            nc.vector.tensor_copy(gcol[:], PS[:, 2, 0:N_PRM]).then_inc(g_ready, 1)
            dve.wait_ge(g_ready, 1)
            nc.vector.tensor_scalar(gx[:, 0:2], gcol[:, R_XQ:R_XQ + 2], XH_DIM ** -0.5, None, ALU.mult)
            nc.vector.tensor_scalar(gx[:, 2:3], col(R_BQ), 64 ** -0.5, None, ALU.mult)
            link(nc.vector.tensor_scalar(gx[:, 3:4], col(R_SL), 1.0 - LAMBDA_INIT, None, ALU.mult))
            dve.wait_ge(lam_e, 1)
            nc.vector.scalar_tensor_tensor(lame[0:1, 0:1], lame[0:1, 2:3], LAMBDA_INIT, lame[0:1, 3:4],
                                           ALU.add, ALU.subtract).then_inc(lam_d, 1)
            dve.wait_ge(msq_done, 1)
            nc.vector.tensor_reduce(macc[:], msq[:].rearrange("p k n -> p n k"), AX.X, ALU.add).then_inc(macc_done, 1)
            for l in range(2):
                for k in range(KD):
                    dve.wait_ge(mhi, 8 * l + k + 1)
                    lo, hi = (A[:, 4 * l:4 * l + 4].rearrange("p a n -> p (a n)")[:, k * MEM:(k + 1) * MEM] for A in (Al, Ah))
                    nc.vector.scalar_tensor_tensor(lo, mT[:, k], col(R_MN + 8 * l + k), hi.bitcast(F32),
                                                   ALU.mult, ALU.subtract).then_inc(mg_ready, 1)
            dve.wait_ge(mstd_done, 1)
            link(nc.vector.reciprocal(rm[:], rm[:]))

            def mem_out(n):
                dve.wait_ge(dense_done, n + 1)
                nc.vector.tensor_tensor(kv[:, n // 4, n % 4], PS[:, n % 2, 0:MEM], rm[:], ALU.mult).then_inc(dense_free, 1)

            xn = [0]

            def x_chunk(k, grow):
                n = xn[0]
                xn[0] += 1
                sq = tmp[6 + n % 2][:, 0:SEQ]
                dve.wait_ge(xsq, n + 1)
                if k == 0:
                    nc.vector.tensor_copy(acc[:], sq).then_inc(xsq_used, 1)
                else:
                    dve.wait_ge(xsq_used, n)
                    nc.vector.tensor_tensor(acc[:], acc[:], sq, ALU.add).then_inc(xsq_used, 1)
                dve.wait_ge(h_hi, n + 1)
                nc.vector.scalar_tensor_tensor(Hl[:, k], xT[:, k], col(grow + k), Hh[:, k].bitcast(F32),
                                               ALU.mult, ALU.subtract).then_inc(h_ready, 1)

            def x_rinv(i):
                dve.wait_ge(std_done, i + 1)
                link(nc.vector.reciprocal(rinv[:], rinv[:]))

            for n in range(4):
                mem_out(n)
            for k in range(4):
                x_chunk(k, R_N1)
            for k in range(4, 8):
                x_chunk(k, R_N1)
            for n in range(4, 8):
                mem_out(n)
            for l in range(2):
                dve.wait_ge(kstd, l + 1)
                link(nc.vector.reciprocal(kvs[:], kvs[:]))
                nc.vector.scalar_tensor_tensor(xk[:, l].rearrange("p a n -> p (a n)"), kv[:, l, 0:2].rearrange("p a n -> p (a n)"),
                                               col(R_XK + l), kvs[:], ALU.mult, ALU.mult).then_inc(kn_ready, 1)
            dve.wait_ge(lam_b, 1)
            nc.vector.tensor_copy(lam[:], PS[:, 2, 0:1]).then_inc(lam_d, 1)
            x_rinv(0)

            def scaled_out(n, dst):
                dve.wait_ge(dense_done, n + 1)
                nc.vector.tensor_tensor(dst, PS[0:dst.shape[0], n % 2], rinv[0:dst.shape[0], :], ALU.mult).then_inc(dense_free, 1)

            scaled_out(T_GATE, tmp[4][0:8, 0:SEQ])

            def conv(i, j):
                raw, n0 = tmp[2 + j], T_QK + j
                dve.wait_ge(dense_done, i * 2 + (n0 + 1))
                nc.vector.tensor_tensor(raw[:, CONV - 1:CONV - 1 + SEQ], PS[:, n0 % 2], rinv[:], ALU.mult).then_inc(dense_free, 1)
                dve.wait_ge(dense_free, i * 2 + (n0 + 1))
                c = i * 2 + j

                def w(r):
                    return gcol[:, bass.ds(c + r, 1)]
                y = QK[:, bass.ds(c, 1)].rearrange("p a n -> p (a n)")
                nc.vector.tensor_scalar(y, raw[:, 3:3 + SEQ], w(R_CW + 3 * QKC), w(R_CB), ALU.mult, ALU.add).then_inc(conv_step, 1)
                for tap in (2, 1, 0):
                    dve.wait_ge(conv_step, i * 6 + (3 * j + 3 - tap))
                    nc.vector.scalar_tensor_tensor(y, raw[:, tap:tap + SEQ], w(R_CW + tap * QKC), y, ALU.mult,
                                                   ALU.add).then_inc(conv_step if tap else conv_done, 1)

            conv(0, 0)
            conv(0, 1)
            F, L = tmp[0][0:MH, 0:SEQ], tmp[1][0:MH, 0:SEQ]
            b_row, a_row = tmp[5][0:MH, 0:SEQ], tmp[6][0:MH, 0:SEQ]
            dve.wait_ge(lnf_done, 1)
            link(nc.vector.scalar_tensor_tensor(L, F, 0.0, L, ALU.min, ALU.subtract))
            link(nc.vector.memset(tmp[7][0:MH, 0:SEQ], 1.0))
            link(nc.vector.tensor_tensor_scan(b_row, tmp[7][0:MH, 0:SEQ], L, 0.0, ALU.mult, ALU.add))
            link(nc.vector.scalar_tensor_tensor(a_row, PS[0:MH, 2], gb[:, 0:1], b_row, ALU.add, ALU.subtract))
            link(nc.vector.tensor_tensor_scan(Mrow[:], a_row, a_row, 0.0, ALU.max, ALU.max))
            nc.vector.tensor_tensor(mrow[:], Mrow[:], b_row, ALU.add).then_inc(a_ready, 1)
            with dve.Fori(1, QKC // 2) as i:
                conv(i, 0)
                conv(i, 1)
            dve.wait_ge(at_done, 1)
            nc.vector.tensor_copy(aT[:], PS[:, 3, 0:NT * MH].rearrange("p (t h) -> p t h", h=MH)).then_inc(at_ready, 1)
            for c in range(MC):
                dve.wait_ge(dense_done, T_O + c + 1)
                nc.vector.tensor_tensor(SO[:, c], PS[:, (T_O + c) % 2], rinv[:], ALU.mult).then_inc(dense_free, 1)
            for c in range(MC):
                if c >= 2:
                    dve.wait_ge(vT_done, c - 1)
                scaled_out(T_V + c, tmp[4 + c % 2][:, 0:SEQ])
            scaled_out(T_XA, xqA[:, 0])

            def head_diag(h):
                dve.wait_ge(mbc_done, 2 * h + 1)
                if h >= 1:
                    dve.wait_ge(wt_ready, 7 * h)
                nc.vector.tensor_tensor(tmp[1][:, 0:SEQ].rearrange("p (t n) -> p t n", t=NT),
                                        PS[:, 4].rearrange("p (t n) -> p t n", t=NT),
                                        big_mask.rearrange("p (a n) -> p a n", a=1).broadcast_to([P, NT, P]),
                                        ALU.add).then_inc(dg_ready, 1)

            def head_p(h):
                for s in range(NT):
                    dve.wait_ge(s_done, NT * h + s + 1)
                    dve.wait_ge(wt_ready, 7 * h + min(2 * s + 2, 7))
                    w = WT[:, W_OFF[s]:W_OFF[s] + SEQ - s * P]
                    nc.vector.scalar_tensor_tensor(w, PS[:, S_BANK[s], s * P:SEQ], MHD ** -0.5, w, ALU.mult,
                                                   ALU.mult).then_inc(p_ready, 1)

            def head_out(h):
                f, (c, r) = FULL[h], HALF[h]
                dve.wait_ge(den_abs, h + 1)
                dve.wait_ge(em_done, h + 1)
                dn = tmp[2][:, 0:SEQ]
                link(nc.vector.tensor_tensor(dn, dn, tmp[0][:, 0:SEQ], ALU.max))
                link(nc.vector.reciprocal(dn, dn))
                nc.vector.tensor_tensor(QK[:, f], PS[:, 0], dn, ALU.mult)
                nc.vector.tensor_tensor(QK[r:r + 64, c], PS[r:r + 64, 1], dn[r:r + 64], ALU.mult).then_inc(hn_ready, 1)

            def head_mix(h):
                f, (c, r) = FULL[h], HALF[h]
                rh = tmp[5][:, 0:SEQ]
                dve.wait_ge(hstd, h + 1)
                link(nc.vector.reciprocal(rh, rh))
                dve.wait_ge(o_gate, 1)
                link(nc.vector.scalar_tensor_tensor(QK[:, f], QK[:, f], col(R_HN + f), rh, ALU.mult, ALU.mult))
                nc.vector.tensor_tensor(QK[:, f], QK[:, f], SO[:, f], ALU.mult).then_inc(mix_t, 1)
                q = QK[r:r + 64, c]
                link(nc.vector.scalar_tensor_tensor(q, q, gcol[r:r + 64, R_HN + c:R_HN + c + 1], rh[r:r + 64], ALU.mult, ALU.mult))
                nc.vector.tensor_tensor(q, q, SO[r:r + 64, c], ALU.mult).then_inc(mix_t, 1)
                dve.wait_ge(mix_hi, 2 * h + 1)
                nc.vector.tensor_tensor(Al[:, f], QK[:, f], Ah[:, f].bitcast(F32), ALU.subtract).then_inc(mix_lo, 1)
                dve.wait_ge(mix_hi, 2 * h + 2)
                nc.vector.tensor_tensor(Al[r:r + 64, c], q, Ah[r:r + 64, c].bitcast(F32), ALU.subtract).then_inc(mix_lo, 1)

            head_diag(0)
            head_p(0)
            scaled_out(T_XA + 1, xqA[:, 1])
            for h in range(MH):
                if h >= 1:
                    head_diag(h)
                    head_p(h)
                head_out(h)
                if h + 1 < MH:
                    pass
                head_mix(h)

            def cross(l, xq, sq, Pb, nm, rs):
                dve.wait_ge(xq_std, l + 1)
                link(nc.vector.reciprocal(sq, sq))
                nc.vector.scalar_tensor_tensor(xq, xq, gx[:, l:l + 1], sq, ALU.mult, ALU.mult).then_inc(xqn, 1)
                for c in range(2):
                    i = 2 * l + c
                    for b in range(4):
                        dve.wait_ge(xs_done, 4 * i + b + 1)
                        nc.vector.tensor_reduce(nm[:, 8 * c + 2 * b:8 * c + 2 * b + 2],
                                                PS[:, 4 + b].rearrange("p (a n) -> p a n", a=2), AX.X, ALU.max,
                                                negate=True).then_inc(xmax, 1)
                    for j in range(8):
                        dve.wait_ge(xexp, 8 * i + j + 1)
                        r = rs[:, 8 * c + j:8 * c + j + 1]
                        link(nc.vector.reciprocal(r, r))
                        nc.vector.tensor_scalar(Pb[:, j], Pb[:, j], r, None, ALU.mult).then_inc(xp_ready, 1)
                    dve.wait_ge(xo_hi, i + 1)
                    nc.vector.tensor_tensor(Al[:, MC + c], PS[:, 2 + c], Ah[:, MC + c].bitcast(F32),
                                            ALU.subtract).then_inc(xo_ready, 1)

            cross(0, xqA[:], SO[:, 0:2], QK[:, 6:10].rearrange("p a (b n) -> p (a b) n", b=2), nmA, rsA)

            def x_add(n, k):
                dve.wait_ge(dense_done, n + 1)
                nc.vector.tensor_tensor(xT[:, k], xT[:, k], PS[:, n % 2], ALU.add).then_inc(dense_free, 1)

            def x_phase(base, grow):
                for k in range(KD):
                    x_add(base + k, k)
                    x_chunk(k, grow)

            def ffn(l, grow):
                n0 = l * HC
                for s, (h0, nh) in enumerate(SEG):
                    base = seg_base(l, s)
                    f0 = n0 + h0
                    with dve.Fori(0, nh) as i:
                        dve.wait_ge(dense_done, i * 2 + (base + 1))
                        nc.vector.tensor_tensor(tmp[1][:, 0:SEQ], PS[:, base % 2], rinv[:], ALU.mult).then_inc(dense_free, 1)
                        dve.wait_ge(dense_done, i * 2 + (base + 2))
                        nc.vector.tensor_tensor(tmp[2][:, 0:SEQ], PS[:, (base + 1) % 2], rinv[:], ALU.mult).then_inc(dense_free, 1)
                        dve.wait_ge(dense_free, i * 2 + (base + 2))
                        dve.wait_ge(silu_done, i + (f0 + 1))
                        nc.vector.tensor_tensor(tmp[3][:, 0:SEQ], tmp[0][:, 0:SEQ], tmp[2][:, 0:SEQ], ALU.mult).then_inc(gu_ready, 1)
                        dve.wait_ge(f_hi, i + (f0 + 1))
                        one = tmp[3][:, 0:SEQ].rearrange("p (a n) -> p a n", a=1)
                        nc.vector.tensor_tensor(Al[:, bass.ds(i, 1)], one, Ah[:, bass.ds(i, 1)].bitcast(F32),
                                                ALU.subtract).then_inc(f_ready, 1)
                    down = base + 2 * nh
                    if s + 1 < len(SEG):
                        with dve.Fori(0, KD // 2) as i:
                            for j in range(2):
                                dve.wait_ge(dense_done, i * 2 + (down + j + 1))
                                xk_ = xT[:, bass.ds(i * 2 + j, 1)]
                                b = (down + j) % 2
                                nc.vector.tensor_tensor(xk_, xk_, PS[:, b:b + 1], ALU.add).then_inc(dense_free, 1)
                    elif grow is not None:
                        x_phase(down, grow)
                    else:
                        for k in range(KD):
                            x_add(down + k, k)

            x_phase(T_OUT[0], R_N2)
            x_rinv(1)
            ffn(0, R_N1 + 8)
            x_rinv(2)

            scaled_out(T_B, QKP[:, 0, 0])
            scaled_out(T_B + 1, QKP[:, 0, 1])
            C1 = 6.28125
            C2 = float(np.float32(int((2 * math.pi - C1) * 2 ** 22) / 2 ** 22))
            C3 = 2 * math.pi - C1 - C2
            MAGIC = 1.5 * 2 ** 23
            pf, an, kk = QR[:, 0], QR[:, 1], QT[:, 1]
            dve.wait_ge(pos_in, 16)
            link(nc.vector.tensor_copy(pf, posi[:]))
            link(nc.vector.tensor_scalar(an, pf, cn[:, C_INV:C_INV + 1], None, ALU.mult))
            link(nc.vector.tensor_scalar(kk, an, 1.0 / (2 * math.pi), MAGIC, ALU.mult, ALU.add))
            link(nc.vector.tensor_scalar(kk, kk, MAGIC, None, ALU.subtract))
            for part in (C1, C2, C3):
                link(nc.vector.scalar_tensor_tensor(an, kk, -part, an, ALU.mult, ALU.add))
            nc.vector.tensor_scalar(QT[:, 0], an, 3.1415925, -3.1415925, ALU.min, ALU.max).then_inc(ang, 1)
            scaled_out(T_B + 2, tmp[2][:, 0:SEQ])

            def b_norm(c):
                dve.wait_ge(bstd, c + 1)
                link(nc.vector.reciprocal(QS[:], QS[:]))
                nc.vector.scalar_tensor_tensor(QKP[:, c % 2, 0], QKP[:, c % 2, 0], gx[:, 2:3], QS[:, 0], ALU.mult, ALU.mult)
                nc.vector.scalar_tensor_tensor(QKP[:, c % 2, 1], QKP[:, c % 2, 1], col(R_BK), QS[:, 1], ALU.mult,
                                               ALU.mult).then_inc(bn_ready, 1)
                if c == 0:
                    dve.wait_ge(trig, 2)
                dve.wait_ge(bn_ready, c + 1)
                cosb, sinb = (t[:].rearrange("p (a n) -> p a n", a=1).broadcast_to([P, 2, SEQ]) for t in (cosT, sinT))
                link(nc.vector.tensor_tensor(QT[:], QKP[:, c % 2], cosb, ALU.mult))

            def b_rope(c):
                sinb = sinT[:].rearrange("p (a n) -> p a n", a=1).broadcast_to([P, 2, SEQ])
                dve.wait_ge(brot, c + 1)
                link(nc.vector.tensor_tensor(QR[:], PS[:, 2:4], sinb, ALU.mult))
                nc.vector.tensor_tensor(QR[:], QR[:], QT[:], ALU.add).then_inc(bqr, 1)

            def b_max(c, u):
                t, b = NT - 1 - u, 4 + 2 * (u % 2)
                n = 4 * c + u
                dve.wait_ge(bs_done, n + 1)
                dg = PS[:, b:b + 2, t * P:(t + 1) * P]
                link(nc.vector.tensor_tensor(dg, dg, neg_mask.rearrange("p (a n) -> p a n", a=1).broadcast_to([P, 2, P]), ALU.add))
                j = (8 * c + 2 * u) % 64
                nc.vector.tensor_reduce(nmB[:, j:j + 2], PS[:, b:b + 2, 0:(t + 1) * P], AX.X, ALU.max,
                                        negate=True).then_inc(bmax, 1)

            def b_prob(c, u):
                t = NT - 1 - u
                n = 4 * c + u
                j = (8 * c + 2 * u) % 64
                w = slice(W_OFF[u], W_OFF[u] + (t + 1) * P)
                dve.wait_ge(bexp, 2 * n + 2)
                link(nc.vector.reciprocal(rsB[:, j:j + 2], rsB[:, j:j + 2]))
                link(nc.vector.tensor_scalar(PB[:, 1, w], PB[:, 1, w], rsB[:, j + 1:j + 2], lam[:], ALU.mult, ALU.mult))
                nc.vector.scalar_tensor_tensor(PB[:, 0, w], PB[:, 0, w], rsB[:, j:j + 1], PB[:, 1, w], ALU.mult,
                                               ALU.subtract).then_inc(ba_ready, 1)

            def b_mix(c):
                dve.wait_ge(bostd, c + 1)
                link(nc.vector.reciprocal(tmp[7][:, 0:SEQ], tmp[7][:, 0:SEQ]))
                nc.vector.scalar_tensor_tensor(tmp[5][:, 0:SEQ], PS[:, 4], gx[:, 3:4], tmp[7][:, 0:SEQ], ALU.mult,
                                               ALU.mult).then_inc(bmix_t, 1)
                dve.wait_ge(bmix_hi, c + 1)
                nc.vector.tensor_tensor(Al[:, c], tmp[5][:, 0:SEQ], Ah[:, c].bitcast(F32), ALU.subtract).then_inc(bmix_lo, 1)

            for c in range(MC):
                b_norm(c)
                n = T_B + 3 * (c + 1)
                last = c + 1 == MC
                scaled_out(n, xqB[:, 0] if last else QKP[:, (c + 1) % 2, 0])
                if c >= 1:
                    b_mix(c - 1)
                b_rope(c)
                scaled_out(n + 1, xqB[:, 1] if last else QKP[:, (c + 1) % 2, 1])
                b_max(c, 0)
                b_max(c, 1)
                b_prob(c, 0)
                b_prob(c, 1)
                if not last:
                    if c >= 1:
                        dve.wait_ge(bvt_done, c)
                    scaled_out(n + 2, tmp[2 + (c + 1) % 2][:, 0:SEQ])
                b_max(c, 2)
                b_max(c, 3)
                b_prob(c, 2)
                b_prob(c, 3)
            b_mix(MC - 1)
            cross(1, xqB[:], QS[:], PB[:].rearrange("p a n -> p (a n)")[:, 0:2048].rearrange("p (a n) -> p a n", a=8), nmX, rsX)
            x_phase(T_OUT[1], R_N2 + 8)
            x_rinv(3)
            ffn(1, None)

        @block.tensor
        def _(pe):
            def mm(out_, a, b, start=True, stop=True):
                return nc.tensor.matmul(out_, a, b, start=start, stop=stop)

            pe.wait_ge(con_in, 16)
            pe.wait_ge(prm_in, 16 * 16)
            nc.tensor.transpose(PS[:, 2, 0:N_PRM], prm[0:N_PRM, :], ident[0:N_PRM, 0:N_PRM]).then_inc(prm_t, 1)
            pe.wait_ge(mem_in, 16)

            def tr_group(g, blocks):
                if g >= 4:
                    pe.wait_ge(tr_free, g - 3)
                for j, b in enumerate(blocks):
                    last = nc.tensor.transpose(PS[:, 4 + g % 4, j * P:(j + 1) * P], b, ident)
                last.then_inc(tr_done, 1)

            for g in range(4):
                tr_group(g, [m_st[:, t, (2 * g + a) * P:(2 * g + a + 1) * P] for a in range(2) for t in range(MT_TILES)])
            pe.wait_ge(x_in, 16)
            for k in range(4):
                tr_group(4 + k, [x_st[:, t, k * P:(k + 1) * P] for t in range(NT)])

            def tile(i, n0, hi, lo, nk=8, step=2, ready=None, n=SEQ):
                sl = n0 % SPLIT
                pe.wait_ge(w_split, i * step + (n0 + 1))
                if not (isinstance(i, int) and n0 + step * i < 2):
                    pe.wait_ge(dense_free, i * step + (n0 - 1))
                for k in range(nk):
                    if ready:
                        for s_, v_ in ready(k):
                            pe.wait_ge(s_, v_)
                    for j, (w, a) in enumerate(((w_hi, hi), (w_hi, lo), (w_lo, hi))):
                        last = mm(PS[:, sl, 0:n], w[:, sl, k], a(k), start=(k == 0 and j == 0), stop=(k == nk - 1 and j == 2))
                last.then_inc(dense_done, 1)

            def h_tile(n0, i=0, ready=None):
                tile(i, n0, lambda k: Hh[:, k], lambda k: Hl[:, k], ready=ready)

            def a_tile(n0, i=0, ready=None, nk=8):
                tile(i, n0, lambda k: Ah[:, k], lambda k: Al[:, k], nk=nk, ready=ready)

            def m_tile(n):
                l = n // 4

                def part(A):
                    return lambda k: A[:, 4 * l:4 * l + 4].rearrange("p a n -> p (a n)")[:, k * MEM:(k + 1) * MEM]
                tile(0, n, part(Ah), part(Al), n=MEM, ready=(lambda k: [(mg_ready, 8 * l + k + 1)]) if n % 4 == 0 else None)

            m_tile(0)
            m_tile(1)
            pe.wait_ge(macc_done, 1)
            pe.wait_ge(set_done, 3)
            mm(PS[:, 3, 0:MEM], ones[:], macc[:]).then_inc(mss_done, 1)
            m_tile(2)
            m_tile(3)
            for k in range(4, 8):
                tr_group(4 + k, [x_st[:, t, k * P:(k + 1) * P] for t in range(NT)])
            for n in range(4, 8):
                m_tile(n)
            pe.wait_ge(lam_d, 1)
            mm(PS[:, 2, 0:1], ones[0:1, :], lame[0:1, 0:1]).then_inc(lam_b, 1)
            for l in range(2):
                pe.wait_ge(ksq, l + 1)
                pe.wait_ge(tr_free, 12)
                mm(PS[:, 4 + l], bdiag, kvs[:]).then_inc(kss, 1)
                pe.wait_ge(dense_free, 4 * l + 4)
                if l == 1:
                    pe.wait_ge(vtr_out, 1)
                for t in range(MT_TILES):
                    for c in range(2):
                        last = nc.tensor.transpose(PS[:, 6, (2 * t + c) * P:(2 * t + c + 1) * P],
                                                   kv[:, l, 2 + c, t * P:(t + 1) * P], ident)
                last.then_inc(vtr, 1)

            def x_ss(i):
                pe.wait_ge(xsq_used, KD * (i + 1))
                mm(PS[:, SS_BANK], ones[:], acc[:]).then_inc(ss_done, 1)

            h_tile(T_GATE, ready=lambda k: [(h_ready, k + 1)])
            x_ss(0)
            h_tile(T_QK)
            pe.wait_ge(dense_free, T_GATE + 1)
            pe.wait_ge(lam_d, 2)
            mm(PS[0:MH, 2], cn[0:8, C_GSEL:C_GSEL + MH], tmp[4][0:8, 0:SEQ])
            mm(PS[0:MH, 3], cn[0:8, C_GSEL + MH:C_GSEL + 2 * MH], tmp[4][0:8, 0:SEQ]).then_inc(gsel_done, 1)
            h_tile(T_QK + 1)
            with pe.Fori(1, QKC // 2) as i:
                h_tile(T_QK, i)
                h_tile(T_QK + 1, i)
            pe.wait_ge(a_ready, 1)
            for t in range(NT):
                last = nc.tensor.transpose(PS[:, 3, t * MH:(t + 1) * MH], tmp[6][0:MH, t * P:(t + 1) * P], ident[0:MH, 0:MH])
            last.then_inc(at_done, 1)
            with pe.Fori(0, MC // 2) as i:
                h_tile(T_O, i)
                h_tile(T_O + 1, i)

            def v_tr(c):
                pe.wait_ge(dense_free, T_V + c + 1)
                if c >= 2:
                    pe.wait_ge(v_ready, c - 1)
                for t in range(NT):
                    last = nc.tensor.transpose(PS[:, 4 + c % 2, t * P:(t + 1) * P], tmp[4 + c % 2][:, t * P:(t + 1) * P], ident)
                last.then_inc(vT_done, 1)

            for c in range(MC):
                h_tile(T_V + c)
                if c >= 1:
                    v_tr(c - 1)
            h_tile(T_XA)
            v_tr(MC - 1)

            def head_scores(h):
                f, (c, r) = FULL[h], HALF[h]
                sel = cn[0:MH, C_SEL + h * P:C_SEL + (h + 1) * P]
                if h == 0:
                    pe.wait_ge(v_ready, MC)
                    pe.wait_ge(at_ready, 1)
                    pe.wait_ge(qk_ready, QKC)
                else:
                    pe.wait_ge(wt_ready, 7 * h)
                    pe.wait_ge(den_abs, h)
                mm(PS[:, 4], sel, Mrow[:]).then_inc(mbc_done, 1)
                mm(PS[:, 5], sel, mrow[:]).then_inc(mbc_done, 1)
                for s in range(NT):
                    o = PS[:, S_BANK[s], s * P:SEQ]
                    if h >= 1:
                        pe.wait_ge(p_ready, NT * (h - 1) + s + 1)
                    mm(o, QK[:, MC + f, s * P:(s + 1) * P], QK[:, f, s * P:SEQ], stop=False)
                    mm(o, QK[r:r + 64, MC + c, s * P:(s + 1) * P], QK[r:r + 64, c, s * P:SEQ], start=False).then_inc(s_done, 1)

            def head_pv(h):
                f, (c, r) = FULL[h], HALF[h]
                pe.wait_ge(em_done, h + 1)
                if h == 0:
                    pe.wait_ge(dense_free, T_XA + 2)
                else:
                    pe.wait_ge(hstd, h)
                for s in range(NT):
                    pe.wait_ge(p_ready, NT * h + s + 1)
                    w = WT[:, W_OFF[s]:W_OFF[s] + SEQ - s * P]
                    st, sp_ = s == 0, s == NT - 1
                    mm(PS[:, 5, s * P:SEQ], ones[:], w, start=st, stop=sp_)
                    mm(PS[:, 0, s * P:SEQ], V[:, s, f * P:(f + 1) * P], w, start=st, stop=sp_)
                    last = mm(PS[r:r + 64, 1, s * P:SEQ], V[:, s, c * P + r:c * P + r + 64], w, start=st, stop=sp_)
                last.then_inc(num_done, 1)

            def head_ss(h):
                c, r = HALF[h]
                pe.wait_ge(hsq, 2 * h + 2)
                mm(PS[:, 0], ones[:], tmp[3][:, 0:SEQ], stop=False)
                mm(PS[:, 0], ones[r:r + 64, :], tmp[4][r:r + 64, 0:SEQ], start=False).then_inc(hss, 1)

            head_scores(0)
            h_tile(T_XA + 1)
            for h in range(MH):
                head_pv(h)
                if h + 1 < MH:
                    head_scores(h + 1)
                head_ss(h)

            def cross(l, xq, sq, Pb, PT):
                pe.wait_ge(xq_sq, l + 1)
                mm(PS[:, 2], bdiag, sq[:, 0])
                mm(PS[:, 3], bdiag, sq[:, 1]).then_inc(xq_ss, 1)
                pe.wait_ge(xqn, l + 1)
                pe.wait_ge(kn_ready, 2)
                for c in range(2):
                    i = 2 * l + c
                    if c == 1:
                        pe.wait_ge(xpt_ready, 4 * i)
                    for b in range(4):
                        r = 64 * (b // 2)
                        for a in range(2):
                            t = 2 * (b % 2) + a
                            last = mm(PS[:, 4 + b, a * MEM:(a + 1) * MEM], xq[r:r + 64, c, t * P:(t + 1) * P], xk[r:r + 64, l, c])
                        last.then_inc(xs_done, 1)
                    for b in range(4):
                        hd, mt = b // 2, b % 2
                        if b == 0:
                            pe.wait_ge(xp_ready, 8 * i + 8)
                        for t in range(NT):
                            last = nc.tensor.transpose(PS[:, 4 + b, t * P:(t + 1) * P], Pb[:, 4 * hd + t, mt * P:(mt + 1) * P], ident)
                    last.then_inc(xpt_done, 1)
                    for hd in range(2):
                        for mt in range(MT_TILES):
                            pe.wait_ge(xpt_ready, 4 * i + 2 * hd + mt + 1)
                            last = mm(PS[64 * hd:64 * hd + 64, 2 + c], xv[:, l, mt, (2 * c + hd) * 64:(2 * c + hd + 1) * 64],
                                      PT[:, 2 * hd + mt], start=mt == 0, stop=mt == 1)
                    last.then_inc(xo_done, 1)

            cross(0, xqA[:], SO[:, 0:2], QK[:, 6:10].rearrange("p a (b n) -> p (a b) n", b=2),
                  V[:].rearrange("p a n -> p (a n)")[:, 0:2048].rearrange("p (a n) -> p a n", a=4))

            def out_proj(l, ready):
                a_tile(T_OUT[l], ready=ready)
                a_tile(T_OUT[l] + 1)
                with pe.Fori(1, KD // 2) as i:
                    a_tile(T_OUT[l], i)
                    a_tile(T_OUT[l] + 1, i)

            MIX_A = [1, 4, 3, 5, 8, 7]
            out_proj(0, lambda k: [(mix_lo, MIX_A[k]) if k < MC else (xo_ready, k - MC + 1)])

            def ffn(l):
                n0 = l * HC
                for s, (h0, nh) in enumerate(SEG):
                    base = seg_base(l, s)
                    if s == 0:
                        h_tile(base, ready=lambda k: [(h_ready, KD * (2 * l + 1) + k + 1)])
                        x_ss(2 * l + 1)
                        h_tile(base + 1)
                    with pe.Fori(1 if s == 0 else 0, nh) as i:
                        h_tile(base, i)
                        h_tile(base + 1, i)
                    down = base + 2 * nh
                    a_tile(down, nk=nh, ready=lambda k: [(f_ready, n0 + h0 + k + 1)])
                    a_tile(down + 1, nk=nh)
                    with pe.Fori(1, KD // 2) as i:
                        a_tile(down, i, nk=nh)
                        a_tile(down + 1, i, nk=nh)

            ffn(0)

            h_tile(T_B, ready=lambda k: [(h_ready, 2 * KD + k + 1)])
            x_ss(2)
            h_tile(T_B + 1)
            h_tile(T_B + 2)

            def b_ss(c):
                pe.wait_ge(bsq, c + 1)
                if c >= 1:
                    pe.wait_ge(bat_ready, 4 * c)
                mm(PS[:, 2], bdiag, QS[:, 0])
                mm(PS[:, 3], bdiag, QS[:, 1]).then_inc(bss, 1)

            def b_rot(c):
                pe.wait_ge(bn_ready, c + 1)
                mm(PS[:, 2], rotm, QKP[:, c % 2, 0])
                mm(PS[:, 3], rotm, QKP[:, c % 2, 1]).then_inc(brot, 1)

            def b_vt(c):
                pe.wait_ge(dense_free, T_B + 3 * c + 3)
                pe.wait_ge(bqr, c + 1)
                for t in range(NT):
                    last = nc.tensor.transpose(PS[:, 2, t * P:(t + 1) * P], tmp[2 + c % 2][:, t * P:(t + 1) * P], ident)
                last.then_inc(bvt_done, 1)

            def b_s(c, u):
                t, b = NT - 1 - u, 4 + 2 * (u % 2)
                if u < 2 and c >= 1:
                    pe.wait_ge(bmix_t, c)
                if u >= 2:
                    pe.wait_ge(bexp, 2 * (4 * c + u - 2) + 2)
                for hd in range(2):
                    r = 64 * hd
                    last = mm(PS[:, b + hd, 0:(t + 1) * P], QR[r:r + 64, 0, t * P:(t + 1) * P], QR[r:r + 64, 1, 0:(t + 1) * P])
                last.then_inc(bs_done, 1)

            def b_t(c, u):
                t = NT - 1 - u
                pe.wait_ge(ba_ready, 4 * c + u + 1)
                if u == 0:
                    pe.wait_ge(bv_ready, c + 1)
                if u >= 2:
                    pe.wait_ge(bat_ready, 4 * c + u - 1)
                for k in range(t + 1):
                    last = nc.tensor.transpose(PS[:, 2 + u % 2, k * P:(k + 1) * P], PB[:, 0, W_OFF[u] + k * P:W_OFF[u] + (k + 1) * P], ident)
                last.then_inc(bt_done, 1)

            def b_pv(c):
                pe.wait_ge(bat_ready, 4 * c + 4)
                for k in range(NT):
                    last = mm(PS[:, 4, k * P:SEQ], VB[:, c % 2, k], ATB[:, k, k * P:SEQ], start=k == 0, stop=k == NT - 1)
                last.then_inc(bpv, 1)

            def b_oss(c):
                pe.wait_ge(bosq, c + 1)
                mm(PS[:, 5], ones[:], tmp[6][:, 0:SEQ]).then_inc(boss, 1)

            b_ss(0)
            for c in range(MC):
                n = T_B + 3 * (c + 1)
                h_tile(n)
                if c >= 1:
                    b_oss(c - 1)
                b_rot(c)
                h_tile(n + 1)
                b_vt(c)
                b_s(c, 0)
                b_s(c, 1)
                if c + 1 < MC:
                    h_tile(n + 2)
                b_s(c, 2)
                b_s(c, 3)
                for u in range(NT):
                    b_t(c, u)
                if c + 1 < MC:
                    b_ss(c + 1)
                b_pv(c)
            b_oss(MC - 1)
            pe.wait_ge(bmix_t, MC)
            cross(1, xqB[:], QS[:], PB[:].rearrange("p a n -> p (a n)")[:, 0:2048].rearrange("p (a n) -> p a n", a=8), ATB[:])
            out_proj(1, lambda k: [(bmix_lo, k + 1) if k < MC else (xo_ready, k - MC + 3)])
            ffn(1)
            for k in range(KD):
                pe.wait_ge(dense_free, seg_base(1, 2) + 2 * SEG[2][1] + k + 1)
                if k >= 2:
                    pe.wait_ge(ot_out, k - 1)
                for t in range(NT):
                    last = nc.tensor.transpose(PS[:, 2 + k % 2, t * P:(t + 1) * P], xT[:, k, t * P:(t + 1) * P], ident)
                last.then_inc(ot_done, 1)


_INS = ['x', 'mem', 'positions', 'norm1', 'w_out', 'xq_norm', 'xk_norm', 'mem_norm', 'w_mem_kv', 'norm2',
        'w_gate_up', 'w_down', 'a_w_in', 'a_conv_w', 'a_conv_b', 'a_gate_b', 'a_head_norm',
        'b_w_in', 'b_q_norm', 'b_k_norm', 'b_lambda', 'b_subln']
_OUTS = [((1, SEQ, D), 'float32')]


def kernel(**inputs):
    import numpy as _np
    import concourse.bacc as _bacc
    from concourse import mybir as _mybir
    from concourse.bass_utils import run_bass_kernel_spmd as _run

    nc = _bacc.Bacc("TRN2", target_bir_lowering=False, num_devices=1)
    arrays, args = {}, []
    for name in _INS:
        a = _np.ascontiguousarray(inputs[name])
        arrays[f"in_{name}_dram"] = a
        args.append(nc.dram_tensor(f"in_{name}_dram", a.shape, _mybir.dt.from_np(a.dtype), kind="ExternalInput").ap())
    con = constants()
    arrays["in_constants_dram"] = con
    args.append(nc.dram_tensor("in_constants_dram", con.shape, _mybir.dt.float32, kind="ExternalInput").ap())
    for i, (shape, dtype) in enumerate(_OUTS):
        dt = _mybir.dt.from_np(_np.dtype(dtype))
        args.append(nc.dram_tensor(f"out_{i}_dram", shape, dt, kind="ExternalOutput").ap())
    hybrid_trunk(nc, *args)
    r = _run(nc, [arrays], core_ids=[0])
    return r.results[0]["out_0_dram"]
```

```python
import math
from contextlib import ExitStack

import concourse.bass as bass
import numpy as np
from concourse import mybir

F32 = mybir.dt.float32
F32R = mybir.dt.float32r
I32 = mybir.dt.int32
ALU = mybir.AluOpType
ACT = mybir.ActivationFunctionType
AX = mybir.AxisListType

P = 128
D = 1024
SEQ = 512
MEM = 256
KD = D // P
NT = SEQ // P
MT_TILES = MEM // P
MIX = 768
XW = 256
XH_DIM = 64
MH = 4
MHD = MIX // MH
CONV = 4
QKC = 2 * MIX // P
MC = MIX // P
FFN = 2816
HC = FFN // P
A_IN = 4 * MIX + 2 * MH + XW
B_IN = 3 * MIX + XW
GATE_COL = 4 * MIX
XQ_COL_A = 4 * MIX + 2 * MH
LAMBDA_INIT = 0.8 - 0.6 * math.exp(-0.3 * 1)
EPS = 1e-6
RAW = 4
SPLIT = 2

R_N1, R_N2, R_MN, R_CW, R_CB, R_HN, R_SL, R_XQ, R_XK, R_BQ, R_BK = 0, 16, 32, 48, 96, 108, 114, 115, 117, 119, 120
N_PRM = 121

C_ID, C_BD, C_ROT, C_NEG, C_BIG, C_SEL, C_GSEL, C_INV = 0, 128, 256, 384, 512, 640, 640 + MH * P, 640 + MH * P + 8
N_CON = C_INV + 1


def constants():
    c = np.zeros((P, N_CON), np.float32)
    r = np.arange(P)
    c[:, C_ID:C_ID + P] = np.eye(P)
    c[:, C_BD:C_BD + P] = r[:, None] // 64 == r[None, :] // 64
    rot = np.zeros((P, P), np.float32)
    for j in range(P):
        rot[j + 32 if j % 64 < 32 else j - 32, j] = -1.0 if j % 64 < 32 else 1.0
    c[:, C_ROT:C_ROT + P] = rot
    c[:, C_NEG:C_NEG + P] = np.where(r[None, :] > r[:, None], -1e30, 0.0)
    c[:, C_BIG:C_BIG + P] = np.where(r[None, :] < r[:, None], 1e30, 0.0)
    for h in range(MH):
        c[h, C_SEL + h * P:C_SEL + (h + 1) * P] = 1.0
    for j in range(8):
        c[j, C_GSEL + j] = 1.0
    inv = np.power(np.float32(10000.0), -np.arange(32, dtype=np.float32) * np.float32(2.0) / np.float32(64))
    c[:, C_INV] = inv[r % 32]
    return c


T_MEM = 0
T_GATE = T_MEM + 8
T_QK = T_GATE + 1
T_V = T_QK + QKC
T_XA = T_V + MC
T_O = T_XA + 2
T_OUT = [T_O + MC, 0]
SEG = [(0, 8), (8, 8), (16, 6)]
N_FFN = 2 * HC + KD * len(SEG)
T_FFN = [T_OUT[0] + KD, 0]
T_B = T_FFN[0] + N_FFN
T_XB = T_B + 3 * MC
T_OUT[1] = T_XB + 2
T_FFN[1] = T_OUT[1] + KD
N_TILES = T_FFN[1] + N_FFN


def seg_base(layer, s):
    return T_FFN[layer] + sum(2 * n + KD for _, n in SEG[:s])


def tile_k(n):
    for layer in range(2):
        for s, (_, nh) in enumerate(SEG):
            down = seg_base(layer, s) + 2 * nh
            if down <= n < down + KD:
                return nh
    return 8


def hybrid_trunk(nc, x, mem, positions, w_out, w_mem_kv, w_gate_up, w_down, a_w_in, a_gate_b, b_w_in,
                 b_lambda, prm_rows, con, out):
    ctx = ExitStack()
    with ctx:
        def sb(name, shape, dt=F32, scope=ctx):
            return scope.enter_context(nc.sbuf_tensor(name, shape, dt))

        def sem(name):
            return ctx.enter_context(nc.semaphore(name))

        PS = ctx.enter_context(nc.psum_tensor("PS", [P, 8, 512], F32))

        xT = sb("xT", [P, KD, SEQ])
        Hh = sb("Hh", [P, KD, SEQ], F32R)
        Hl = sb("Hl", [P, KD, SEQ], F32R)
        Ah = sb("Ah", [P, 8, SEQ], F32R)
        Al = sb("Al", [P, 8, SEQ], F32R)
        w_raw = sb("w_raw", [P, RAW, 8, P])
        w_hi = sb("w_hi", [P, SPLIT, 8, P], F32R)
        w_lo = sb("w_lo", [P, SPLIT, 8, P], F32R)
        cn = sb("cn", [P, N_CON])
        ones = sb("ones", [P, P])
        gcol = sb("gcol", [P, N_PRM])
        gx = sb("gx", [P, 4])
        rot_q = sb("rot_q", [P, P])
        rot_k = sb("rot_k", [P, P])
        epsc = sb("epsc", [P, 1])
        hpi = sb("hpi", [P, 1])
        eps64 = sb("eps64", [P, 1])
        rinv = sb("rinv", [P, SEQ])
        acc = sb("acc", [P, SEQ])
        xk = sb("xk", [P, 2, 2, MEM])
        xv = sb("xv", [P, 2, MT_TILES, XW])
        lam = sb("lam", [P, 1])
        lame = sb("lame", [1, 4])
        ident = cn[:, C_ID:C_ID + P]
        bdiag = cn[:, C_BD:C_BD + P]
        rotm = cn[:, C_ROT:C_ROT + P]
        half_sel = bdiag[:, 0:P:64]
        neg_mask = cn[:, C_NEG:C_NEG + P]
        big_mask = cn[:, C_BIG:C_BIG + P]

        tmp = [sb(f"tmp{i}", [P, 516]) for i in range(8)]

        s0 = ExitStack()
        x_st = sb("x_st", [P, NT, D], scope=s0)
        m_st = sb("m_st", [P, MT_TILES, D], scope=s0)
        prm = sb("prm", [P, P], scope=s0)
        mT = sb("mT", [P, KD, MEM], scope=s0)
        msq = sb("msq", [P, KD, MEM], scope=s0)
        rm = sb("rm", [P, MEM], scope=s0)
        kv = sb("kv", [P, 2, 4, MEM], scope=s0)
        kvs = sb("kvs", [P, 512], scope=s0)
        lamv = sb("lamv", [1, 4, 64], scope=s0)
        lamw = sb("lamw", [1, 2, 64], scope=s0)
        s0.close()
        sA = ExitStack()
        QK = sb("QK", [P, QKC, SEQ], scope=sA)
        V = sb("V", [P, NT, MIX], scope=sA)
        SO = sb("SO", [P, MC, SEQ], scope=sA)
        xqA = sb("xqA", [P, 2, SEQ], scope=sA)
        WT = sb("WT", [P, 1280], scope=sA)
        Mrow = sb("Mrow", [MH, SEQ], scope=sA)
        amT = sb("amT", [P, 2, NT, MH], scope=sA)
        emT = sb("emT", [P, NT, MH], scope=sA)
        rcA = sb("rcA", [P, 4, NT], scope=sA)
        rqA = sb("rqA", [P, 2, NT, 2], scope=sA)
        gb = sb("gb", [MH, 2], scope=sA)
        nmA = sb("nmA", [P, 16], scope=sA)
        rsA = sb("rsA", [P, 16], scope=sA)
        sA.close()
        sB = ExitStack()
        QKP = sb("QKP", [P, 2, 2, SEQ], scope=sB)
        VB = sb("VB", [P, 2, NT, P], scope=sB)
        PB = sb("PB", [P, 2, 1280], scope=sB)
        ATB = sb("ATB", [P, NT, SEQ], scope=sB)
        QS = sb("QS", [P, 2, SEQ], scope=sB)
        QT = sb("QT", [P, 2, SEQ], scope=sB)
        QR = sb("QR", [P, 2, SEQ], scope=sB)
        cosT = sb("cosT", [P, SEQ], scope=sB)
        sinT = sb("sinT", [P, SEQ], scope=sB)
        xqB = sb("xqB", [P, 2, SEQ], scope=sB)
        nmB = sb("nmB", [P, 64], scope=sB)
        rsB = sb("rsB", [P, 64], scope=sB)
        posi = sb("posi", [P, SEQ], I32, scope=sB)
        rqk = sb("rqk", [P, 2, NT, 2], scope=sB)
        rqk_all = sb("rqk_all", [P, 2, NT, 2], scope=sB)
        roB = sb("roB", [P, NT], scope=sB)
        ro_all = sb("ro_all", [P, NT], scope=sB)
        rqB = sb("rqB", [P, 2, NT, 2], scope=sB)
        nmX = sb("nmX", [P, 16], scope=sB)
        rsX = sb("rsX", [P, 16], scope=sB)
        sB.close()
        sC = ExitStack()
        o_st = sb("o_st", [P, 2, NT, P], scope=sC)
        sC.close()

        w_in = [sem(f"w_in{i}") for i in range(RAW)]
        w_round = sem("w_round")
        w_split = sem("w_split")
        dense_done = sem("dense_done")
        dense_free = sem("dense_free")
        con_in = sem("con_in")
        prm_in = sem("prm_in")
        mem_in = sem("mem_in")
        x_in = sem("x_in")
        set_done = sem("set_done")
        prm_t = sem("prm_t")
        g_ready = sem("g_ready")
        tr_done = sem("tr_done")
        tr_free = sem("tr_free")
        msq_done = sem("msq_done")
        mss_done = sem("mss_done")
        mstd_done = sem("mstd_done")
        mhi = sem("mhi")
        mg_ready = sem("mg_ready")
        ksq = sem("ksq")
        kss = sem("kss")
        kstd = sem("kstd")
        kn_ready = sem("kn_ready")
        vtr = sem("vtr")
        vtr_out = sem("vtr_out")
        vch = sem("vch")
        ach = sem("ach")
        xsq = sem("xsq")
        xsq_used = sem("xsq_used")
        h_hi = sem("h_hi")
        h_ready = sem("h_ready")
        ss_done = sem("ss_done")
        std_done = sem("std_done")
        gt_ready = sem("gt_ready")
        gsel_done = sem("gsel_done")
        lnf_done = sem("lnf_done")
        a_ready = sem("a_ready")
        at_done = sem("at_done")
        at_ready = sem("at_ready")
        conv_done = sem("conv_done")
        conv_step = sem("conv_step")
        qk_ready = sem("qk_ready")
        o_gate = sem("o_gate")
        vT_done = sem("vT_done")
        v_ready = sem("v_ready")
        mbc_done = sem("mbc_done")
        s_done = sem("s_done")
        dg_ready = sem("dg_ready")
        em_done = sem("em_done")
        wt_ready = sem("wt_ready")
        p_ready = sem("p_ready")
        num_done = sem("num_done")
        num_out = sem("num_out")
        hsq = sem("hsq")
        hcol = sem("hcol")
        hd2 = sem("hd2")
        hstd = sem("hstd")
        hr_wide = sem("hr_wide")
        hr_done = sem("hr_done")
        hr_out = sem("hr_out")
        hnorm = sem("hnorm")
        mix_t = sem("mix_t")
        mix_hi = sem("mix_hi")
        mix_lo = sem("mix_lo")
        xq_sq = sem("xq_sq")
        xq_ss = sem("xq_ss")
        xq_std = sem("xq_std")
        xs_done = sem("xs_done")
        xmax = sem("xmax")
        xexp = sem("xexp")
        xp_ready = sem("xp_ready")
        xpt_done = sem("xpt_done")
        xpt_ready = sem("xpt_ready")
        xo_done = sem("xo_done")
        xo_hi = sem("xo_hi")
        xo_ready = sem("xo_ready")
        silu_done = sem("silu_done")
        gu_ready = sem("gu_ready")
        f_hi = sem("f_hi")
        f_ready = sem("f_ready")
        pos_in = sem("pos_in")
        lam_in = sem("lam_in")
        lam_s = sem("lam_s")
        lam_e = sem("lam_e")
        lam_d = sem("lam_d")
        lam_b = sem("lam_b")
        ang = sem("ang")
        trig = sem("trig")
        bsq = sem("bsq")
        bss = sem("bss")
        bqk_std = sem("bqk_std")
        bo_std = sem("bo_std")
        bn_ready = sem("bn_ready")
        bk_bc = sem("bk_bc")
        brot = sem("brot")
        bqt = sem("bqt")
        bqr = sem("bqr")
        bkr = sem("bkr")
        bvt_done = sem("bvt_done")
        bv_ready = sem("bv_ready")
        bs_done = sem("bs_done")
        bmax = sem("bmax")
        bexp = sem("bexp")
        ba_ready = sem("ba_ready")
        bt_done = sem("bt_done")
        bat_ready = sem("bat_ready")
        bpv = sem("bpv")
        bosq = sem("bosq")
        bon_ready = sem("bon_ready")
        bo_bc = sem("bo_bc")
        bmix_t = sem("bmix_t")
        bmix_hi = sem("bmix_hi")
        bmix_lo = sem("bmix_lo")
        ot_done = sem("ot_done")
        ot_out = sem("ot_out")
        o_store = [sem("o_store0"), sem("o_store1")]

        def wview(w, r0, nk, col):
            return w[r0:r0 + nk * P, :].rearrange("(k p) n -> p k n", p=P)[:, :, bass.ds(col, P)]

        kvw = [w_mem_kv[l] for l in range(2)]
        aw, bw = a_w_in[0], b_w_in[0]

        FULL = [0, 2, 3, 5]
        HALF = [(1, 0), (1, 64), (4, 0), (4, 64)]
        W_OFF = [0, 512, 896, 1152]

        S_BANK = [2, 3, 6, 7]
        SS_BANK = 7

        def flat(ap):
            return ap.rearrange("p a n -> p (a n)")

        def slots(ap, n):
            return [ap[:, i * n:(i + 1) * n] for i in range(ap.shape[1] // n)]

        t512 = [t[:, 0:SEQ] for t in tmp]
        X_SQ = [[t512[0], t512[2]], [t512[0], t512[1]]]
        X_P = [[slots(flat(QK[:, 6:10]), MEM), slots(flat(V[:])[:, 0:2048], MEM)],
               [slots(flat(PB[:])[:, 0:2048], MEM), slots(flat(QT[:]), MEM) + slots(flat(QR[:]), MEM)]]
        X_PT = [[t512[4:8], [QK[:, 10], QK[:, 11]] + slots(flat(V[:])[:, 2048:3072], SEQ)],
                [[ATB[:, k] for k in range(NT)], [QKP[:, i, j] for i in range(2) for j in range(2)]]]
        X_BANK = [0, 4]
        XSS_BANK = [2, 1]
        X_NM, X_RS, X_RQ = [nmA, nmX], [rsA, rsX], [rqA, rqB]

        block = ctx.enter_context(nc.Block())

        @block.sync
        def _(sp):
            sp.dma_start(m_st[:], mem[0].rearrange("(t p) n -> p t n", p=P)).then_inc(mem_in, 16)

            def load(n, slot, src, nk, first=False):
                if not first:
                    sp.wait_ge(w_split, n - (RAW - 1))
                sp.dma_start(w_raw[:, slot, 0:nk, :], src).then_inc(w_in[slot], 16)

            def run(base, count, w, r0, nk, col, step4=None):
                loops = count // 4 if step4 else 0
                if loops > 1:
                    with sp.Fori(0, loops) as i:
                        for s in range(4):
                            load(i * 4 + (base + s), (base + s) % RAW, wview(w, r0, nk, i * step4 + col(s)), nk)
                    done = loops * 4
                else:
                    done = 0
                for j in range(done, count):
                    load(base + j, (base + j) % RAW, wview(w, r0, nk, col(j)), nk)

            for n in range(RAW):
                load(n, n, wview(kvw[0], 0, 8, n * P), 8, first=True)
            sp.dma_start(x_st[:], x[0].rearrange("(t p) n -> p t n", p=P)).then_inc(x_in, 16)
            for n in range(4, 8):
                load(n, n % RAW, wview(kvw[1], 0, 8, (n - 4) * P), 8)
            run(T_GATE, 1, aw, 0, 8, lambda j: GATE_COL)
            run(T_QK, QKC, aw, 0, 8, lambda j: j * P, 4 * P)
            run(T_V, MC, aw, 0, 8, lambda j: 2 * MIX + j * P)
            run(T_XA, 2, aw, 0, 8, lambda j: XQ_COL_A + j * P)
            run(T_O, MC, aw, 0, 8, lambda j: 3 * MIX + j * P)
            for layer in range(2):
                if layer == 1:
                    for c in range(MC):
                        for j in range(3):
                            n = T_B + 3 * c + j
                            load(n, n % RAW, wview(bw, 0, 8, j * MIX + c * P), 8)
                    run(T_XB, 2, bw, 0, 8, lambda j: 3 * MIX + j * P)
                run(T_OUT[layer], KD, w_out[layer], 0, 8, lambda j: j * P, 4 * P)
                for s, (h0, nh) in enumerate(SEG):
                    base = seg_base(layer, s)
                    run(base, 2 * nh, w_gate_up[layer], 0, 8,
                        lambda j, h0=h0: (h0 + j // 2) * P + (j % 2) * FFN, 2 * P)
                    run(base + 2 * nh, KD, w_down[layer], h0 * P, nh, lambda j: j * P, 4 * P)
            ov = out[0].rearrange("(t p) n -> p t n", p=P)
            for k in range(KD):
                sp.wait_ge(ot_out, k + 1)
                sp.dma_start(ov[:, :, k * P:(k + 1) * P], o_st[:, k % 2]).then_inc(o_store[k % 2], 16)
            for j in range(2):
                sp.wait_ge(o_store[j], 16 * KD // 2)

        @block.gpsimd
        def _(pool):
            nc.gpsimd.memset(ones[:], 1.0).then_inc(set_done, 1)
            nc.gpsimd.memset(epsc[:], EPS).then_inc(set_done, 1)
            nc.gpsimd.memset(hpi[:], math.pi / 2).then_inc(set_done, 1)
            nc.gpsimd.memset(eps64[:], XH_DIM * EPS).then_inc(set_done, 1)

            for n in range(N_TILES):
                raw, sl, nk = n % RAW, n % SPLIT, tile_k(n)
                pool.wait_ge(w_in[raw], (n // RAW + 1) * 16)
                if n >= SPLIT:
                    pool.wait_ge(dense_done, n - SPLIT + 1)
                nc.gpsimd.tensor_scalar(w_hi[:, sl, 0:nk], w_raw[:, raw, 0:nk], 0.0, 1.0, ALU.add,
                                        ALU.mult).then_inc(w_round, 1)
                pool.wait_ge(w_round, n + 1)
                nc.gpsimd.tensor_tensor(w_lo[:, sl, 0:nk], w_raw[:, raw, 0:nk],
                                        w_hi[:, sl, 0:nk].bitcast(F32), ALU.subtract).then_inc(w_split, 1)

        @block.scalar
        def _(act):
            link_n = [0]

            def link(ins):
                link_n[0] += 1
                ins.then_inc(ach, 1)
                act.wait_ge(ach, link_n[0])

            act.dma_start(cn[:], con).then_inc(con_in, 16)
            act.dma_start(prm[0:N_PRM, :], prm_rows).then_inc(prm_in, 16)
            with nc.allow_non_contiguous_dma(reason="eight gate biases, once"):
                act.dma_start(gb[:], a_gate_b.rearrange("a (g h) -> h (a g)", g=2)).then_inc(lam_in, 16)
            act.dma_start(lamv[:], b_lambda).then_inc(lam_in, 16)

            def tr_out(g, dst):
                act.wait_ge(tr_done, g + 1)
                nc.scalar.activation(dst, PS[:, 4 + g % 4], ACT.Copy).then_inc(tr_free, 1)

            for g in range(5):
                if g < 4:
                    tr_out(g, flat(mT[:, 2 * g:2 * g + 2]))
                if g >= 1:
                    act.wait_ge(tr_free, g)
                    nc.scalar.activation(msq[:, 2 * g - 2:2 * g], mT[:, 2 * g - 2:2 * g], ACT.Square).then_inc(msq_done, 1)
            act.wait_ge(g_ready, 1)

            def mem_hi(l):
                for k in range(KD):
                    nc.scalar.activation(flat(Ah[:, 4 * l:4 * l + 4])[:, k * MEM:(k + 1) * MEM],
                                         mT[:, k], ACT.Copy,
                                         scale=gcol[:, R_MN + 8 * l + k:R_MN + 8 * l + k + 1]).then_inc(mhi, 1)

            mem_hi(0)
            act.wait_ge(mss_done, 1)
            act.wait_ge(set_done, 4)
            nc.scalar.activation(rm[:], PS[:, 3, 0:MEM], ACT.Sqrt, scale=1.0 / D, bias=epsc[:]).then_inc(mstd_done, 1)
            mem_hi(1)
            for g in range(4, 8):
                tr_out(g, xT[:, g - 4])

            xn = [0]

            def x_chunk(k, grow):
                n = xn[0]
                xn[0] += 1
                if n >= 2:
                    act.wait_ge(xsq_used, n - 1)
                nc.scalar.activation(tmp[6 + n % 2][:, 0:SEQ], xT[:, k], ACT.Square).then_inc(xsq, 1)
                nc.scalar.activation(Hh[:, k], xT[:, k], ACT.Copy,
                                     scale=gcol[:, grow + k:grow + k + 1]).then_inc(h_hi, 1)

            def x_std(i):
                act.wait_ge(ss_done, i + 1)
                nc.scalar.activation(rinv[:], PS[:, SS_BANK], ACT.Sqrt, scale=1.0 / D, bias=epsc[:]).then_inc(std_done, 1)

            for k in range(4):
                act.wait_ge(tr_free, 5 + k)
                x_chunk(k, R_N1)
            for g in range(8, 12):
                tr_out(g, xT[:, g - 4])
            for k in range(4, 8):
                act.wait_ge(tr_free, 5 + k)
                x_chunk(k, R_N1)

            act.wait_ge(lam_s, 1)
            nc.scalar.activation(lame[0:1, 2:4], lame[0:1, 0:2], ACT.Exp).then_inc(lam_e, 1)
            act.wait_ge(dense_free, 2)
            nc.scalar.activation(kvs[:], flat(kv[:, 0, 0:2]), ACT.Square).then_inc(ksq, 1)
            x_std(0)

            for l in range(2):
                if l == 1:
                    act.wait_ge(dense_free, 6)
                    act.wait_ge(kn_ready, 1)
                    nc.scalar.activation(kvs[:], flat(kv[:, 1, 0:2]), ACT.Square).then_inc(ksq, 1)
                act.wait_ge(kss, l + 1)
                nc.scalar.activation(kvs[:], PS[:, 4 + l], ACT.Sqrt, scale=1.0 / XH_DIM, bias=epsc[:]).then_inc(kstd, 1)
                act.wait_ge(vtr, l + 1)
                nc.scalar.activation(flat(xv[:, l]), PS[:, 6], ACT.Copy).then_inc(vtr_out, 1)

            act.wait_ge(gsel_done, 1)
            link(nc.scalar.activation(tmp[0][0:MH, 0:SEQ], PS[0:MH, 3], ACT.Identity, bias=gb[:, 1:2]))
            link(nc.scalar.activation(tmp[1][0:MH, 0:SEQ], tmp[0][0:MH, 0:SEQ], ACT.Abs))
            link(nc.scalar.activation(tmp[1][0:MH, 0:SEQ], tmp[1][0:MH, 0:SEQ], ACT.Exp, scale=-1.0))
            nc.scalar.activation(tmp[1][0:MH, 0:SEQ], tmp[1][0:MH, 0:SEQ], ACT.Ln, bias=1.0).then_inc(lnf_done, 1)
            with act.Fori(0, QKC) as c:
                act.wait_ge(conv_done, c + 1)
                nc.scalar.activation(QK[:, bass.ds(c, 1)], QK[:, bass.ds(c, 1)], ACT.Silu).then_inc(qk_ready, 1)
            act.wait_ge(at_ready, 1)
            nc.scalar.activation(emT[:], amT[:, 1], ACT.Exp, scale=-1.0).then_inc(em_done, 1)
            for c in range(MC):
                act.wait_ge(vT_done, c + 1)
                nc.scalar.activation(V[:, :, c * P:(c + 1) * P], PS[:, 4 + c % 2].rearrange("p (t n) -> p t n", t=NT),
                                     ACT.Copy).then_inc(v_ready, 1)

            def head_weights(h):
                act.wait_ge(dg_ready, h + 1)
                if h >= 1:
                    act.wait_ge(num_done, h)
                for s in range(NT):
                    a = amT[:, 0, s, h:h + 1]
                    nc.scalar.activation(WT[:, W_OFF[s]:W_OFF[s] + P], tmp[1][:, s * P:(s + 1) * P], ACT.Exp,
                                         scale=-1.0, bias=a).then_inc(wt_ready, 1)
                    if s < NT - 1:
                        nc.scalar.activation(WT[:, W_OFF[s] + P:W_OFF[s] + SEQ - s * P], PS[:, 4, (s + 1) * P:SEQ],
                                             ACT.Exp, scale=-1.0, bias=a).then_inc(wt_ready, 1)

            def head_num(h):
                f, (c, r) = FULL[h], HALF[h]
                act.wait_ge(num_done, h + 1)
                nc.scalar.activation(QK[:, f], PS[:, 5], ACT.Copy).then_inc(num_out, 1)
                nc.scalar.activation(QK[r:r + 64, c], PS[r:r + 64, 4], ACT.Copy).then_inc(num_out, 1)
                if h >= 1:
                    act.wait_ge(hcol, h)
                act.wait_ge(num_out, 2 * h + 2)
                nc.scalar.activation(t512[3], QK[:, f], ACT.Square).then_inc(hsq, 1)
                nc.scalar.activation(t512[4][r:r + 64], QK[r:r + 64, c], ACT.Square).then_inc(hsq, 1)

            def head_std(h):
                act.wait_ge(hd2, h + 1)
                nc.scalar.activation(rcA[:, 3], rcA[:, 2], ACT.Sqrt).then_inc(hstd, 1)

            def head_r(h):
                act.wait_ge(hr_done, h + 1)
                if h >= 1:
                    act.wait_ge(hnorm, h)
                nc.scalar.activation(t512[5], PS[:, 5], ACT.Copy).then_inc(hr_out, 1)

            def cross_sq(l):
                for c in range(2):
                    nc.scalar.activation(X_SQ[l][c], (xqA, xqB)[l][:, c], ACT.Square).then_inc(xq_sq, 1)

            def cross_std(l):
                act.wait_ge(xq_ss, l + 1)
                nc.scalar.activation(X_RQ[l][:], PS[:, XSS_BANK[l], 0:16].rearrange("p (a t h) -> p a t h", a=2, t=NT),
                                     ACT.Sqrt, bias=eps64[:]).then_inc(xq_std, 1)

            for h in range(MH):
                head_weights(h)
                if h >= 1:
                    head_r(h - 1)
                head_num(h)
                if h == MH - 2:
                    act.wait_ge(dense_free, T_XA + 2)
                    cross_sq(0)
                if h == MH - 1:
                    cross_std(0)
                head_std(h)

            def cross_exp(l, c, then=None):
                i = 2 * l + c
                for hd in range(2):
                    if hd == 1 and then:
                        then()
                    for t in range(NT):
                        act.wait_ge(xmax, 4 * i + 2 * hd + t // 2 + 1)
                        j = 4 * hd + t
                        nc.scalar.activation(X_P[l][c][j], PS[:, X_BANK[c] + 2 * hd + t // 2, (t % 2) * MEM:(t % 2 + 1) * MEM],
                                             ACT.Exp, scale=X_RQ[l][:, c, t, hd:hd + 1],
                                             bias=X_NM[l][:, 8 * c + j:8 * c + j + 1],
                                             accum_out=X_RS[l][:, 8 * c + j:8 * c + j + 1]).then_inc(xexp, 1)

            def cross_pt(l, c):
                i = 2 * l + c
                for j in range(4):
                    act.wait_ge(xpt_done, 4 * i + j + 1)
                    nc.scalar.activation(X_PT[l][c][j], PS[:, X_BANK[c] + j], ACT.Copy).then_inc(xpt_ready, 1)

            def cross_hi(l, c):
                act.wait_ge(xo_done, 2 * l + c + 1)
                nc.scalar.activation(Ah[:, MC + c], PS[:, X_BANK[c]], ACT.Copy).then_inc(xo_hi, 1)

            cross_exp(0, 0, then=lambda: head_r(MH - 1))
            cross_exp(0, 1)
            act.wait_ge(dense_free, T_O + MC)
            nc.scalar.activation(SO[:], SO[:], ACT.Sigmoid).then_inc(o_gate, 1)
            cross_pt(0, 0)
            cross_pt(0, 1)
            cross_hi(0, 0)
            for c in range(MC):
                act.wait_ge(mix_t, c + 1)
                nc.scalar.activation(Ah[:, c], QK[:, c], ACT.Copy).then_inc(mix_hi, 1)
            cross_hi(0, 1)

            def x_phase(grow, base):
                for k in range(KD):
                    act.wait_ge(dense_free, base + k + 1)
                    x_chunk(k, grow)

            def ffn(l):
                n0 = l * HC
                for s, (h0, nh) in enumerate(SEG):
                    base = seg_base(l, s)
                    with act.Fori(0, nh) as i:
                        act.wait_ge(dense_free, i * 2 + (base + 1))
                        nc.scalar.activation(tmp[0][:, 0:SEQ], tmp[1][:, 0:SEQ], ACT.Silu).then_inc(silu_done, 1)
                        act.wait_ge(gu_ready, i + (n0 + h0 + 1))
                        nc.scalar.activation(Ah[:, bass.ds(i, 1)], tmp[3][:, 0:SEQ].rearrange("p (a n) -> p a n", a=1),
                                             ACT.Copy).then_inc(f_hi, 1)

            x_phase(R_N2, T_OUT[0])
            x_std(1)
            ffn(0)
            act.dma_start(posi[:], positions.broadcast_to([P, SEQ])).then_inc(pos_in, 16)
            x_phase(R_N1 + 8, seg_base(0, 2) + 2 * SEG[2][1])
            x_std(2)
            act.wait_ge(ang, 1)
            nc.scalar.activation(sinT[:], QT[:, 0], ACT.Sin).then_inc(trig, 1)
            link(nc.scalar.activation(cosT[:], QT[:, 0], ACT.Abs))
            nc.scalar.activation(cosT[:], cosT[:], ACT.Sin, scale=-1.0, bias=hpi[:]).then_inc(trig, 1)

            def b_sq(c):
                act.wait_ge(dense_free, T_B + 3 * c + 2)
                if c >= 1:
                    act.wait_ge(bss, c)
                nc.scalar.activation(QS[:], QKP[:, c % 2], ACT.Square).then_inc(bsq, 1)

            def b_std(c):
                act.wait_ge(bss, c + 1)
                if c < MC:
                    if c >= 1:
                        act.wait_ge(bkr, c)
                    last = nc.scalar.activation(rqk[:], PS[:, 6, 0:16].rearrange("p (a t h) -> p a t h", a=2, t=NT), ACT.Sqrt,
                                                bias=eps64[:])
                if c >= 1:
                    if c < MC:
                        last.then_inc(bqk_std, 1)
                    if c >= 2:
                        act.wait_ge(bon_ready, c - 1)
                    last = nc.scalar.activation(roB[:], PS[:, 6, 16:16 + NT], ACT.Sqrt, scale=1.0 / P, bias=epsc[:])
                    last.then_inc(bo_std, 1)
                else:
                    last.then_inc(bqk_std, 1)

            def b_v(c):
                act.wait_ge(bvt_done, c + 1)
                if c >= 2:
                    act.wait_ge(bpv, c - 1)
                nc.scalar.activation(VB[:, c % 2], PS[:, 2].rearrange("p (t n) -> p t n", t=NT), ACT.Copy).then_inc(bv_ready, 1)

            def b_exp(c, u):
                t = NT - 1 - u
                n = 4 * c + u
                act.wait_ge(bmax, n + 1)
                if c >= 1:
                    act.wait_ge(bt_done, 4 * (c - 1) + u + 1)
                for hd in range(2):
                    j = (8 * c + 2 * u + hd) % 64
                    nc.scalar.activation(PB[:, hd, W_OFF[u]:W_OFF[u] + (t + 1) * P], PS[:, 6 - 2 * (u % 2) + hd, 0:(t + 1) * P],
                                         ACT.Exp, scale=rqk_all[:, 0, t, hd:hd + 1],
                                         bias=nmB[:, j:j + 1], accum_out=rsB[:, j:j + 1]).then_inc(bexp, 1)

            def b_at(c, u):
                t = NT - 1 - u
                act.wait_ge(bt_done, 4 * c + u + 1)
                if c >= 1 and u == 0:
                    act.wait_ge(bpv, c)
                nc.scalar.activation(ATB[:, 0:t + 1, t * P:(t + 1) * P],
                                     PS[:, 2 + u % 2, 0:(t + 1) * P].rearrange("p (a n) -> p a n", n=P),
                                     ACT.Copy).then_inc(bat_ready, 1)

            def b_osq(c):
                act.wait_ge(bpv, c + 1)
                nc.scalar.activation(t512[6], PS[:, 4], ACT.Square).then_inc(bosq, 1)

            def b_hi(c):
                act.wait_ge(bmix_t, c + 1)
                nc.scalar.activation(Ah[:, c], t512[5], ACT.Copy).then_inc(bmix_hi, 1)

            b_sq(0)
            for c in range(MC):
                if c >= 1:
                    b_osq(c - 1)
                b_std(c)
                b_exp(c, 0)
                b_v(c)
                b_exp(c, 1)
                if c >= 1:
                    b_hi(c - 1)
                if c + 1 < MC:
                    b_sq(c + 1)
                else:
                    act.wait_ge(dense_free, T_XB + 2)
                    cross_sq(1)
                b_exp(c, 2)
                b_exp(c, 3)
                for u in range(NT):
                    if u == 2 and c + 1 == MC:
                        cross_std(1)
                    b_at(c, u)
            b_osq(MC - 1)
            b_std(MC)
            cross_exp(1, 0)
            b_hi(MC - 1)
            cross_exp(1, 1)
            cross_pt(1, 0)
            cross_pt(1, 1)
            cross_hi(1, 0)
            cross_hi(1, 1)
            x_phase(R_N2 + 8, T_OUT[1])
            x_std(3)
            ffn(1)
            for k in range(KD):
                act.wait_ge(ot_done, k + 1)
                if k >= 2:
                    act.wait_ge(o_store[k % 2], 16 * (k // 2))
                nc.scalar.activation(o_st[:, k % 2].rearrange("p t n -> p (t n)"), PS[:, 2 + k % 2], ACT.Copy).then_inc(ot_out, 1)

        @block.vector
        def _(dve):
            link_n = [0]

            def link(ins):
                link_n[0] += 1
                ins.then_inc(vch, 1)
                dve.wait_ge(vch, link_n[0])

            def col(r):
                return gcol[:, r:r + 1]

            nc.vector.memset(tmp[2][:, 0:CONV - 1], 0.0)
            nc.vector.memset(tmp[3][:, 0:CONV - 1], 0.0)
            dve.wait_ge(prm_t, 1)
            nc.vector.tensor_copy(gcol[:], PS[:, 2, 0:N_PRM]).then_inc(g_ready, 1)
            dve.wait_ge(g_ready, 1)
            link(nc.vector.tensor_tensor(gx[:, 0:2], gcol[:, R_XQ:R_XQ + 2], gcol[:, R_XK:R_XK + 2], ALU.mult))
            link(nc.vector.tensor_scalar(gx[:, 2:3], col(R_BK), 8.0, None, ALU.mult))
            nc.vector.tensor_scalar(gx[:, 3:4], col(R_SL), 1.0 - LAMBDA_INIT, None, ALU.mult)
            dve.wait_ge(con_in, 16)
            nc.vector.tensor_scalar(rot_q[:], rotm, col(R_BQ), None, ALU.mult)
            link(nc.vector.tensor_scalar(rot_k[:], rotm, gx[:, 2:3], None, ALU.mult))
            def mem_lo(l):
                for k in range(KD):
                    dve.wait_ge(mhi, 8 * l + k + 1)
                    lo, hi = (flat(A[:, 4 * l:4 * l + 4])[:, k * MEM:(k + 1) * MEM] for A in (Al, Ah))
                    nc.vector.scalar_tensor_tensor(lo, mT[:, k], col(R_MN + 8 * l + k), hi.bitcast(F32),
                                                   ALU.mult, ALU.subtract).then_inc(mg_ready, 1)

            mem_lo(0)
            dve.wait_ge(mstd_done, 1)
            link(nc.vector.reciprocal(rm[:], rm[:]))

            def mem_out(n):
                dve.wait_ge(dense_done, n + 1)
                nc.vector.tensor_tensor(kv[:, n // 4, n % 4], PS[:, n % 2, 0:MEM], rm[:], ALU.mult).then_inc(dense_free, 1)

            xn = [0]

            def x_chunk(k, grow):
                n = xn[0]
                xn[0] += 1
                sq = tmp[6 + n % 2][:, 0:SEQ]
                dve.wait_ge(xsq, n + 1)
                if k == 0:
                    nc.vector.tensor_copy(acc[:], sq).then_inc(xsq_used, 1)
                else:
                    dve.wait_ge(xsq_used, n)
                    nc.vector.tensor_tensor(acc[:], acc[:], sq, ALU.add).then_inc(xsq_used, 1)
                dve.wait_ge(h_hi, n + 1)
                nc.vector.scalar_tensor_tensor(Hl[:, k], xT[:, k], col(grow + k), Hh[:, k].bitcast(F32),
                                               ALU.mult, ALU.subtract).then_inc(h_ready, 1)

            def x_rinv(i):
                dve.wait_ge(std_done, i + 1)
                link(nc.vector.reciprocal(rinv[:], rinv[:]))

            mem_out(0)
            mem_lo(1)
            mem_out(1)
            for n in range(2, 6):
                x_chunk(n - 2, R_N1)
                mem_out(n)
            dve.wait_ge(lam_in, 32)
            link(nc.vector.tensor_tensor(lamw[:], lamv[0:1, 0:4:2], lamv[0:1, 1:4:2], ALU.mult))
            nc.vector.tensor_reduce(lame[0:1, 0:2], lamw[:], AX.X, ALU.add).then_inc(lam_s, 1)
            for k in range(4, 8):
                x_chunk(k, R_N1)
            mem_out(6)
            mem_out(7)
            dve.wait_ge(lam_e, 1)
            nc.vector.scalar_tensor_tensor(lame[0:1, 0:1], lame[0:1, 2:3], LAMBDA_INIT, lame[0:1, 3:4],
                                           ALU.add, ALU.subtract).then_inc(lam_d, 1)

            def k_norm(l):
                dve.wait_ge(kstd, l + 1)
                link(nc.vector.reciprocal(kvs[:], kvs[:]))
                nc.vector.scalar_tensor_tensor(flat(xk[:, l]), flat(kv[:, l, 0:2]), gx[:, l:l + 1], kvs[:], ALU.mult,
                                               ALU.mult).then_inc(kn_ready, 1)

            x_rinv(0)

            def scaled_out(n, dst):
                dve.wait_ge(dense_done, n + 1)
                nc.vector.tensor_tensor(dst, PS[0:dst.shape[0], n % 2], rinv[0:dst.shape[0], :], ALU.mult).then_inc(dense_free, 1)

            scaled_out(T_GATE, tmp[4][0:8, 0:SEQ])
            k_norm(0)

            def conv(i, j):
                raw, n0 = tmp[2 + j], T_QK + j
                dve.wait_ge(dense_done, i * 2 + (n0 + 1))
                nc.vector.tensor_tensor(raw[:, CONV - 1:CONV - 1 + SEQ], PS[:, n0 % 2], rinv[:], ALU.mult).then_inc(dense_free, 1)
                dve.wait_ge(dense_free, i * 2 + (n0 + 1))
                c = i * 2 + j

                def w(r):
                    return gcol[:, bass.ds(c + r, 1)]
                y = QK[:, bass.ds(c, 1)].rearrange("p a n -> p (a n)")
                nc.vector.tensor_scalar(y, raw[:, 3:3 + SEQ], w(R_CW + 3 * QKC), w(R_CB), ALU.mult, ALU.add).then_inc(conv_step, 1)
                for tap in (2, 1, 0):
                    dve.wait_ge(conv_step, i * 6 + (3 * j + 3 - tap))
                    nc.vector.scalar_tensor_tensor(y, raw[:, tap:tap + SEQ], w(R_CW + tap * QKC), y, ALU.mult,
                                                   ALU.add).then_inc(conv_step if tap else conv_done, 1)

            conv(0, 0)
            dve.wait_ge(lam_b, 1)
            nc.vector.tensor_copy(lam[:], PS[:, 2, 0:1]).then_inc(lam_d, 1)
            conv(0, 1)
            k_norm(1)
            F, L = tmp[0][0:MH, 0:SEQ], tmp[1][0:MH, 0:SEQ]
            b_row, a_row = tmp[5][0:MH, 0:SEQ], tmp[6][0:MH, 0:SEQ]
            dve.wait_ge(lnf_done, 1)
            link(nc.vector.scalar_tensor_tensor(L, F, 0.0, L, ALU.min, ALU.subtract))
            link(nc.vector.memset(tmp[7][0:MH, 0:SEQ], 1.0))
            link(nc.vector.tensor_tensor_scan(b_row, tmp[7][0:MH, 0:SEQ], L, 0.0, ALU.mult, ALU.add))
            link(nc.vector.scalar_tensor_tensor(a_row, PS[0:MH, 2], gb[:, 0:1], b_row, ALU.add, ALU.subtract))
            link(nc.vector.tensor_tensor_scan(Mrow[:], a_row, a_row, 0.0, ALU.max, ALU.max))
            nc.vector.tensor_tensor(tmp[0][0:MH, 0:SEQ], Mrow[:], b_row, ALU.add).then_inc(a_ready, 1)
            with dve.Fori(1, QKC // 2) as i:
                conv(i, 0)
                conv(i, 1)
            dve.wait_ge(at_done, 1)
            nc.vector.tensor_copy(amT[:], PS[:, 3, 0:2 * NT * MH].rearrange("p (a t h) -> p a t h", a=2, h=MH)).then_inc(at_ready, 1)
            for c in range(MC):
                if c >= 2:
                    dve.wait_ge(vT_done, c - 1)
                scaled_out(T_V + c, tmp[4 + c % 2][:, 0:SEQ])

            def head_diag(h):
                dve.wait_ge(mbc_done, h + 1)
                if h >= 1:
                    dve.wait_ge(wt_ready, 7 * h)
                nc.vector.tensor_tensor(tmp[1][:, 0:SEQ].rearrange("p (t n) -> p t n", t=NT),
                                        PS[:, 4].rearrange("p (t n) -> p t n", t=NT),
                                        big_mask.rearrange("p (a n) -> p a n", a=1).broadcast_to([P, NT, P]),
                                        ALU.add).then_inc(dg_ready, 1)

            def head_p(h):
                for s in range(NT):
                    dve.wait_ge(s_done, NT * h + s + 1)
                    dve.wait_ge(wt_ready, 7 * h + min(2 * s + 2, 7))
                    w = WT[:, W_OFF[s]:W_OFF[s] + SEQ - s * P]
                    nc.vector.scalar_tensor_tensor(w, PS[:, S_BANK[s], s * P:SEQ], MHD ** -0.5, w, ALU.mult,
                                                   ALU.mult).then_inc(p_ready, 1)

            def head_cols(h):
                dve.wait_ge(hcol, h + 1)
                dve.wait_ge(em_done, 1)
                if h >= 1:
                    dve.wait_ge(hr_wide, h)
                d, d2 = rcA[:, 0], rcA[:, 1]
                link(nc.vector.scalar_tensor_tensor(d, PS[:, 7, 0:NT], -1.0, emT[:, :, h], ALU.mult, ALU.max))
                link(nc.vector.tensor_tensor(d, d, PS[:, 7, 0:NT], ALU.max))
                link(nc.vector.tensor_scalar(d, d, 2.0 ** 57, EPS ** 0.5, ALU.min, ALU.mult))
                link(nc.vector.tensor_tensor(d2, d, d, ALU.mult))
                nc.vector.scalar_tensor_tensor(rcA[:, 2], PS[:, 7, NT:2 * NT], 1.0 / MHD, d2, ALU.mult,
                                               ALU.add).then_inc(hd2, 1)
                dve.wait_ge(hstd, h + 1)
                link(nc.vector.reciprocal(rcA[:, 3], rcA[:, 3]))
                nc.vector.tensor_copy(t512[6].rearrange("p (t n) -> p t n", t=NT),
                                      rcA[:, 3].rearrange("p (t a) -> p t a", a=1).broadcast_to([P, NT, P])).then_inc(hr_wide, 1)

            def head_norm(h):
                f, (c, r) = FULL[h], HALF[h]
                rh = t512[5]
                dve.wait_ge(hr_out, h + 1)
                nc.vector.scalar_tensor_tensor(QK[:, f], QK[:, f], col(R_HN + f), rh, ALU.mult, ALU.mult)
                q = QK[r:r + 64, c]
                nc.vector.scalar_tensor_tensor(q, q, gcol[r:r + 64, R_HN + c:R_HN + c + 1], rh[r:r + 64], ALU.mult,
                                               ALU.mult).then_inc(hnorm, 1)

            fill = [(T_XA, xqA[:, 0]), (T_XA + 1, xqA[:, 1])] + [(T_O + c, SO[:, c]) for c in range(MC)]
            for h in range(MH):
                head_diag(h)
                head_p(h)
                scaled_out(*fill[2 * h])
                if h >= 1:
                    head_norm(h - 1)
                scaled_out(*fill[2 * h + 1])
                head_cols(h)

            def cross_rq(l):
                dve.wait_ge(xq_std, l + 1)
                link(nc.vector.reciprocal(X_RQ[l][:], X_RQ[l][:]))

            def cross_max(l, c):
                i = 2 * l + c
                nm = X_NM[l]
                for b in range(4):
                    hd, t0 = b // 2, 2 * (b % 2)
                    o = nm[:, 8 * c + 2 * b:8 * c + 2 * b + 2]
                    dve.wait_ge(xs_done, 4 * i + b + 1)
                    link(nc.vector.tensor_reduce(o, PS[:, X_BANK[c] + b].rearrange("p (a n) -> p a n", a=2), AX.X,
                                                 ALU.max, negate=True))
                    nc.vector.tensor_tensor(o, o, X_RQ[l][:, c, t0:t0 + 2, hd], ALU.mult).then_inc(xmax, 1)

            def cross_p(l, c):
                i = 2 * l + c
                for hd in range(2):
                    dve.wait_ge(xexp, 8 * i + 4 * hd + 4)
                    r = X_RS[l][:, 8 * c + 4 * hd:8 * c + 4 * hd + 4]
                    link(nc.vector.reciprocal(r, r))
                    for t in range(NT):
                        j = 4 * hd + t
                        p = X_P[l][c][j]
                        nc.vector.tensor_scalar(p, p, r[:, t:t + 1], None, ALU.mult).then_inc(xp_ready, 1)

            def cross_lo(l, c):
                dve.wait_ge(xo_hi, 2 * l + c + 1)
                nc.vector.tensor_tensor(Al[:, MC + c], PS[:, X_BANK[c]], Ah[:, MC + c].bitcast(F32),
                                        ALU.subtract).then_inc(xo_ready, 1)

            cross_rq(0)
            cross_max(0, 0)
            head_norm(MH - 1)
            cross_p(0, 0)
            cross_max(0, 1)
            cross_p(0, 1)
            dve.wait_ge(hnorm, MH)
            dve.wait_ge(o_gate, 1)
            for c in range(MC):
                nc.vector.tensor_tensor(QK[:, c], QK[:, c], SO[:, c], ALU.mult).then_inc(mix_t, 1)
            cross_lo(0, 0)
            for c in range(MC):
                dve.wait_ge(mix_hi, c + 1)
                nc.vector.tensor_tensor(Al[:, c], QK[:, c], Ah[:, c].bitcast(F32), ALU.subtract).then_inc(mix_lo, 1)
            cross_lo(0, 1)

            def x_add(n, k):
                dve.wait_ge(dense_done, n + 1)
                nc.vector.tensor_tensor(xT[:, k], xT[:, k], PS[:, n % 2], ALU.add).then_inc(dense_free, 1)

            def x_phase(base, grow):
                for k in range(KD):
                    x_add(base + k, k)
                    x_chunk(k, grow)

            def ffn(l, grow):
                n0 = l * HC
                for s, (h0, nh) in enumerate(SEG):
                    base = seg_base(l, s)
                    f0 = n0 + h0
                    with dve.Fori(0, nh) as i:
                        dve.wait_ge(dense_done, i * 2 + (base + 1))
                        nc.vector.tensor_tensor(tmp[1][:, 0:SEQ], PS[:, base % 2], rinv[:], ALU.mult).then_inc(dense_free, 1)
                        dve.wait_ge(dense_done, i * 2 + (base + 2))
                        nc.vector.tensor_tensor(tmp[2][:, 0:SEQ], PS[:, (base + 1) % 2], rinv[:], ALU.mult).then_inc(dense_free, 1)
                        dve.wait_ge(dense_free, i * 2 + (base + 2))
                        dve.wait_ge(silu_done, i + (f0 + 1))
                        nc.vector.tensor_tensor(tmp[3][:, 0:SEQ], tmp[0][:, 0:SEQ], tmp[2][:, 0:SEQ], ALU.mult).then_inc(gu_ready, 1)
                        dve.wait_ge(f_hi, i + (f0 + 1))
                        one = tmp[3][:, 0:SEQ].rearrange("p (a n) -> p a n", a=1)
                        nc.vector.tensor_tensor(Al[:, bass.ds(i, 1)], one, Ah[:, bass.ds(i, 1)].bitcast(F32),
                                                ALU.subtract).then_inc(f_ready, 1)
                    down = base + 2 * nh
                    if s + 1 < len(SEG):
                        with dve.Fori(0, KD // 2) as i:
                            for j in range(2):
                                dve.wait_ge(dense_done, i * 2 + (down + j + 1))
                                xk_ = xT[:, bass.ds(i * 2 + j, 1)]
                                b = (down + j) % 2
                                nc.vector.tensor_tensor(xk_, xk_, PS[:, b:b + 1], ALU.add).then_inc(dense_free, 1)
                    elif grow is not None:
                        x_phase(down, grow)
                    else:
                        for k in range(KD):
                            x_add(down + k, k)

            x_phase(T_OUT[0], R_N2)
            x_rinv(1)
            ffn(0, R_N1 + 8)
            x_rinv(2)

            scaled_out(T_B, QKP[:, 0, 0])
            scaled_out(T_B + 1, QKP[:, 0, 1])
            C1 = 6.28125
            C2 = float(np.float32(int((2 * math.pi - C1) * 2 ** 22) / 2 ** 22))
            C3 = 2 * math.pi - C1 - C2
            MAGIC = 1.5 * 2 ** 23
            pf, an, kk = QR[:, 0], QR[:, 1], QT[:, 1]
            dve.wait_ge(pos_in, 16)
            link(nc.vector.tensor_copy(pf, posi[:]))
            link(nc.vector.tensor_scalar(an, pf, cn[:, C_INV:C_INV + 1], None, ALU.mult))
            link(nc.vector.tensor_scalar(kk, an, 1.0 / (2 * math.pi), MAGIC, ALU.mult, ALU.add))
            link(nc.vector.tensor_scalar(kk, kk, MAGIC, None, ALU.subtract))
            for part in (C1, C2, C3):
                link(nc.vector.scalar_tensor_tensor(an, kk, -part, an, ALU.mult, ALU.add))
            nc.vector.tensor_scalar(QT[:, 0], an, 3.1415925, -3.1415925, ALU.min, ALU.max).then_inc(ang, 1)
            scaled_out(T_B + 2, tmp[2][:, 0:SEQ])

            def b_rope(c):
                q2 = QKP[:, c % 2]
                nc.vector.scalar_tensor_tensor(QT[:, 0], q2[:, 0], col(R_BQ), cosT[:], ALU.mult, ALU.mult)
                nc.vector.scalar_tensor_tensor(QT[:, 1], q2[:, 1], gx[:, 2:3], cosT[:], ALU.mult, ALU.mult).then_inc(bqt, 1)
                sinb = sinT[:].rearrange("p (a n) -> p a n", a=1).broadcast_to([P, 2, SEQ])
                dve.wait_ge(brot, c + 1)
                link(nc.vector.tensor_tensor(QR[:], PS[:, 2:4], sinb, ALU.mult))
                dve.wait_ge(bqt, c + 1)
                nc.vector.tensor_tensor(QR[:], QR[:], QT[:], ALU.add).then_inc(bqr, 1)

            def b_norm(c):
                dve.wait_ge(bqk_std, c + 1)
                link(nc.vector.reciprocal(rqk_all[:], rqk[:]))
                nc.vector.tensor_copy(t512[4].rearrange("p (t h n) -> p (t h) n", t=NT, h=2),
                                      rqk_all[:, 1].rearrange("p t (h a) -> p (t h) a", a=1).broadcast_to([P, 2 * NT, 64])).then_inc(bn_ready, 1)

            def b_onorm(c):
                dve.wait_ge(bo_std, c + 1)
                link(nc.vector.reciprocal(ro_all[:], roB[:]))
                nc.vector.tensor_copy(t512[7].rearrange("p (t n) -> p t n", t=NT),
                                      ro_all[:].rearrange("p (t a) -> p t a", a=1).broadcast_to([P, NT, P])).then_inc(bon_ready, 1)

            def b_knorm(c):
                dve.wait_ge(bk_bc, c + 1)
                dve.wait_ge(bqr, c + 1)
                nc.vector.tensor_tensor(QR[:, 1], QR[:, 1], PS[:, 7], ALU.mult).then_inc(bkr, 1)

            def b_max(c, u):
                t, b = NT - 1 - u, 6 - 2 * (u % 2)
                n = 4 * c + u
                dve.wait_ge(bs_done, n + 1)
                dg = PS[:, b:b + 2, t * P:(t + 1) * P]
                link(nc.vector.tensor_tensor(dg, dg, neg_mask.rearrange("p (a n) -> p a n", a=1).broadcast_to([P, 2, P]), ALU.add))
                j = (8 * c + 2 * u) % 64
                link(nc.vector.tensor_reduce(nmB[:, j:j + 2], PS[:, b:b + 2, 0:(t + 1) * P], AX.X, ALU.max, negate=True))
                nc.vector.tensor_tensor(nmB[:, j:j + 2], nmB[:, j:j + 2], rqk_all[:, 0, t], ALU.mult).then_inc(bmax, 1)

            def b_prob(c, u):
                t = NT - 1 - u
                n = 4 * c + u
                j = (8 * c + 2 * u) % 64
                w = slice(W_OFF[u], W_OFF[u] + (t + 1) * P)
                dve.wait_ge(bexp, 2 * n + 2)
                link(nc.vector.reciprocal(rsB[:, j:j + 2], rsB[:, j:j + 2]))
                link(nc.vector.tensor_scalar(PB[:, 1, w], PB[:, 1, w], rsB[:, j + 1:j + 2], lam[:], ALU.mult, ALU.mult))
                nc.vector.scalar_tensor_tensor(PB[:, 0, w], PB[:, 0, w], rsB[:, j:j + 1], PB[:, 1, w], ALU.mult,
                                               ALU.subtract).then_inc(ba_ready, 1)

            def b_mix(c):
                dve.wait_ge(bo_bc, c + 1)
                link(nc.vector.tensor_scalar(t512[5], PS[:, 4], gx[:, 3:4], None, ALU.mult))
                nc.vector.tensor_tensor(t512[5], t512[5], PS[:, 5], ALU.mult).then_inc(bmix_t, 1)

            def b_lo(c):
                dve.wait_ge(bmix_hi, c + 1)
                nc.vector.tensor_tensor(Al[:, c], t512[5], Ah[:, c].bitcast(F32), ALU.subtract).then_inc(bmix_lo, 1)

            for c in range(MC):
                n = T_B + 3 * (c + 1)
                last = c + 1 == MC
                if c == 0:
                    dve.wait_ge(trig, 2)
                b_rope(c)
                b_norm(c)
                if c >= 1:
                    b_onorm(c - 1)
                scaled_out(n, xqB[:, 0] if last else QKP[:, (c + 1) % 2, 0])
                b_knorm(c)
                if c >= 1:
                    b_mix(c - 1)
                b_max(c, 0)
                scaled_out(n + 1, xqB[:, 1] if last else QKP[:, (c + 1) % 2, 1])
                b_max(c, 1)
                b_prob(c, 0)
                b_max(c, 2)
                b_prob(c, 1)
                b_max(c, 3)
                b_prob(c, 2)
                b_prob(c, 3)
                if c >= 1:
                    b_lo(c - 1)
                if not last:
                    if c >= 1:
                        dve.wait_ge(bvt_done, c)
                    scaled_out(n + 2, t512[2 + (c + 1) % 2])
            cross_rq(1)
            b_onorm(MC - 1)
            cross_max(1, 0)
            b_mix(MC - 1)
            cross_p(1, 0)
            cross_max(1, 1)
            cross_p(1, 1)
            b_lo(MC - 1)
            cross_lo(1, 0)
            cross_lo(1, 1)
            x_phase(T_OUT[1], R_N2 + 8)
            x_rinv(3)
            ffn(1, None)

        @block.tensor
        def _(pe):
            def mm(out_, a, b, start=True, stop=True):
                return nc.tensor.matmul(out_, a, b, start=start, stop=stop)

            pe.wait_ge(con_in, 16)
            pe.wait_ge(prm_in, 16)
            nc.tensor.transpose(PS[:, 2, 0:N_PRM], prm[0:N_PRM, :], ident[0:N_PRM, 0:N_PRM]).then_inc(prm_t, 1)
            pe.wait_ge(mem_in, 16)

            def tr_group(g, blocks):
                if g >= 4:
                    pe.wait_ge(tr_free, g - 3)
                for j, b in enumerate(blocks):
                    last = nc.tensor.transpose(PS[:, 4 + g % 4, j * P:(j + 1) * P], b, ident)
                last.then_inc(tr_done, 1)

            for g in range(4):
                tr_group(g, [m_st[:, t, (2 * g + a) * P:(2 * g + a + 1) * P] for a in range(2) for t in range(MT_TILES)])

            def tile(i, n0, hi, lo, nk=8, step=2, ready=None, n=SEQ, between=None):
                sl = n0 % SPLIT
                pe.wait_ge(w_split, i * step + (n0 + 1))
                if not (isinstance(i, int) and n0 + step * i < 2):
                    pe.wait_ge(dense_free, i * step + (n0 - 1))
                for k in range(nk):
                    if ready:
                        for s_, v_ in ready(k):
                            pe.wait_ge(s_, v_)
                    for j, (w, a) in enumerate(((w_hi, hi), (w_hi, lo), (w_lo, hi))):
                        last = mm(PS[:, sl, 0:n], w[:, sl, k], a(k), start=(k == 0 and j == 0), stop=(k == nk - 1 and j == 2))
                    if k == nk - 1:
                        last.then_inc(dense_done, 1)
                    for small in (between or {}).get(k, ()):
                        small()

            def h_tile(n0, i=0, ready=None, between=None):
                tile(i, n0, lambda k: Hh[:, k], lambda k: Hl[:, k], ready=ready, between=between)

            def a_tile(n0, i=0, ready=None, nk=8, between=None):
                tile(i, n0, lambda k: Ah[:, k], lambda k: Al[:, k], nk=nk, ready=ready, between=between)

            def m_tile(n):
                l = n // 4

                def part(A):
                    return lambda k: A[:, 4 * l:4 * l + 4].rearrange("p a n -> p (a n)")[:, k * MEM:(k + 1) * MEM]
                tile(0, n, part(Ah), part(Al), n=MEM, ready=(lambda k: [(mg_ready, 8 * l + k + 1)]) if n % 4 == 0 else None)

            pe.wait_ge(set_done, 4)
            for k in range(KD):
                pe.wait_ge(msq_done, k // 2 + 1)
                last = mm(PS[:, 3, 0:MEM], ones[:], msq[:, k], start=k == 0, stop=k == KD - 1)
            last.then_inc(mss_done, 1)
            m_tile(0)
            m_tile(1)
            m_tile(2)
            pe.wait_ge(x_in, 16)
            for k in range(4):
                tr_group(4 + k, [x_st[:, t, k * P:(k + 1) * P] for t in range(NT)])
            m_tile(3)
            m_tile(4)
            for k in range(4, 8):
                tr_group(4 + k, [x_st[:, t, k * P:(k + 1) * P] for t in range(NT)])
            m_tile(5)
            m_tile(6)
            m_tile(7)

            def k_ss(l):
                pe.wait_ge(ksq, l + 1)
                pe.wait_ge(tr_free, 12)
                mm(PS[:, 4 + l], bdiag, kvs[:]).then_inc(kss, 1)
                pe.wait_ge(dense_free, 4 * l + 4)
                if l == 1:
                    pe.wait_ge(vtr_out, 1)
                for t in range(MT_TILES):
                    for c in range(2):
                        last = nc.tensor.transpose(PS[:, 6, (2 * t + c) * P:(2 * t + c + 1) * P],
                                                   kv[:, l, 2 + c, t * P:(t + 1) * P], ident)
                last.then_inc(vtr, 1)

            def x_ss(i):
                pe.wait_ge(xsq_used, KD * (i + 1))
                mm(PS[:, SS_BANK], ones[:], acc[:]).then_inc(ss_done, 1)

            h_tile(T_GATE, ready=lambda k: [(h_ready, k + 1)])
            x_ss(0)
            k_ss(0)
            pe.wait_ge(lam_d, 1)
            mm(PS[:, 2, 0:1], ones[0:1, :], lame[0:1, 0:1]).then_inc(lam_b, 1)
            h_tile(T_QK)
            h_tile(T_QK + 1)
            k_ss(1)
            pe.wait_ge(dense_free, T_GATE + 1)
            pe.wait_ge(lam_d, 2)
            mm(PS[0:MH, 2], cn[0:8, C_GSEL:C_GSEL + MH], tmp[4][0:8, 0:SEQ])
            mm(PS[0:MH, 3], cn[0:8, C_GSEL + MH:C_GSEL + 2 * MH], tmp[4][0:8, 0:SEQ]).then_inc(gsel_done, 1)
            with pe.Fori(1, QKC // 2) as i:
                h_tile(T_QK, i)
                h_tile(T_QK + 1, i)
            pe.wait_ge(a_ready, 1)
            for i, row in enumerate((tmp[6], tmp[0])):
                for t in range(NT):
                    last = nc.tensor.transpose(PS[:, 3, (i * NT + t) * MH:(i * NT + t + 1) * MH], row[0:MH, t * P:(t + 1) * P],
                                               ident[0:MH, 0:MH])
            last.then_inc(at_done, 1)

            def v_tr(c):
                pe.wait_ge(dense_free, T_V + c + 1)
                if c >= 2:
                    pe.wait_ge(v_ready, c - 1)
                for t in range(NT):
                    last = nc.tensor.transpose(PS[:, 4 + c % 2, t * P:(t + 1) * P], tmp[4 + c % 2][:, t * P:(t + 1) * P], ident)
                last.then_inc(vT_done, 1)

            for c in range(MC):
                h_tile(T_V + c)
                if c >= 1:
                    v_tr(c - 1)
            v_tr(MC - 1)

            def head_scores(h):
                f, (c, r) = FULL[h], HALF[h]
                if h == 0:
                    pe.wait_ge(v_ready, MC)
                    pe.wait_ge(at_ready, 1)
                    pe.wait_ge(qk_ready, QKC)
                else:
                    pe.wait_ge(num_out, 2 * h)
                mm(PS[:, 4], cn[0:MH, C_SEL + h * P:C_SEL + (h + 1) * P], Mrow[:]).then_inc(mbc_done, 1)
                for s in range(NT):
                    o = PS[:, S_BANK[s], s * P:SEQ]
                    if h >= 1:
                        pe.wait_ge(p_ready, NT * (h - 1) + s + 1)
                    if h >= 1 and s == NT - 1:
                        pe.wait_ge(hd2, h)
                    mm(o, QK[:, MC + f, s * P:(s + 1) * P], QK[:, f, s * P:SEQ], stop=False)
                    mm(o, QK[r:r + 64, MC + c, s * P:(s + 1) * P], QK[r:r + 64, c, s * P:SEQ], start=False).then_inc(s_done, 1)

            def head_pv(h):
                f, (c, r) = FULL[h], HALF[h]
                if h >= 1:
                    pe.wait_ge(hr_out, h)
                for s in range(NT):
                    pe.wait_ge(p_ready, NT * h + s + 1)
                    w = WT[:, W_OFF[s]:W_OFF[s] + SEQ - s * P]
                    st, sp_ = s == 0, s == NT - 1
                    if s == 0:
                        pe.wait_ge(wt_ready, 7 * h + 7)
                    mm(PS[:, 5, s * P:SEQ], V[:, s, f * P:(f + 1) * P], w, start=st, stop=sp_)
                    last = mm(PS[r:r + 64, 4, s * P:SEQ], V[:, s, c * P + r:c * P + r + 64], w, start=st, stop=sp_)
                last.then_inc(num_done, 1)

            def head_den(h, t):
                for s in range(t + 1):
                    mm(PS[:, 7, t:t + 1], WT[:, W_OFF[s] + (t - s) * P:W_OFF[s] + (t - s + 1) * P], ones[:, 0:1],
                       start=s == 0, stop=s == t)

            def head_ss(h, t):
                c, r = HALF[h]
                if t == 0:
                    pe.wait_ge(hsq, 2 * h + 2)
                o = PS[:, 7, NT + t:NT + t + 1]
                mm(o, t512[3][:, t * P:(t + 1) * P], ones[:, 0:1], stop=False)
                last = mm(o, t512[4][r:r + 64, t * P:(t + 1) * P], ones[r:r + 64, 0:1], start=False)
                if t == NT - 1:
                    last.then_inc(hcol, 1)

            def head_r(h):
                pe.wait_ge(hr_wide, h + 1)
                for t in range(NT):
                    last = nc.tensor.transpose(PS[:, 5, t * P:(t + 1) * P], t512[6][:, t * P:(t + 1) * P], ident)
                last.then_inc(hr_done, 1)

            def cross_ss(l, c, t):
                if c == 0 and t == 0:
                    pe.wait_ge(xq_sq, 2 * l + 2)
                    if l == 0:
                        pe.wait_ge(p_ready, NT * (MH - 1) + 1)
                    else:
                        pe.wait_ge(dense_free, T_OUT[1])
                j = 2 * (NT * c + t)
                last = mm(PS[:, XSS_BANK[l], j:j + 2], X_SQ[l][c][:, t * P:(t + 1) * P], half_sel)
                if c == 1 and t == NT - 1:
                    last.then_inc(xq_ss, 1)

            def part(f, *a):
                return lambda: f(*a)

            fill = [T_XA, T_XA + 1] + [T_O + c for c in range(MC)]
            for h in range(MH):
                head_scores(h)
                if h >= 1:
                    head_r(h - 1)
                h_tile(fill[2 * h], between={3 + t: [part(cross_ss, 0, c, t) for c in range(2)] for t in range(NT)} if h == MH - 1 else None)
                head_pv(h)
                h_tile(fill[2 * h + 1], between={**{t: [part(head_den, h, t)] for t in range(NT)},
                                                 **{3 + t: [part(head_ss, h, t)] for t in range(1, NT)},
                                                 3: [part(head_den, h, 3), part(head_ss, h, 0)]})

            def cross_s(l, c, between=None):
                for b in range(4):
                    r = 64 * (b // 2)
                    for a in range(2):
                        t = 2 * (b % 2) + a
                        last = mm(PS[:, X_BANK[c] + b, a * MEM:(a + 1) * MEM], (xqA, xqB)[l][r:r + 64, c, t * P:(t + 1) * P],
                                  xk[r:r + 64, l, c])
                    last.then_inc(xs_done, 1)
                    if between and b in between:
                        between[b]()

            def cross_t(l, c):
                i = 2 * l + c
                for b in range(4):
                    hd, mt = b // 2, b % 2
                    pe.wait_ge(xp_ready, 8 * i + 4 * hd + 4)
                    for t in range(NT):
                        last = nc.tensor.transpose(PS[:, X_BANK[c] + b, t * P:(t + 1) * P],
                                                   X_P[l][c][4 * hd + t][:, mt * P:(mt + 1) * P], ident)
                    last.then_inc(xpt_done, 1)

            def cross_pv(l, c):
                i = 2 * l + c
                for hd in range(2):
                    for mt in range(MT_TILES):
                        pe.wait_ge(xpt_ready, 4 * i + 2 * hd + mt + 1)
                        last = mm(PS[64 * hd:64 * hd + 64, X_BANK[c]], xv[:, l, mt, (2 * c + hd) * 64:(2 * c + hd + 1) * 64],
                                  X_PT[l][c][2 * hd + mt], start=mt == 0, stop=mt == 1)
                last.then_inc(xo_done, 1)

            pe.wait_ge(dense_free, T_OUT[0])
            pe.wait_ge(xq_std, 1)
            pe.wait_ge(p_ready, NT * MH)
            cross_s(0, 0, between={1: part(head_r, MH - 1)})
            pe.wait_ge(num_out, 2 * MH)
            pe.wait_ge(hd2, MH)
            pe.wait_ge(hr_out, MH)
            cross_s(0, 1)
            cross_t(0, 0)
            cross_t(0, 1)
            cross_pv(0, 0)
            cross_pv(0, 1)

            def out_proj(l, ready):
                a_tile(T_OUT[l], ready=ready)
                a_tile(T_OUT[l] + 1)
                with pe.Fori(1, KD // 2) as i:
                    a_tile(T_OUT[l], i)
                    a_tile(T_OUT[l] + 1, i)

            pe.wait_ge(xo_ready, 1)
            out_proj(0, lambda k: [(mix_lo, k + 1)] if k < MC else [(xo_ready, k - MC + 1)])

            def out_t(k, t):
                if t == 0:
                    pe.wait_ge(dense_free, seg_base(1, 2) + 2 * SEG[2][1] + k + 1)
                    if k >= 2:
                        pe.wait_ge(ot_out, k - 1)
                last = nc.tensor.transpose(PS[:, 2 + k % 2, t * P:(t + 1) * P], xT[:, k, t * P:(t + 1) * P], ident)
                if t == NT - 1:
                    last.then_inc(ot_done, 1)

            def ffn(l):
                n0 = l * HC
                for s, (h0, nh) in enumerate(SEG):
                    base = seg_base(l, s)
                    if s == 0:
                        h_tile(base, ready=lambda k: [(h_ready, KD * (2 * l + 1) + k + 1)])
                        x_ss(2 * l + 1)
                        h_tile(base + 1)
                    with pe.Fori(1 if s == 0 else 0, nh) as i:
                        h_tile(base, i)
                        h_tile(base + 1, i)
                    down = base + 2 * nh
                    a_tile(down, nk=nh, ready=lambda k: [(f_ready, n0 + h0 + k + 1)])
                    a_tile(down + 1, nk=nh)
                    if l == 1 and s == len(SEG) - 1:
                        for j in range(2, KD):
                            a_tile(down + j, nk=nh, between={1 + t: [part(out_t, j - 2, t)] for t in range(NT)})
                        break
                    with pe.Fori(1, KD // 2) as i:
                        a_tile(down, i, nk=nh)
                        a_tile(down + 1, i, nk=nh)

            ffn(0)

            h_tile(T_B, ready=lambda k: [(h_ready, 2 * KD + k + 1)])
            x_ss(2)
            h_tile(T_B + 1)
            h_tile(T_B + 2)

            def b_ss(c, a, t):
                if a == 0 and t == 0:
                    pe.wait_ge(bsq, c + 1)
                    if c >= 1:
                        pe.wait_ge(bexp, 8 * c)
                j = 2 * (NT * a + t)
                last = mm(PS[:, 6, j:j + 2], QS[:, a, t * P:(t + 1) * P], half_sel)
                if c == 0 and a == 1 and t == NT - 1:
                    last.then_inc(bss, 1)

            def b_oss(c, t):
                if t == 0:
                    pe.wait_ge(bosq, c + 1)
                last = mm(PS[:, 6, 16 + t:17 + t], t512[6][:, t * P:(t + 1) * P], ones[:, 0:1])
                if t == NT - 1:
                    last.then_inc(bss, 1)

            def b_rot(c):
                pe.wait_ge(dense_free, T_B + 3 * c + 2)
                if c >= 1:
                    pe.wait_ge(bat_ready, 4 * c)
                mm(PS[:, 2], rot_q[:], QKP[:, c % 2, 0])
                mm(PS[:, 3], rot_k[:], QKP[:, c % 2, 1]).then_inc(brot, 1)

            def b_kbc(c, t):
                if t == 0:
                    pe.wait_ge(bn_ready, c + 1)
                last = nc.tensor.transpose(PS[:, 7, t * P:(t + 1) * P], t512[4][:, t * P:(t + 1) * P], ident)
                if t == NT - 1:
                    last.then_inc(bk_bc, 1)

            def b_obc(c, t):
                if t == 0:
                    pe.wait_ge(bon_ready, c + 1)
                last = nc.tensor.transpose(PS[:, 5, t * P:(t + 1) * P], t512[7][:, t * P:(t + 1) * P], ident)
                if t == NT - 1:
                    last.then_inc(bo_bc, 1)

            def b_vt(c, t):
                if t == 0:
                    pe.wait_ge(dense_free, T_B + 3 * c + 3)
                    pe.wait_ge(bqr, c + 1)
                last = nc.tensor.transpose(PS[:, 2, t * P:(t + 1) * P], t512[2 + c % 2][:, t * P:(t + 1) * P], ident)
                if t == NT - 1:
                    last.then_inc(bvt_done, 1)

            def b_s(c, u):
                t, b = NT - 1 - u, 6 - 2 * (u % 2)
                if u == 0:
                    pe.wait_ge(bkr, c + 1)
                if u == 1 and c >= 1:
                    pe.wait_ge(bmix_t, c)
                if u >= 2:
                    pe.wait_ge(bexp, 2 * (4 * c + u - 2) + 2)
                for hd in range(2):
                    r = 64 * hd
                    last = mm(PS[:, b + hd, 0:(t + 1) * P], QR[r:r + 64, 0, t * P:(t + 1) * P], QR[r:r + 64, 1, 0:(t + 1) * P])
                last.then_inc(bs_done, 1)

            def b_t(c, u):
                t = NT - 1 - u
                pe.wait_ge(ba_ready, 4 * c + u + 1)
                if u == 0:
                    pe.wait_ge(bv_ready, c + 1)
                if u >= 2:
                    pe.wait_ge(bat_ready, 4 * c + u - 1)
                for k in range(t + 1):
                    last = nc.tensor.transpose(PS[:, 2 + u % 2, k * P:(k + 1) * P], PB[:, 0, W_OFF[u] + k * P:W_OFF[u] + (k + 1) * P], ident)
                last.then_inc(bt_done, 1)

            def b_pv(c):
                pe.wait_ge(bat_ready, 4 * c + 4)
                for k in range(NT):
                    last = mm(PS[:, 4, k * P:SEQ], VB[:, c % 2, k], ATB[:, k, k * P:SEQ], start=k == 0, stop=k == NT - 1)
                last.then_inc(bpv, 1)

            b_rot(0)
            for c in range(MC):
                n = T_B + 3 * (c + 1)
                cols = {t: [part(b_ss, c, a, t) for a in range(2)] for t in range(NT)}
                if c >= 1:
                    cols[0] = [part(b_pv, c - 1), part(b_rot, c)] + cols[0]
                    cols[4] = [part(b_oss, c - 1, t) for t in range(2)]
                    cols[5] = [part(b_oss, c - 1, t) for t in range(2, NT)]
                h_tile(n, between=cols)
                turns = {0: [part(b_kbc, c, t) for t in range(2)], 1: [part(b_kbc, c, t) for t in range(2, NT)],
                         4: [part(b_s, c, 0)], 5: [part(b_vt, c, t) for t in range(2)],
                         6: [part(b_vt, c, t) for t in range(2, NT)], 7: [part(b_s, c, 1)]}
                if c >= 1:
                    turns[2] = [part(b_obc, c - 1, t) for t in range(2)]
                    turns[3] = [part(b_obc, c - 1, t) for t in range(2, NT)]
                h_tile(n + 1, between=turns)
                if c + 1 < MC:
                    h_tile(n + 2, between={0: [part(b_s, c, 2)], 2: [part(b_s, c, 3)],
                                           **{4 + u: [part(b_t, c, u)] for u in range(NT)}})
                else:
                    b_s(c, 2)
                    b_s(c, 3)
                    for t in range(NT):
                        for xc in range(2):
                            cross_ss(1, xc, t)
                    for u in range(NT):
                        b_t(c, u)
            b_pv(MC - 1)

            def last_oss():
                for t in range(NT):
                    b_oss(MC - 1, t)

            pe.wait_ge(bat_ready, 4 * MC)
            pe.wait_ge(xq_std, 2)
            cross_s(1, 0, between={0: last_oss})
            for t in range(NT):
                b_obc(MC - 1, t)
            pe.wait_ge(bmix_t, MC)
            cross_s(1, 1)
            cross_t(1, 0)
            cross_t(1, 1)
            cross_pv(1, 0)
            cross_pv(1, 1)
            pe.wait_ge(xo_ready, 3)
            out_proj(1, lambda k: [(bmix_lo, k + 1)] if k < MC else [(xo_ready, k - MC + 3)])
            ffn(1)
            for k in range(KD - 2, KD):
                for t in range(NT):
                    out_t(k, t)


_INS = ['x', 'mem', 'positions', 'w_out', 'w_mem_kv', 'w_gate_up', 'w_down', 'a_w_in', 'a_gate_b', 'b_w_in',
        'b_lambda']
_ROWS = ['norm1', 'norm2', 'mem_norm', 'a_conv_w', 'a_conv_b', 'a_head_norm', 'b_subln']
_HALF_ROWS = ['xq_norm', 'xk_norm', 'b_q_norm', 'b_k_norm']
_OUTS = [((1, SEQ, D), 'float32')]


def kernel(**inputs):
    import numpy as _np
    import concourse.bacc as _bacc
    from concourse import mybir as _mybir
    from concourse.bass_utils import run_bass_kernel_spmd as _run

    nc = _bacc.Bacc("TRN2", target_bir_lowering=False, num_devices=1)
    arrays, args = {}, []
    for name in _INS:
        a = _np.ascontiguousarray(inputs[name])
        arrays[f"in_{name}_dram"] = a
        args.append(nc.dram_tensor(f"in_{name}_dram", a.shape, _mybir.dt.from_np(a.dtype), kind="ExternalInput").ap())
    rows = [_np.asarray(inputs[name]).reshape(-1, P) for name in _ROWS]
    rows += [_np.concatenate([_np.asarray(inputs[name])] * 2, axis=1) for name in _HALF_ROWS]
    for name, a in (("rows", _np.ascontiguousarray(_np.concatenate(rows))), ("constants", constants())):
        arrays[f"in_{name}_dram"] = a
        args.append(nc.dram_tensor(f"in_{name}_dram", a.shape, _mybir.dt.from_np(a.dtype), kind="ExternalInput").ap())
    for i, (shape, dtype) in enumerate(_OUTS):
        dt = _mybir.dt.from_np(_np.dtype(dtype))
        args.append(nc.dram_tensor(f"out_{i}_dram", shape, dt, kind="ExternalOutput").ap())
    hybrid_trunk(nc, *args)
    r = _run(nc, [arrays], core_ids=[0])
    return r.results[0]["out_0_dram"]
```

```python
import math
from contextlib import ExitStack

import concourse.bass as bass
import numpy as np
from concourse import mybir

F32 = mybir.dt.float32
F32R = mybir.dt.float32r
I32 = mybir.dt.int32
ALU = mybir.AluOpType
ACT = mybir.ActivationFunctionType
AX = mybir.AxisListType

P = 128
D = 1024
SEQ = 512
MEM = 256
KD = D // P
NT = SEQ // P
MT_TILES = MEM // P
MIX = 768
XW = 256
XH_DIM = 64
MH = 4
MHD = MIX // MH
VW = MHD + 1
CONV = 4
QKC = 2 * MIX // P
MC = MIX // P
FFN = 2816
HC = FFN // P
A_IN = 4 * MIX + 2 * MH + XW
B_IN = 3 * MIX + XW
GATE_COL = 4 * MIX
XQ_COL_A = 4 * MIX + 2 * MH
LAMBDA_INIT = 0.8 - 0.6 * math.exp(-0.3 * 1)
EPS = 1e-6
RAW = 4
SPLIT = 2

R_N1, R_N2, R_MN, R_CW, R_CB, R_HN, R_SL, R_XQ, R_XK, R_BQ, R_BK = 0, 16, 32, 48, 96, 108, 114, 115, 117, 119, 120
N_PRM = 121

C_ID, C_BD, C_ROT, C_NEG, C_BIG, C_SEL, C_GSEL, C_INV = 0, 128, 256, 384, 512, 640, 640 + MH * P, 640 + MH * P + 8
N_CON = C_INV + 1


def constants():
    c = np.zeros((P, N_CON), np.float32)
    r = np.arange(P)
    c[:, C_ID:C_ID + P] = np.eye(P)
    c[:, C_BD:C_BD + P] = r[:, None] // 64 == r[None, :] // 64
    rot = np.zeros((P, P), np.float32)
    for j in range(P):
        rot[j + 32 if j % 64 < 32 else j - 32, j] = -1.0 if j % 64 < 32 else 1.0
    c[:, C_ROT:C_ROT + P] = rot
    c[:, C_NEG:C_NEG + P] = np.where(r[None, :] > r[:, None], -1e30, 0.0)
    c[:, C_BIG:C_BIG + P] = np.where(r[None, :] < r[:, None], 1e30, 0.0)
    for h in range(MH):
        c[h, C_SEL + h * P:C_SEL + (h + 1) * P] = 1.0
    for j in range(8):
        c[j, C_GSEL + j] = 1.0
    inv = np.power(np.float32(10000.0), -np.arange(32, dtype=np.float32) * np.float32(2.0) / np.float32(64))
    c[:, C_INV] = inv[r % 32]
    return c


T_MEM = 0
T_GATE = T_MEM + 8
T_QK = T_GATE + 1
T_V = T_QK + QKC
T_XA = T_V + MC
T_O = T_XA + 2
T_OUT = [T_O + MC, 0]
SEG = [(0, 8), (8, 8), (16, 6)]
N_FFN = 2 * HC + KD * len(SEG)
T_FFN = [T_OUT[0] + KD, 0]
T_B = T_FFN[0] + N_FFN
T_XB = T_B + 3 * MC
T_OUT[1] = T_XB + 2
T_FFN[1] = T_OUT[1] + KD
N_TILES = T_FFN[1] + N_FFN


def seg_base(layer, s):
    return T_FFN[layer] + sum(2 * n + KD for _, n in SEG[:s])


def tile_k(n):
    for layer in range(2):
        for s, (_, nh) in enumerate(SEG):
            down = seg_base(layer, s) + 2 * nh
            if down <= n < down + KD:
                return nh
    return 8


def hybrid_trunk(nc, x, mem, positions, w_out, w_mem_kv, w_gate_up, w_down, a_w_in, a_gate_b, b_w_in,
                 b_lambda, prm_rows, con, out):
    ctx = ExitStack()
    with ctx:
        def sb(name, shape, dt=F32, scope=ctx):
            return scope.enter_context(nc.sbuf_tensor(name, shape, dt))

        def sem(name):
            return ctx.enter_context(nc.semaphore(name))

        PS = ctx.enter_context(nc.psum_tensor("PS", [P, 8, 512], F32))

        xT = sb("xT", [P, KD, SEQ])
        Hh = sb("Hh", [P, KD, SEQ], F32R)
        Hl = sb("Hl", [P, KD, SEQ], F32R)
        Ah = sb("Ah", [P, 8, SEQ], F32R)
        Al = sb("Al", [P, 8, SEQ], F32R)
        w_raw = sb("w_raw", [P, RAW, 8, P])
        w_hi = sb("w_hi", [P, SPLIT, 8, P], F32R)
        w_lo = sb("w_lo", [P, SPLIT, 8, P], F32R)
        cn = sb("cn", [P, N_CON])
        ones = sb("ones", [P, P])
        gcol = sb("gcol", [P, N_PRM])
        gx = sb("gx", [P, 5])
        grot = sb("grot", [P, 2])
        epsc = sb("epsc", [P, 1])
        hpi = sb("hpi", [P, 1])
        eps64 = sb("eps64", [P, 1])
        rinv = sb("rinv", [P, SEQ])
        acc = sb("acc", [P, SEQ])
        xk = sb("xk", [P, 2, 2, MEM])
        xv = sb("xv", [P, 2, MT_TILES, XW])
        lam = sb("lam", [P, 1])
        lame = sb("lame", [1, 4])
        ident = cn[:, C_ID:C_ID + P]
        bdiag = cn[:, C_BD:C_BD + P]
        rotm = cn[:, C_ROT:C_ROT + P]
        half_sel = bdiag[:, 0:P:64]
        neg_mask = cn[:, C_NEG:C_NEG + P]
        big_mask = cn[:, C_BIG:C_BIG + P]

        tmp = [sb(f"tmp{i}", [P, 516]) for i in range(8)]

        s0 = ExitStack()
        x_st = sb("x_st", [P, NT, D], scope=s0)
        m_st = sb("m_st", [P, MT_TILES, D], scope=s0)
        prm = sb("prm", [P, P], scope=s0)
        mT = sb("mT", [P, KD, MEM], scope=s0)
        msq = sb("msq", [P, KD, MEM], scope=s0)
        rm = sb("rm", [P, MEM], scope=s0)
        kv = sb("kv", [P, 2, 4, MEM], scope=s0)
        kvs = sb("kvs", [P, 512], scope=s0)
        lamv = sb("lamv", [1, 4, 64], scope=s0)
        lamw = sb("lamw", [1, 2, 64], scope=s0)
        s0.close()
        sA = ExitStack()
        QK = sb("QK", [P, QKC, SEQ], scope=sA)
        V = sb("V", [P, NT, MH * VW], scope=sA)
        SO = sb("SO", [P, MC, SEQ], scope=sA)
        xqA = sb("xqA", [P, 2, SEQ], scope=sA)
        WT = sb("WT", [P, 1280], scope=sA)
        Mrow = sb("Mrow", [MH, SEQ], scope=sA)
        amT = sb("amT", [P, 2, NT, MH], scope=sA)
        emT = sb("emT", [P, NT, MH], scope=sA)
        rcA = sb("rcA", [P, 5, NT], scope=sA)
        rqA = sb("rqA", [P, 2, NT, 2], scope=sA)
        gb = sb("gb", [MH, 2], scope=sA)
        nmA = sb("nmA", [P, 16], scope=sA)
        rsA = sb("rsA", [P, 16], scope=sA)
        sA.close()
        sB = ExitStack()
        QKP = sb("QKP", [P, 2, 2, SEQ], scope=sB)
        VB = sb("VB", [P, 2, NT, P], scope=sB)
        PB = sb("PB", [P, 2, 1280], scope=sB)
        ATB = sb("ATB", [P, NT, SEQ], scope=sB)
        QKR = sb("QKR", [P, 2, SEQ], scope=sB)
        QS = sb("QS", [P, 2, SEQ], scope=sB)
        QT = sb("QT", [P, 2, SEQ], scope=sB)
        QR = sb("QR", [P, 2, SEQ], scope=sB)
        cosT = sb("cosT", [P, SEQ], scope=sB)
        sinT = sb("sinT", [P, SEQ], scope=sB)
        xqB = sb("xqB", [P, 2, SEQ], scope=sB)
        nmB = sb("nmB", [P, 64], scope=sB)
        rsB = sb("rsB", [P, 64], scope=sB)
        posi = sb("posi", [P, SEQ], I32, scope=sB)
        rqk = sb("rqk", [P, 2, NT, 2], scope=sB)
        rqk_all = sb("rqk_all", [P, 2, NT, 2], scope=sB)
        roB = sb("roB", [P, NT], scope=sB)
        ro_all = sb("ro_all", [P, NT], scope=sB)
        rqB = sb("rqB", [P, 2, NT, 2], scope=sB)
        nmX = sb("nmX", [P, 16], scope=sB)
        rsX = sb("rsX", [P, 16], scope=sB)
        sB.close()
        sC = ExitStack()
        o_st = sb("o_st", [P, 2, NT, P], scope=sC)
        sC.close()

        w_in = [sem(f"w_in{i}") for i in range(RAW)]
        w_round = sem("w_round")
        w_split = sem("w_split")
        dense_done = sem("dense_done")
        dense_free = sem("dense_free")
        con_in = sem("con_in")
        prm_in = sem("prm_in")
        mem_in = sem("mem_in")
        x_in = sem("x_in")
        set_done = sem("set_done")
        prm_t = sem("prm_t")
        g_ready = sem("g_ready")
        tr_done = sem("tr_done")
        tr_free = sem("tr_free")
        msq_done = sem("msq_done")
        mss_done = sem("mss_done")
        mstd_done = sem("mstd_done")
        mhi = sem("mhi")
        mg_ready = sem("mg_ready")
        ksq = sem("ksq")
        kss = sem("kss")
        kstd = sem("kstd")
        kn_ready = sem("kn_ready")
        vtr = sem("vtr")
        vtr_out = sem("vtr_out")
        vch = sem("vch")
        ach = sem("ach")
        xsq = sem("xsq")
        xsq_used = sem("xsq_used")
        h_hi = sem("h_hi")
        h_ready = sem("h_ready")
        ss_done = sem("ss_done")
        std_done = sem("std_done")
        gsel_done = sem("gsel_done")
        lnf_done = sem("lnf_done")
        a_ready = sem("a_ready")
        at_done = sem("at_done")
        at_ready = sem("at_ready")
        conv_done = sem("conv_done")
        conv_step = sem("conv_step")
        qk_ready = sem("qk_ready")
        o_gate = sem("o_gate")
        vT_done = sem("vT_done")
        v_ready = sem("v_ready")
        v_ones = sem("v_ones")
        mbc_done = sem("mbc_done")
        s_done = sem("s_done")
        dg_ready = sem("dg_ready")
        em_done = sem("em_done")
        wt_ready = sem("wt_ready")
        p_ready = sem("p_ready")
        num_done = sem("num_done")
        hsq = sem("hsq")
        hd2 = sem("hd2")
        hstd = sem("hstd")
        hrec = sem("hrec")
        hn_low = sem("hn_low")
        hn_high = sem("hn_high")
        ht_done = sem("ht_done")
        hout = sem("hout")
        mix_t = sem("mix_t")
        mix_hi = sem("mix_hi")
        mix_lo = sem("mix_lo")
        xq_sq = sem("xq_sq")
        xq_ss = sem("xq_ss")
        xq_std = sem("xq_std")
        xs_done = sem("xs_done")
        xmax = sem("xmax")
        xexp = sem("xexp")
        xrec = sem("xrec")
        xp_ready = sem("xp_ready")
        xp_second = sem("xp_second")
        xpt_done = sem("xpt_done")
        xpt_ready = sem("xpt_ready")
        xo_done = sem("xo_done")
        xo_hi = sem("xo_hi")
        xo_ready = sem("xo_ready")
        silu_done = sem("silu_done")
        gu_ready = sem("gu_ready")
        f_hi = sem("f_hi")
        f_ready = sem("f_ready")
        pos_in = sem("pos_in")
        lam_in = sem("lam_in")
        lam_s = sem("lam_s")
        lam_e = sem("lam_e")
        lam_d = sem("lam_d")
        lam_b = sem("lam_b")
        ang = sem("ang")
        trig = sem("trig")
        bsq = sem("bsq")
        bss = sem("bss")
        bqk_std = sem("bqk_std")
        bo_std = sem("bo_std")
        bn_ready = sem("bn_ready")
        bk_bc = sem("bk_bc")
        gx_ready = sem("gx_ready")
        rot_in = sem("rot_in")
        bqt = sem("bqt")
        bqr = sem("bqr")
        bkr = sem("bkr")
        bvt_done = sem("bvt_done")
        bv_ready = sem("bv_ready")
        bs_done = sem("bs_done")
        bmax = sem("bmax")
        bexp = sem("bexp")
        ba_ready = sem("ba_ready")
        bt_done = sem("bt_done")
        bat_ready = sem("bat_ready")
        bpv = sem("bpv")
        bosq = sem("bosq")
        bo_norm = sem("bo_norm")
        bo_turn = sem("bo_turn")
        bmix_hi = sem("bmix_hi")
        bmix_lo = sem("bmix_lo")
        ot_done = sem("ot_done")
        ot_out = sem("ot_out")
        o_store = [sem("o_store0"), sem("o_store1")]

        def wview(w, r0, nk, col):
            return w[r0:r0 + nk * P, :].rearrange("(k p) n -> p k n", p=P)[:, :, bass.ds(col, P)]

        kvw = [w_mem_kv[l] for l in range(2)]
        aw, bw = a_w_in[0], b_w_in[0]

        FULL = [0, 2, 3, 5]
        HALF = [(1, 0), (1, 64), (4, 0), (4, 64)]
        W_OFF = [0, 512, 896, 1152]

        V_PIECE = []
        for c in range(MC):
            cuts = sorted({c * P, (c + 1) * P} | {h * MHD for h in range(MH) if c * P < h * MHD < (c + 1) * P})
            V_PIECE.append([(a // MHD, a % MHD, a - c * P, b - a) for a, b in zip(cuts, cuts[1:])])
        V_DONE = [sum(len(p) for p in V_PIECE[:c + 1]) for c in range(MC)]

        DONE_MC = (MH - 1) * MHD // P

        S_BANK = [2, 3, 6, 7]
        SS_BANK = 7

        def flat(ap):
            return ap.rearrange("p a n -> p (a n)")

        def slots(ap, n):
            return [ap[:, i * n:(i + 1) * n] for i in range(ap.shape[1] // n)]

        t512 = [t[:, 0:SEQ] for t in tmp]
        X_SQ = [[t512[0], t512[2]], [t512[0], t512[1]]]
        X_P = [[slots(flat(QK[:, 6:10]), MEM), slots(flat(V[:])[:, 0:2048], MEM)],
               [slots(flat(PB[:])[:, 0:2048], MEM), slots(flat(QT[:]), MEM) + slots(flat(QR[:]), MEM)]]
        X_PT = [[t512[4:8], [QK[:, 10], QK[:, 11]] + slots(flat(V[:])[:, 2048:3072], SEQ)],
                [[ATB[:, k] for k in range(NT)], [QKP[:, i, j] for i in range(2) for j in range(2)]]]
        X_BANK = [0, 4]
        XSS_BANK = [2, 1]
        X_NM, X_RS, X_RQ = [nmA, nmX], [rsA, rsX], [rqA, rqB]

        block = ctx.enter_context(nc.Block())

        @block.sync
        def _(sp):
            sp.dma_start(m_st[:], mem[0].rearrange("(t p) n -> p t n", p=P)).then_inc(mem_in, 16)

            def load(n, slot, src, nk, first=False):
                if not first:
                    sp.wait_ge(w_split, n - (RAW - 1))
                sp.dma_start(w_raw[:, slot, 0:nk, :], src).then_inc(w_in[slot], 16)

            def run(base, count, w, r0, nk, col, step4=None):
                loops = count // 4 if step4 else 0
                if loops > 1:
                    with sp.Fori(0, loops) as i:
                        for s in range(4):
                            load(i * 4 + (base + s), (base + s) % RAW, wview(w, r0, nk, i * step4 + col(s)), nk)
                    done = loops * 4
                else:
                    done = 0
                for j in range(done, count):
                    load(base + j, (base + j) % RAW, wview(w, r0, nk, col(j)), nk)

            for n in range(RAW):
                load(n, n, wview(kvw[0], 0, 8, n * P), 8, first=True)
            sp.dma_start(x_st[:], x[0].rearrange("(t p) n -> p t n", p=P)).then_inc(x_in, 16)
            for n in range(4, 8):
                load(n, n % RAW, wview(kvw[1], 0, 8, (n - 4) * P), 8)
            run(T_GATE, 1, aw, 0, 8, lambda j: GATE_COL)
            run(T_QK, QKC, aw, 0, 8, lambda j: j * P, 4 * P)
            run(T_V, MC, aw, 0, 8, lambda j: 2 * MIX + j * P)
            run(T_XA, 2, aw, 0, 8, lambda j: XQ_COL_A + j * P)
            run(T_O, MC, aw, 0, 8, lambda j: 3 * MIX + j * P)
            for layer in range(2):
                if layer == 1:
                    for c in range(MC):
                        for j in range(3):
                            n = T_B + 3 * c + j
                            load(n, n % RAW, wview(bw, 0, 8, j * MIX + c * P), 8)
                    run(T_XB, 2, bw, 0, 8, lambda j: 3 * MIX + j * P)
                run(T_OUT[layer], KD, w_out[layer], 0, 8, lambda j: j * P, 4 * P)
                for s, (h0, nh) in enumerate(SEG):
                    base = seg_base(layer, s)
                    run(base, 2 * nh, w_gate_up[layer], 0, 8,
                        lambda j, h0=h0: (h0 + j // 2) * P + (j % 2) * FFN, 2 * P)
                    run(base + 2 * nh, KD, w_down[layer], h0 * P, nh, lambda j: j * P, 4 * P)
            ov = out[0].rearrange("(t p) n -> p t n", p=P)
            for k in range(KD):
                sp.wait_ge(ot_out, k + 1)
                sp.dma_start(ov[:, :, k * P:(k + 1) * P], o_st[:, k % 2]).then_inc(o_store[k % 2], 16)
            for j in range(2):
                sp.wait_ge(o_store[j], 16 * KD // 2)

        @block.gpsimd
        def _(pool):
            nc.gpsimd.memset(ones[:], 1.0).then_inc(set_done, 1)
            nc.gpsimd.memset(epsc[:], EPS).then_inc(set_done, 1)
            nc.gpsimd.memset(hpi[:], math.pi / 2).then_inc(set_done, 1)
            nc.gpsimd.memset(eps64[:], XH_DIM * EPS).then_inc(set_done, 1)

            for n in range(N_TILES):
                raw, sl, nk = n % RAW, n % SPLIT, tile_k(n)
                pool.wait_ge(w_in[raw], (n // RAW + 1) * 16)
                if n >= SPLIT:
                    pool.wait_ge(dense_done, n - SPLIT + 1)
                nc.gpsimd.tensor_scalar(w_hi[:, sl, 0:nk], w_raw[:, raw, 0:nk], 0.0, 1.0, ALU.add,
                                        ALU.mult).then_inc(w_round, 1)
                pool.wait_ge(w_round, n + 1)
                nc.gpsimd.tensor_tensor(w_lo[:, sl, 0:nk], w_raw[:, raw, 0:nk],
                                        w_hi[:, sl, 0:nk].bitcast(F32), ALU.subtract).then_inc(w_split, 1)

        @block.scalar
        def _(act):
            link_n = [0]

            def link(ins):
                link_n[0] += 1
                ins.then_inc(ach, 1)
                act.wait_ge(ach, link_n[0])

            act.dma_start(cn[:], con).then_inc(con_in, 16)
            act.dma_start(prm[0:N_PRM, :], prm_rows).then_inc(prm_in, 16)
            with nc.allow_non_contiguous_dma(reason="eight gate biases, once"):
                act.dma_start(gb[:], a_gate_b.rearrange("a (g h) -> h (a g)", g=2)).then_inc(lam_in, 16)
            act.dma_start(lamv[:], b_lambda).then_inc(lam_in, 16)

            def tr_out(g, dst):
                act.wait_ge(tr_done, g + 1)
                nc.scalar.activation(dst, PS[:, 4 + g % 4], ACT.Copy).then_inc(tr_free, 1)

            for g in range(5):
                if g < 4:
                    tr_out(g, flat(mT[:, 2 * g:2 * g + 2]))
                if g >= 1:
                    act.wait_ge(tr_free, g)
                    nc.scalar.activation(msq[:, 2 * g - 2:2 * g], mT[:, 2 * g - 2:2 * g], ACT.Square).then_inc(msq_done, 1)
            act.wait_ge(g_ready, 1)

            def mem_hi(l):
                for k in range(KD):
                    nc.scalar.activation(flat(Ah[:, 4 * l:4 * l + 4])[:, k * MEM:(k + 1) * MEM],
                                         mT[:, k], ACT.Copy,
                                         scale=gcol[:, R_MN + 8 * l + k:R_MN + 8 * l + k + 1]).then_inc(mhi, 1)

            mem_hi(0)
            act.wait_ge(mss_done, 1)
            act.wait_ge(set_done, 4)
            nc.scalar.activation(rm[:], PS[:, 3, 0:MEM], ACT.Sqrt, scale=1.0 / D, bias=epsc[:]).then_inc(mstd_done, 1)
            mem_hi(1)
            for g in range(4, 8):
                tr_out(g, xT[:, g - 4])

            xn = [0]

            def x_chunk(k, grow):
                n = xn[0]
                xn[0] += 1
                if n >= 2:
                    act.wait_ge(xsq_used, n - 1)
                nc.scalar.activation(tmp[6 + n % 2][:, 0:SEQ], xT[:, k], ACT.Square).then_inc(xsq, 1)
                nc.scalar.activation(Hh[:, k], xT[:, k], ACT.Copy,
                                     scale=gcol[:, grow + k:grow + k + 1]).then_inc(h_hi, 1)

            def x_std(i):
                act.wait_ge(ss_done, i + 1)
                nc.scalar.activation(rinv[:], PS[:, SS_BANK], ACT.Sqrt, scale=1.0 / D, bias=epsc[:]).then_inc(std_done, 1)

            for k in range(4):
                act.wait_ge(tr_free, 5 + k)
                x_chunk(k, R_N1)
            for g in range(8, 12):
                tr_out(g, xT[:, g - 4])
            for k in range(4, 8):
                act.wait_ge(tr_free, 5 + k)
                x_chunk(k, R_N1)

            act.wait_ge(lam_s, 1)
            nc.scalar.activation(lame[0:1, 2:4], lame[0:1, 0:2], ACT.Exp).then_inc(lam_e, 1)
            act.wait_ge(dense_free, 2)
            nc.scalar.activation(kvs[:], flat(kv[:, 0, 0:2]), ACT.Square).then_inc(ksq, 1)
            x_std(0)

            for l in range(2):
                if l == 1:
                    act.wait_ge(dense_free, 6)
                    act.wait_ge(kn_ready, 1)
                    nc.scalar.activation(kvs[:], flat(kv[:, 1, 0:2]), ACT.Square).then_inc(ksq, 1)
                act.wait_ge(kss, l + 1)
                nc.scalar.activation(kvs[:], PS[:, 4 + l], ACT.Sqrt, scale=1.0 / XH_DIM, bias=epsc[:]).then_inc(kstd, 1)
                act.wait_ge(vtr, l + 1)
                nc.scalar.activation(flat(xv[:, l]), PS[:, 6], ACT.Copy).then_inc(vtr_out, 1)

            act.wait_ge(gsel_done, 1)
            link(nc.scalar.activation(tmp[0][0:MH, 0:SEQ], PS[0:MH, 3], ACT.Identity, bias=gb[:, 1:2]))
            link(nc.scalar.activation(tmp[1][0:MH, 0:SEQ], tmp[0][0:MH, 0:SEQ], ACT.Abs))
            link(nc.scalar.activation(tmp[1][0:MH, 0:SEQ], tmp[1][0:MH, 0:SEQ], ACT.Exp, scale=-1.0))
            nc.scalar.activation(tmp[1][0:MH, 0:SEQ], tmp[1][0:MH, 0:SEQ], ACT.Ln, bias=1.0).then_inc(lnf_done, 1)
            with act.Fori(0, QKC) as c:
                act.wait_ge(conv_done, c + 1)
                nc.scalar.activation(QK[:, bass.ds(c, 1)], QK[:, bass.ds(c, 1)], ACT.Silu).then_inc(qk_ready, 1)
            act.wait_ge(at_ready, 1)
            nc.scalar.activation(emT[:], amT[:, 1], ACT.Exp, scale=-1.0).then_inc(em_done, 1)
            for c in range(MC):
                act.wait_ge(vT_done, c + 1)
                for h, at, frm, n in V_PIECE[c]:
                    nc.scalar.activation(V[:, :, h * VW + at:h * VW + at + n],
                                         PS[:, 4 + c % 2].rearrange("p (t n) -> p t n", t=NT)[:, :, frm:frm + n],
                                         ACT.Copy).then_inc(v_ready, 1)

            def head_weights(h):
                act.wait_ge(dg_ready, h + 1)
                if h >= 1:
                    act.wait_ge(num_done, 2 * h)
                for s in range(NT):
                    a = amT[:, 0, s, h:h + 1]
                    nc.scalar.activation(WT[:, W_OFF[s]:W_OFF[s] + P], tmp[1][:, s * P:(s + 1) * P], ACT.Exp,
                                         scale=-1.0, bias=a).then_inc(wt_ready, 1)
                    if s < NT - 1:
                        nc.scalar.activation(WT[:, W_OFF[s] + P:W_OFF[s] + SEQ - s * P], PS[:, 4, (s + 1) * P:SEQ],
                                             ACT.Exp, scale=-1.0, bias=a).then_inc(wt_ready, 1)

            def head_num(h):
                for t in range(NT):
                    act.wait_ge(num_done, 2 * h + t // 2 + 1)
                    if h >= 1:
                        act.wait_ge(hd2, h)
                    nc.scalar.activation(t512[5 + t // 2][:, (t % 2) * MHD:(t % 2 + 1) * MHD], PS[:, 4 + t // 2, (t % 2) * VW:(t % 2) * VW + MHD], ACT.Square,
                                         accum_out=rcA[:, 4, t:t + 1]).then_inc(hsq, 1)

            def head_std(h):
                act.wait_ge(hd2, h + 1)
                nc.scalar.activation(rcA[:, 3], rcA[:, 2], ACT.Sqrt).then_inc(hstd, 1)

            def head_high(h):
                act.wait_ge(hrec, h + 1)
                for t in range(2, NT):
                    nc.scalar.activation(t512[4][:, (t - 2) * MHD:(t - 1) * MHD], PS[:, 5, (t - 2) * VW:(t - 2) * VW + MHD],
                                         ACT.Copy, scale=rcA[:, 3, t:t + 1]).then_inc(hn_high, 1)

            def cross_sq(l, c):
                act.wait_ge(dense_free, (T_XA, T_XB)[l] + c + 1)
                nc.scalar.activation(X_SQ[l][c], (xqA, xqB)[l][:, c], ACT.Square).then_inc(xq_sq, 1)

            def cross_std(l):
                act.wait_ge(xq_ss, l + 1)
                nc.scalar.activation(X_RQ[l][:], PS[:, XSS_BANK[l], 0:16].rearrange("p (a t h) -> p a t h", a=2, t=NT),
                                     ACT.Sqrt, bias=eps64[:]).then_inc(xq_std, 1)

            def out_gate(c0, c1):
                act.wait_ge(dense_free, T_O + c1)
                nc.scalar.activation(SO[:, c0:c1], SO[:, c0:c1], ACT.Sigmoid).then_inc(o_gate, 1)

            def mixer_hi(c0, c1):
                for c in range(c0, c1):
                    act.wait_ge(mix_t, c + 1)
                    nc.scalar.activation(Ah[:, c], QK[:, c], ACT.Copy).then_inc(mix_hi, 1)

            for h in range(MH):
                head_weights(h)
                if h == MH - 1:
                    out_gate(0, DONE_MC)
                    mixer_hi(0, DONE_MC)
                head_num(h)
                if h == MH - 2:
                    cross_sq(0, 0)
                    cross_sq(0, 1)
                if h == MH - 1:
                    cross_std(0)
                head_std(h)
                head_high(h)

            def cross_exp(l, c):
                i = 2 * l + c
                for hd in range(2):
                    if hd == 1 and c == 1:
                        cross_p(l, 0)
                    for t in range(NT):
                        act.wait_ge(xmax, 4 * i + 2 * hd + t // 2 + 1)
                        j = 4 * hd + t
                        nc.scalar.activation(X_P[l][c][j], PS[:, X_BANK[c] + 2 * hd + t // 2, (t % 2) * MEM:(t % 2 + 1) * MEM],
                                             ACT.Exp, scale=X_RQ[l][:, c, t, hd:hd + 1],
                                             bias=X_NM[l][:, 8 * c + j:8 * c + j + 1],
                                             accum_out=X_RS[l][:, 8 * c + j:8 * c + j + 1]).then_inc(xexp, 1)

            def cross_p(l, c):
                act.wait_ge(xrec, 2 * (2 * l + c) + 2)
                for t in range(NT):
                    p = X_P[l][c][4 + t]
                    r = 8 * c + 4 + t
                    nc.scalar.activation(p, p, ACT.Copy, scale=X_RS[l][:, r:r + 1]).then_inc(xp_second, 1)

            def cross_pt(l, c):
                i = 2 * l + c
                for j in range(4):
                    act.wait_ge(xpt_done, 4 * i + j + 1)
                    nc.scalar.activation(X_PT[l][c][j], PS[:, X_BANK[c] + j], ACT.Copy).then_inc(xpt_ready, 1)

            def cross_hi(l, c):
                act.wait_ge(xo_done, 2 * l + c + 1)
                nc.scalar.activation(Ah[:, MC + c], PS[:, X_BANK[c]], ACT.Copy).then_inc(xo_hi, 1)

            cross_exp(0, 0)
            cross_exp(0, 1)
            cross_p(0, 1)
            cross_pt(0, 0)
            cross_pt(0, 1)
            cross_hi(0, 0)
            out_gate(DONE_MC, MC)
            mixer_hi(DONE_MC, MC)
            cross_hi(0, 1)

            def x_phase(grow, base):
                for k in range(KD):
                    act.wait_ge(dense_free, base + k + 1)
                    x_chunk(k, grow)

            def ffn(l):
                n0 = l * HC
                for s, (h0, nh) in enumerate(SEG):
                    base = seg_base(l, s)
                    with act.Fori(0, nh) as i:
                        act.wait_ge(dense_free, i * 2 + (base + 1))
                        nc.scalar.activation(tmp[0][:, 0:SEQ], tmp[1][:, 0:SEQ], ACT.Silu).then_inc(silu_done, 1)
                        act.wait_ge(gu_ready, i + (n0 + h0 + 1))
                        nc.scalar.activation(Ah[:, bass.ds(i, 1)], tmp[3][:, 0:SEQ].rearrange("p (a n) -> p a n", a=1),
                                             ACT.Copy).then_inc(f_hi, 1)

            x_phase(R_N2, T_OUT[0])
            x_std(1)
            ffn(0)
            act.dma_start(posi[:], positions.broadcast_to([P, SEQ])).then_inc(pos_in, 16)
            x_phase(R_N1 + 8, seg_base(0, 2) + 2 * SEG[2][1])
            x_std(2)
            def b_sq(c):
                act.wait_ge(dense_free, T_B + 3 * c + 2)
                if c >= 1:
                    act.wait_ge(bqr, c)
                for r in range(0, P, 32):
                    src = r + 32 if r % 64 == 0 else r - 32
                    act.dma_start(QKR[r:r + 32], QKP[src:src + 32, c % 2]).then_inc(rot_in, 16)
                if c >= 1:
                    act.wait_ge(bss, c)
                nc.scalar.activation(QS[:], QKP[:, c % 2], ACT.Square).then_inc(bsq, 1)

            def b_std(c):
                act.wait_ge(bss, c + 1)
                if c >= 1:
                    act.wait_ge(bkr, c)
                nc.scalar.activation(rqk[:], PS[:, 6, 0:16].rearrange("p (a t h) -> p a t h", a=2, t=NT), ACT.Sqrt,
                                     bias=eps64[:]).then_inc(bqk_std, 1)

            def b_ostd(c):
                act.wait_ge(bosq, NT * (c + 1))
                if c >= 1:
                    act.wait_ge(bo_norm, c)
                nc.scalar.activation(ro_all[:], roB[:], ACT.Sqrt, scale=1.0 / P, bias=epsc[:]).then_inc(bo_std, 1)

            def b_v(c):
                act.wait_ge(bvt_done, c + 1)
                if c >= 2:
                    act.wait_ge(bpv, c - 1)
                nc.scalar.activation(VB[:, c % 2], PS[:, 2].rearrange("p (t n) -> p t n", t=NT), ACT.Copy).then_inc(bv_ready, 1)

            def b_exp(c, u):
                t = NT - 1 - u
                n = 4 * c + u
                act.wait_ge(bmax, n + 1)
                if c >= 1:
                    act.wait_ge(bt_done, 4 * (c - 1) + u + 1)
                for hd in range(2):
                    j = (8 * c + 2 * u + hd) % 64
                    nc.scalar.activation(PB[:, hd, W_OFF[u]:W_OFF[u] + (t + 1) * P], PS[:, 6 - 2 * (u % 2) + hd, 0:(t + 1) * P],
                                         ACT.Exp, scale=rqk_all[:, 0, t, hd:hd + 1],
                                         bias=nmB[:, j:j + 1], accum_out=rsB[:, j:j + 1]).then_inc(bexp, 1)

            def b_at(c, u):
                t = NT - 1 - u
                act.wait_ge(bt_done, 4 * c + u + 1)
                if c >= 1 and u == 0:
                    act.wait_ge(bpv, c)
                nc.scalar.activation(ATB[:, 0:t + 1, t * P:(t + 1) * P],
                                     PS[:, 2 + u % 2, 0:(t + 1) * P].rearrange("p (a n) -> p a n", n=P),
                                     ACT.Copy).then_inc(bat_ready, 1)

            def b_osq(c):
                act.wait_ge(bpv, c + 1)
                if c >= 1:
                    act.wait_ge(bosq, NT * c)
                    act.wait_ge(bo_std, c)
                for t in range(NT):
                    nc.scalar.activation(t512[6][:, t * P:(t + 1) * P], PS[:, 4, t * P:(t + 1) * P], ACT.Square,
                                         accum_out=roB[:, t:t + 1]).then_inc(bosq, 1)

            def b_hi(c):
                act.wait_ge(bo_turn, c + 1)
                nc.scalar.activation(Ah[:, c], PS[:, 5], ACT.Copy, scale=gx[:, 2:3]).then_inc(bmix_hi, 1)

            b_sq(0)
            act.wait_ge(ang, 1)
            nc.scalar.activation(sinT[:], QT[:, 0], ACT.Sin).then_inc(trig, 1)
            link(nc.scalar.activation(cosT[:], QT[:, 0], ACT.Abs))
            nc.scalar.activation(cosT[:], cosT[:], ACT.Sin, scale=-1.0, bias=hpi[:]).then_inc(trig, 1)

            for c in range(MC):
                b_std(c)
                if c >= 1:
                    b_osq(c - 1)
                    b_ostd(c - 1)
                    b_hi(c - 1)
                if c + 1 == MC:
                    cross_sq(1, 0)
                b_exp(c, 0)
                b_v(c)
                b_exp(c, 1)
                if c + 1 < MC:
                    b_sq(c + 1)
                else:
                    cross_sq(1, 1)
                b_exp(c, 2)
                b_exp(c, 3)
                for u in range(NT):
                    b_at(c, u)
            cross_std(1)
            b_osq(MC - 1)
            b_ostd(MC - 1)
            b_hi(MC - 1)
            cross_exp(1, 0)
            cross_exp(1, 1)
            cross_p(1, 1)
            cross_pt(1, 0)
            cross_pt(1, 1)
            cross_hi(1, 0)
            cross_hi(1, 1)
            x_phase(R_N2 + 8, T_OUT[1])
            x_std(3)
            ffn(1)
            for k in range(KD):
                act.wait_ge(ot_done, k + 1)
                if k >= 2:
                    act.wait_ge(o_store[k % 2], 16 * (k // 2))
                nc.scalar.activation(o_st[:, k % 2].rearrange("p t n -> p (t n)"), PS[:, 2 + k % 2], ACT.Copy).then_inc(ot_out, 1)

        @block.vector
        def _(dve):
            link_n = [0]

            def link(ins):
                link_n[0] += 1
                ins.then_inc(vch, 1)
                dve.wait_ge(vch, link_n[0])

            def col(r):
                return gcol[:, r:r + 1]

            nc.vector.memset(tmp[2][:, 0:CONV - 1], 0.0)
            nc.vector.memset(tmp[3][:, 0:CONV - 1], 0.0)
            dve.wait_ge(prm_t, 1)
            nc.vector.tensor_copy(gcol[:], PS[:, 2, 0:N_PRM]).then_inc(g_ready, 1)
            dve.wait_ge(g_ready, 1)
            link(nc.vector.tensor_tensor(gx[:, 0:2], gcol[:, R_XQ:R_XQ + 2], gcol[:, R_XK:R_XK + 2], ALU.mult))
            nc.vector.tensor_scalar(gx[:, 2:3], col(R_SL), 1.0 - LAMBDA_INIT, None, ALU.mult)
            link(nc.vector.tensor_scalar(gx[:, 4:5], col(R_BK), 8.0, None, ALU.mult))
            nc.vector.tensor_copy(gx[:, 3:4], col(R_BQ)).then_inc(gx_ready, 1)

            def mem_lo(l):
                for k in range(KD):
                    dve.wait_ge(mhi, 8 * l + k + 1)
                    lo, hi = (flat(A[:, 4 * l:4 * l + 4])[:, k * MEM:(k + 1) * MEM] for A in (Al, Ah))
                    nc.vector.scalar_tensor_tensor(lo, mT[:, k], col(R_MN + 8 * l + k), hi.bitcast(F32),
                                                   ALU.mult, ALU.subtract).then_inc(mg_ready, 1)

            mem_lo(0)
            dve.wait_ge(mstd_done, 1)
            link(nc.vector.reciprocal(rm[:], rm[:]))

            def mem_out(n):
                dve.wait_ge(dense_done, n + 1)
                nc.vector.tensor_tensor(kv[:, n // 4, n % 4], PS[:, n % 2, 0:MEM], rm[:], ALU.mult).then_inc(dense_free, 1)

            xn = [0]

            def x_chunk(k, grow):
                n = xn[0]
                xn[0] += 1
                sq = tmp[6 + n % 2][:, 0:SEQ]
                dve.wait_ge(xsq, n + 1)
                if k == 0:
                    nc.vector.tensor_copy(acc[:], sq).then_inc(xsq_used, 1)
                else:
                    dve.wait_ge(xsq_used, n)
                    nc.vector.tensor_tensor(acc[:], acc[:], sq, ALU.add).then_inc(xsq_used, 1)
                dve.wait_ge(h_hi, n + 1)
                nc.vector.scalar_tensor_tensor(Hl[:, k], xT[:, k], col(grow + k), Hh[:, k].bitcast(F32),
                                               ALU.mult, ALU.subtract).then_inc(h_ready, 1)

            def x_rinv(i):
                dve.wait_ge(std_done, i + 1)
                link(nc.vector.reciprocal(rinv[:], rinv[:]))

            mem_out(0)
            mem_lo(1)
            mem_out(1)
            for n in range(2, 6):
                x_chunk(n - 2, R_N1)
                mem_out(n)
            dve.wait_ge(lam_in, 32)
            link(nc.vector.tensor_tensor(lamw[:], lamv[0:1, 0:4:2], lamv[0:1, 1:4:2], ALU.mult))
            nc.vector.tensor_reduce(lame[0:1, 0:2], lamw[:], AX.X, ALU.add).then_inc(lam_s, 1)
            for k in range(4, 8):
                x_chunk(k, R_N1)
            mem_out(6)
            mem_out(7)
            dve.wait_ge(lam_e, 1)
            nc.vector.scalar_tensor_tensor(lame[0:1, 0:1], lame[0:1, 2:3], LAMBDA_INIT, lame[0:1, 3:4],
                                           ALU.add, ALU.subtract).then_inc(lam_d, 1)

            def k_norm(l):
                dve.wait_ge(kstd, l + 1)
                link(nc.vector.reciprocal(kvs[:], kvs[:]))
                nc.vector.scalar_tensor_tensor(flat(xk[:, l]), flat(kv[:, l, 0:2]), gx[:, l:l + 1], kvs[:], ALU.mult,
                                               ALU.mult).then_inc(kn_ready, 1)

            x_rinv(0)

            def scaled_out(n, dst):
                dve.wait_ge(dense_done, n + 1)
                nc.vector.tensor_tensor(dst, PS[0:dst.shape[0], n % 2], rinv[0:dst.shape[0], :], ALU.mult).then_inc(dense_free, 1)

            scaled_out(T_GATE, tmp[4][0:8, 0:SEQ])
            k_norm(0)

            def conv(i, j):
                raw, n0 = tmp[2 + j], T_QK + j
                dve.wait_ge(dense_done, i * 2 + (n0 + 1))
                nc.vector.tensor_tensor(raw[:, CONV - 1:CONV - 1 + SEQ], PS[:, n0 % 2], rinv[:], ALU.mult).then_inc(dense_free, 1)
                dve.wait_ge(dense_free, i * 2 + (n0 + 1))
                c = i * 2 + j

                def w(r):
                    return gcol[:, bass.ds(c + r, 1)]
                y = QK[:, bass.ds(c, 1)].rearrange("p a n -> p (a n)")
                nc.vector.tensor_scalar(y, raw[:, 3:3 + SEQ], w(R_CW + 3 * QKC), w(R_CB), ALU.mult, ALU.add).then_inc(conv_step, 1)
                for tap in (2, 1, 0):
                    dve.wait_ge(conv_step, i * 6 + (3 * j + 3 - tap))
                    nc.vector.scalar_tensor_tensor(y, raw[:, tap:tap + SEQ], w(R_CW + tap * QKC), y, ALU.mult,
                                                   ALU.add).then_inc(conv_step if tap else conv_done, 1)

            conv(0, 0)
            dve.wait_ge(lam_b, 1)
            nc.vector.tensor_copy(grot[:], PS[:, 2, 2:4])
            nc.vector.tensor_copy(lam[:], PS[:, 2, 0:1]).then_inc(lam_d, 1)
            conv(0, 1)
            k_norm(1)
            F, L = tmp[0][0:MH, 0:SEQ], tmp[1][0:MH, 0:SEQ]
            b_row, a_row = tmp[5][0:MH, 0:SEQ], tmp[6][0:MH, 0:SEQ]
            dve.wait_ge(lnf_done, 1)
            link(nc.vector.scalar_tensor_tensor(L, F, 0.0, L, ALU.min, ALU.subtract))
            link(nc.vector.memset(tmp[7][0:MH, 0:SEQ], 1.0))
            link(nc.vector.tensor_tensor_scan(b_row, tmp[7][0:MH, 0:SEQ], L, 0.0, ALU.mult, ALU.add))
            link(nc.vector.scalar_tensor_tensor(a_row, PS[0:MH, 2], gb[:, 0:1], b_row, ALU.add, ALU.subtract))
            link(nc.vector.tensor_tensor_scan(Mrow[:], a_row, a_row, 0.0, ALU.max, ALU.max))
            nc.vector.tensor_tensor(tmp[0][0:MH, 0:SEQ], Mrow[:], b_row, ALU.add).then_inc(a_ready, 1)
            with dve.Fori(1, QKC // 2) as i:
                conv(i, 0)
                conv(i, 1)
            dve.wait_ge(at_done, 1)
            nc.vector.tensor_copy(amT[:], PS[:, 3, 0:2 * NT * MH].rearrange("p (a t h) -> p a t h", a=2, h=MH)).then_inc(at_ready, 1)
            nc.vector.memset(V[:, :, MHD:MH * VW:VW], 1.0).then_inc(v_ones, 1)
            for c in range(MC):
                if c >= 2:
                    dve.wait_ge(vT_done, c - 1)
                scaled_out(T_V + c, tmp[4 + c % 2][:, 0:SEQ])

            def head_diag(h):
                dve.wait_ge(mbc_done, h + 1)
                if h >= 1:
                    dve.wait_ge(wt_ready, 7 * h)
                nc.vector.tensor_tensor(tmp[1][:, 0:SEQ].rearrange("p (t n) -> p t n", t=NT),
                                        PS[:, 4].rearrange("p (t n) -> p t n", t=NT),
                                        big_mask.rearrange("p (a n) -> p a n", a=1).broadcast_to([P, NT, P]),
                                        ALU.add).then_inc(dg_ready, 1)

            def head_p(h):
                for s in range(NT):
                    dve.wait_ge(s_done, NT * h + s + 1)
                    dve.wait_ge(wt_ready, 7 * h + min(2 * s + 2, 7))
                    w = WT[:, W_OFF[s]:W_OFF[s] + SEQ - s * P]
                    nc.vector.scalar_tensor_tensor(w, PS[:, S_BANK[s], s * P:SEQ], MHD ** -0.5, w, ALU.mult,
                                                   ALU.mult).then_inc(p_ready, 1)

            def head_cols(h):
                dve.wait_ge(hsq, NT * (h + 1))
                dve.wait_ge(em_done, 1)
                if h >= 1:
                    dve.wait_ge(hn_high, 2 * h)
                d, d2, arg, r, ss = (rcA[:, i] for i in range(5))
                den = PS[:, 4:6, MHD:2 * VW:VW]
                half = d.rearrange("p (a b) -> p a b", a=2)
                link(nc.vector.scalar_tensor_tensor(half, den, -1.0, emT[:, :, h].rearrange("p (a b) -> p a b", a=2),
                                                    ALU.mult, ALU.max))
                link(nc.vector.tensor_tensor(half, half, den, ALU.max))
                link(nc.vector.tensor_scalar(d, d, 2.0 ** 57, EPS ** 0.5, ALU.min, ALU.mult))
                link(nc.vector.tensor_tensor(d2, d, d, ALU.mult))
                nc.vector.scalar_tensor_tensor(arg, ss, 1.0 / MHD, d2, ALU.mult, ALU.add).then_inc(hd2, 1)
                dve.wait_ge(hstd, h + 1)
                nc.vector.reciprocal(r, r).then_inc(hrec, 1)
                dve.wait_ge(hrec, h + 1)
                for t in range(2):
                    nc.vector.tensor_scalar(t512[3][:, t * MHD:(t + 1) * MHD], PS[:, 4, t * VW:t * VW + MHD], r[:, t:t + 1], None,
                                            ALU.mult).then_inc(hn_low, 1)

            def head_out(h):
                f, (c, r) = FULL[h], HALF[h]
                dve.wait_ge(ht_done, h + 1)
                nc.vector.tensor_scalar(QK[:, f], PS[:, 6], col(R_HN + f), None, ALU.mult).then_inc(hout, 1)
                nc.vector.tensor_scalar(QK[r:r + 64, c], PS[r:r + 64, 7], gcol[r:r + 64, R_HN + c:R_HN + c + 1], None,
                                        ALU.mult).then_inc(hout, 1)

            fill = [(T_XA, xqA[:, 0]), (T_XA + 1, xqA[:, 1])] + [(T_O + c, SO[:, c]) for c in range(MC)]
            def cross_rq(l):
                dve.wait_ge(xq_std, l + 1)
                link(nc.vector.reciprocal(X_RQ[l][:], X_RQ[l][:]))

            def mixer_out(c0, c1):
                dve.wait_ge(o_gate, 1 if c1 < MC else 2)
                dve.wait_ge(hout, 2 * (MH if c1 == MC else MH - 1))
                for c in range(c0, c1):
                    nc.vector.tensor_tensor(QK[:, c], QK[:, c], SO[:, c], ALU.mult).then_inc(mix_t, 1)

            def mixer_lo(c0, c1):
                for c in range(c0, c1):
                    dve.wait_ge(mix_hi, c + 1)
                    nc.vector.tensor_tensor(Al[:, c], QK[:, c], Ah[:, c].bitcast(F32), ALU.subtract).then_inc(mix_lo, 1)

            for h in range(MH):
                head_diag(h)
                head_p(h)
                if h == MH - 1:
                    mixer_out(0, DONE_MC)
                scaled_out(*fill[2 * h])
                if h == MH - 1:
                    mixer_lo(0, DONE_MC)
                head_cols(h)
                if h == MH - 1:
                    scaled_out(*fill[2 * h + 1])
                    cross_rq(0)
                head_out(h)
                if h < MH - 1:
                    scaled_out(*fill[2 * h + 1])

            def cross_max(l, c, after=None):
                i = 2 * l + c
                nm = X_NM[l]
                for b in range(4):
                    hd, t0 = b // 2, 2 * (b % 2)
                    o = nm[:, 8 * c + 2 * b:8 * c + 2 * b + 2]
                    dve.wait_ge(xs_done, 4 * i + b + 1)
                    link(nc.vector.tensor_reduce(o, PS[:, X_BANK[c] + b].rearrange("p (a n) -> p a n", a=2), AX.X,
                                                 ALU.max, negate=True))
                    nc.vector.tensor_tensor(o, o, X_RQ[l][:, c, t0:t0 + 2, hd], ALU.mult).then_inc(xmax, 1)
                    if after:
                        after(b)

            def cross_p(l, c, hd):
                i = 2 * l + c
                dve.wait_ge(xexp, 8 * i + 4 * hd + 4)
                r = X_RS[l][:, 8 * c + 4 * hd:8 * c + 4 * hd + 4]
                nc.vector.reciprocal(r, r).then_inc(xrec, 1)
                if hd == 0:
                    dve.wait_ge(xrec, 2 * i + 1)
                    for t in range(NT):
                        p = X_P[l][c][t]
                        nc.vector.tensor_scalar(p, p, r[:, t:t + 1], None, ALU.mult).then_inc(xp_ready, 1)

            def cross_lo(l, c):
                dve.wait_ge(xo_hi, 2 * l + c + 1)
                nc.vector.tensor_tensor(Al[:, MC + c], PS[:, X_BANK[c]], Ah[:, MC + c].bitcast(F32),
                                        ALU.subtract).then_inc(xo_ready, 1)

            cross_max(0, 0)
            cross_p(0, 0, 0)
            cross_max(0, 1, after=lambda b: cross_p(0, 0, 1) if b == 1 else None)
            cross_p(0, 1, 0)
            cross_p(0, 1, 1)
            cross_lo(0, 0)
            mixer_out(DONE_MC, MC)
            mixer_lo(DONE_MC, MC)
            cross_lo(0, 1)

            def x_add(n, k):
                dve.wait_ge(dense_done, n + 1)
                nc.vector.tensor_tensor(xT[:, k], xT[:, k], PS[:, n % 2], ALU.add).then_inc(dense_free, 1)

            def x_phase(base, grow):
                for k in range(KD):
                    x_add(base + k, k)
                    x_chunk(k, grow)

            def ffn(l, grow):
                n0 = l * HC
                for s, (h0, nh) in enumerate(SEG):
                    base = seg_base(l, s)
                    f0 = n0 + h0
                    with dve.Fori(0, nh) as i:
                        dve.wait_ge(dense_done, i * 2 + (base + 1))
                        nc.vector.tensor_tensor(tmp[1][:, 0:SEQ], PS[:, base % 2], rinv[:], ALU.mult).then_inc(dense_free, 1)
                        dve.wait_ge(dense_done, i * 2 + (base + 2))
                        nc.vector.tensor_tensor(tmp[2][:, 0:SEQ], PS[:, (base + 1) % 2], rinv[:], ALU.mult).then_inc(dense_free, 1)
                        dve.wait_ge(dense_free, i * 2 + (base + 2))
                        dve.wait_ge(silu_done, i + (f0 + 1))
                        nc.vector.tensor_tensor(tmp[3][:, 0:SEQ], tmp[0][:, 0:SEQ], tmp[2][:, 0:SEQ], ALU.mult).then_inc(gu_ready, 1)
                        dve.wait_ge(f_hi, i + (f0 + 1))
                        one = tmp[3][:, 0:SEQ].rearrange("p (a n) -> p a n", a=1)
                        nc.vector.tensor_tensor(Al[:, bass.ds(i, 1)], one, Ah[:, bass.ds(i, 1)].bitcast(F32),
                                                ALU.subtract).then_inc(f_ready, 1)
                    down = base + 2 * nh
                    if s + 1 < len(SEG):
                        with dve.Fori(0, KD // 2) as i:
                            for j in range(2):
                                dve.wait_ge(dense_done, i * 2 + (down + j + 1))
                                xk_ = xT[:, bass.ds(i * 2 + j, 1)]
                                b = (down + j) % 2
                                nc.vector.tensor_tensor(xk_, xk_, PS[:, b:b + 1], ALU.add).then_inc(dense_free, 1)
                    elif grow is not None:
                        x_phase(down, grow)
                    else:
                        for k in range(KD):
                            x_add(down + k, k)

            x_phase(T_OUT[0], R_N2)
            x_rinv(1)
            ffn(0, R_N1 + 8)
            x_rinv(2)

            scaled_out(T_B, QKP[:, 0, 0])
            scaled_out(T_B + 1, QKP[:, 0, 1])
            C1 = 6.28125
            C2 = float(np.float32(int((2 * math.pi - C1) * 2 ** 22) / 2 ** 22))
            C3 = 2 * math.pi - C1 - C2
            MAGIC = 1.5 * 2 ** 23
            pf, an, kk = QR[:, 0], QR[:, 1], QT[:, 1]
            dve.wait_ge(pos_in, 16)
            link(nc.vector.tensor_copy(pf, posi[:]))
            link(nc.vector.tensor_scalar(an, pf, cn[:, C_INV:C_INV + 1], None, ALU.mult))
            link(nc.vector.tensor_scalar(kk, an, 1.0 / (2 * math.pi), MAGIC, ALU.mult, ALU.add))
            link(nc.vector.tensor_scalar(kk, kk, MAGIC, None, ALU.subtract))
            for part in (C1, C2, C3):
                link(nc.vector.scalar_tensor_tensor(an, kk, -part, an, ALU.mult, ALU.add))
            nc.vector.tensor_scalar(QT[:, 0], an, 3.1415925, -3.1415925, ALU.min, ALU.max).then_inc(ang, 1)
            scaled_out(T_B + 2, tmp[2][:, 0:SEQ])

            def b_rope(c):
                q2 = QKP[:, c % 2]
                for i in range(2):
                    nc.vector.scalar_tensor_tensor(QT[:, i], q2[:, i], gx[:, 3 + i:4 + i], cosT[:], ALU.mult, ALU.mult).then_inc(bqt, 1)
                dve.wait_ge(rot_in, 64 * (c + 1))
                for i in range(2):
                    nc.vector.scalar_tensor_tensor(QR[:, i], QKR[:, i], grot[:, i:i + 1], sinT[:], ALU.mult, ALU.mult).then_inc(bqt, 1)
                dve.wait_ge(bqt, 4 * c + 4)
                nc.vector.tensor_tensor(QR[:], QR[:], QT[:], ALU.add).then_inc(bqr, 1)

            def b_norm(c):
                dve.wait_ge(bqk_std, c + 1)
                link(nc.vector.reciprocal(rqk_all[:], rqk[:]))
                nc.vector.tensor_copy(t512[4].rearrange("p (t h n) -> p (t h) n", t=NT, h=2),
                                      rqk_all[:, 1].rearrange("p t (h a) -> p (t h) a", a=1).broadcast_to([P, 2 * NT, 64])).then_inc(bn_ready, 1)

            def b_onorm(c):
                dve.wait_ge(bo_std, c + 1)
                link(nc.vector.reciprocal(ro_all[:], ro_all[:]))
                nc.vector.tensor_tensor(t512[5].rearrange("p (t n) -> p t n", t=NT), PS[:, 4].rearrange("p (t n) -> p t n", t=NT),
                                        ro_all[:].rearrange("p (t a) -> p t a", a=1).broadcast_to([P, NT, P]),
                                        ALU.mult).then_inc(bo_norm, 1)

            def b_knorm(c):
                dve.wait_ge(bk_bc, c + 1)
                dve.wait_ge(bqr, c + 1)
                nc.vector.tensor_tensor(QR[:, 1], QR[:, 1], PS[:, 7], ALU.mult).then_inc(bkr, 1)

            def b_max(c, u):
                t, b = NT - 1 - u, 6 - 2 * (u % 2)
                n = 4 * c + u
                dve.wait_ge(bs_done, n + 1)
                dg = PS[:, b:b + 2, t * P:(t + 1) * P]
                link(nc.vector.tensor_tensor(dg, dg, neg_mask.rearrange("p (a n) -> p a n", a=1).broadcast_to([P, 2, P]), ALU.add))
                j = (8 * c + 2 * u) % 64
                link(nc.vector.tensor_reduce(nmB[:, j:j + 2], PS[:, b:b + 2, 0:(t + 1) * P], AX.X, ALU.max, negate=True))
                nc.vector.tensor_tensor(nmB[:, j:j + 2], nmB[:, j:j + 2], rqk_all[:, 0, t], ALU.mult).then_inc(bmax, 1)

            def b_prob(c, u):
                t = NT - 1 - u
                n = 4 * c + u
                j = (8 * c + 2 * u) % 64
                w = slice(W_OFF[u], W_OFF[u] + (t + 1) * P)
                dve.wait_ge(bexp, 2 * n + 2)
                link(nc.vector.reciprocal(rsB[:, j:j + 2], rsB[:, j:j + 2]))
                link(nc.vector.tensor_scalar(PB[:, 1, w], PB[:, 1, w], rsB[:, j + 1:j + 2], lam[:], ALU.mult, ALU.mult))
                nc.vector.scalar_tensor_tensor(PB[:, 0, w], PB[:, 0, w], rsB[:, j:j + 1], PB[:, 1, w], ALU.mult,
                                               ALU.subtract).then_inc(ba_ready, 1)

            def b_lo(c):
                dve.wait_ge(bmix_hi, c + 1)
                nc.vector.scalar_tensor_tensor(Al[:, c], PS[:, 5], gx[:, 2:3], Ah[:, c].bitcast(F32), ALU.mult,
                                               ALU.subtract).then_inc(bmix_lo, 1)

            for c in range(MC):
                n = T_B + 3 * (c + 1)
                last = c + 1 == MC
                if c == 0:
                    dve.wait_ge(trig, 2)
                b_rope(c)
                b_norm(c)
                if c >= 1:
                    b_onorm(c - 1)
                scaled_out(n, xqB[:, 0] if last else QKP[:, (c + 1) % 2, 0])
                b_knorm(c)
                if c >= 1:
                    b_lo(c - 1)
                b_max(c, 0)
                scaled_out(n + 1, xqB[:, 1] if last else QKP[:, (c + 1) % 2, 1])
                b_max(c, 1)
                b_prob(c, 0)
                b_max(c, 2)
                b_prob(c, 1)
                b_max(c, 3)
                b_prob(c, 2)
                b_prob(c, 3)
                if not last:
                    if c >= 1:
                        dve.wait_ge(bvt_done, c)
                    scaled_out(n + 2, t512[2 + (c + 1) % 2])
            cross_rq(1)
            b_onorm(MC - 1)
            cross_max(1, 0, after=lambda b: b_lo(MC - 1) if b == 1 else None)
            cross_p(1, 0, 0)
            cross_max(1, 1, after=lambda b: cross_p(1, 0, 1) if b == 1 else None)
            cross_p(1, 1, 0)
            cross_p(1, 1, 1)
            cross_lo(1, 0)
            cross_lo(1, 1)
            x_phase(T_OUT[1], R_N2 + 8)
            x_rinv(3)
            ffn(1, None)

        @block.tensor
        def _(pe):
            def mm(out_, a, b, start=True, stop=True):
                return nc.tensor.matmul(out_, a, b, start=start, stop=stop)

            pe.wait_ge(con_in, 16)
            pe.wait_ge(prm_in, 16)
            nc.tensor.transpose(PS[:, 2, 0:N_PRM], prm[0:N_PRM, :], ident[0:N_PRM, 0:N_PRM]).then_inc(prm_t, 1)
            pe.wait_ge(mem_in, 16)

            def tr_group(g, blocks):
                if g >= 4:
                    pe.wait_ge(tr_free, g - 3)
                for j, b in enumerate(blocks):
                    last = nc.tensor.transpose(PS[:, 4 + g % 4, j * P:(j + 1) * P], b, ident)
                last.then_inc(tr_done, 1)

            for g in range(4):
                tr_group(g, [m_st[:, t, (2 * g + a) * P:(2 * g + a + 1) * P] for a in range(2) for t in range(MT_TILES)])

            def tile(i, n0, hi, lo, nk=8, step=2, ready=None, n=SEQ, after=None):
                sl = n0 % SPLIT
                pe.wait_ge(w_split, i * step + (n0 + 1))
                if not (isinstance(i, int) and n0 + step * i < 2):
                    pe.wait_ge(dense_free, i * step + (n0 - 1))
                for k in range(nk):
                    if ready:
                        for s_, v_ in ready(k):
                            pe.wait_ge(s_, v_)
                    for j, (w, a) in enumerate(((w_hi, hi), (w_hi, lo), (w_lo, hi))):
                        last = mm(PS[:, sl, 0:n], w[:, sl, k], a(k), start=(k == 0 and j == 0), stop=(k == nk - 1 and j == 2))
                    if k == nk - 1:
                        last.then_inc(dense_done, 1)
                    if after:
                        after(k)

            def h_tile(n0, i=0, ready=None, after=None):
                tile(i, n0, lambda k: Hh[:, k], lambda k: Hl[:, k], ready=ready, after=after)

            def a_tile(n0, i=0, ready=None, nk=8, after=None):
                tile(i, n0, lambda k: Ah[:, k], lambda k: Al[:, k], nk=nk, ready=ready, after=after)

            def m_tile(n):
                l = n // 4

                def part(A):
                    return lambda k: A[:, 4 * l:4 * l + 4].rearrange("p a n -> p (a n)")[:, k * MEM:(k + 1) * MEM]
                tile(0, n, part(Ah), part(Al), n=MEM, ready=(lambda k: [(mg_ready, 8 * l + k + 1)]) if n % 4 == 0 else None)

            pe.wait_ge(set_done, 4)
            for k in range(KD):
                pe.wait_ge(msq_done, k // 2 + 1)
                last = mm(PS[:, 3, 0:MEM], ones[:], msq[:, k], start=k == 0, stop=k == KD - 1)
            last.then_inc(mss_done, 1)
            m_tile(0)
            m_tile(1)
            m_tile(2)
            pe.wait_ge(x_in, 16)
            for k in range(4):
                tr_group(4 + k, [x_st[:, t, k * P:(k + 1) * P] for t in range(NT)])
            m_tile(3)
            m_tile(4)
            for k in range(4, 8):
                tr_group(4 + k, [x_st[:, t, k * P:(k + 1) * P] for t in range(NT)])
            m_tile(5)
            m_tile(6)
            m_tile(7)

            def k_ss(l):
                pe.wait_ge(ksq, l + 1)
                pe.wait_ge(tr_free, 12)
                mm(PS[:, 4 + l], bdiag, kvs[:]).then_inc(kss, 1)
                pe.wait_ge(dense_free, 4 * l + 4)
                if l == 1:
                    pe.wait_ge(vtr_out, 1)
                for t in range(MT_TILES):
                    for c in range(2):
                        last = nc.tensor.transpose(PS[:, 6, (2 * t + c) * P:(2 * t + c + 1) * P],
                                                   kv[:, l, 2 + c, t * P:(t + 1) * P], ident)
                last.then_inc(vtr, 1)

            def x_ss(i):
                pe.wait_ge(xsq_used, KD * (i + 1))
                mm(PS[:, SS_BANK], ones[:], acc[:]).then_inc(ss_done, 1)

            h_tile(T_GATE, ready=lambda k: [(h_ready, k + 1)])
            x_ss(0)
            k_ss(0)
            pe.wait_ge(lam_d, 1)
            pe.wait_ge(gx_ready, 1)
            mm(PS[:, 2, 2:4], rotm, gx[:, 3:5])
            mm(PS[:, 2, 0:1], ones[0:1, :], lame[0:1, 0:1]).then_inc(lam_b, 1)
            h_tile(T_QK)
            h_tile(T_QK + 1)
            k_ss(1)
            pe.wait_ge(dense_free, T_GATE + 1)
            pe.wait_ge(lam_d, 2)
            mm(PS[0:MH, 2], cn[0:8, C_GSEL:C_GSEL + MH], tmp[4][0:8, 0:SEQ])
            mm(PS[0:MH, 3], cn[0:8, C_GSEL + MH:C_GSEL + 2 * MH], tmp[4][0:8, 0:SEQ]).then_inc(gsel_done, 1)
            with pe.Fori(1, QKC // 2) as i:
                h_tile(T_QK, i)
                h_tile(T_QK + 1, i)
            pe.wait_ge(a_ready, 1)
            for i, row in enumerate((tmp[6], tmp[0])):
                for t in range(NT):
                    last = nc.tensor.transpose(PS[:, 3, (i * NT + t) * MH:(i * NT + t + 1) * MH], row[0:MH, t * P:(t + 1) * P],
                                               ident[0:MH, 0:MH])
            last.then_inc(at_done, 1)

            def v_tr(c):
                pe.wait_ge(dense_free, T_V + c + 1)
                if c >= 2:
                    pe.wait_ge(v_ready, V_DONE[c - 2])
                for t in range(NT):
                    last = nc.tensor.transpose(PS[:, 4 + c % 2, t * P:(t + 1) * P], tmp[4 + c % 2][:, t * P:(t + 1) * P], ident)
                last.then_inc(vT_done, 1)

            for c in range(MC):
                h_tile(T_V + c)
                if c >= 1:
                    v_tr(c - 1)
            v_tr(MC - 1)

            def head_scores(h):
                f, (c, r) = FULL[h], HALF[h]
                if h == 0:
                    pe.wait_ge(v_ready, V_DONE[-1])
                    pe.wait_ge(v_ones, 1)
                    pe.wait_ge(at_ready, 1)
                    pe.wait_ge(qk_ready, QKC)
                else:
                    pe.wait_ge(hn_low, 2 * h)
                mm(PS[:, 4], cn[0:MH, C_SEL + h * P:C_SEL + (h + 1) * P], Mrow[:]).then_inc(mbc_done, 1)
                for s in range(NT):
                    o = PS[:, S_BANK[s], s * P:SEQ]
                    if h >= 1:
                        pe.wait_ge(p_ready, NT * (h - 1) + s + 1)
                    if h >= 1 and s >= 2:
                        pe.wait_ge(hout, 2 * h)
                    mm(o, QK[:, MC + f, s * P:(s + 1) * P], QK[:, f, s * P:SEQ], stop=False)
                    mm(o, QK[r:r + 64, MC + c, s * P:(s + 1) * P], QK[r:r + 64, c, s * P:SEQ], start=False).then_inc(s_done, 1)

            def head_pv(h):
                pe.wait_ge(wt_ready, 7 * h + 7)
                if h >= 1:
                    pe.wait_ge(hn_high, 2 * h)
                for t in range(NT):
                    pe.wait_ge(p_ready, NT * h + t + 1)
                    for s in range(t + 1):
                        last = mm(PS[:, 4 + t // 2, (t % 2) * VW:(t % 2 + 1) * VW], WT[:, W_OFF[s] + (t - s) * P:W_OFF[s] + (t - s + 1) * P],
                                  V[:, s, h * VW:(h + 1) * VW], start=s == 0, stop=s == t)
                    if t % 2:
                        last.then_inc(num_done, 1)

            def head_turn(h, t):
                f, (c, r) = FULL[h], HALF[h]
                if t == 0:
                    pe.wait_ge(hn_low, 2 * h + 2)
                    pe.wait_ge(p_ready, NT * (h + 1))
                if t == 2:
                    pe.wait_ge(hn_high, 2 * h + 2)
                o = t512[3 + t // 2][:, (t % 2) * MHD:(t % 2 + 1) * MHD]
                full, half = f * P - h * MHD, c * P + r - h * MHD
                nc.tensor.transpose(PS[:, 6, t * P:(t + 1) * P], o[:, full:full + P], ident)
                last = mm(PS[r:r + 64, 7, t * P:(t + 1) * P], o[:, half:half + 64], ident)
                if t == NT - 1:
                    last.then_inc(ht_done, 1)

            def cross_ss(l, c, t):
                if t == 0:
                    pe.wait_ge(xq_sq, 2 * l + c + 1)
                if c == 0 and t == 0:
                    if l == 0:
                        pe.wait_ge(p_ready, NT * (MH - 1) + 1)
                    else:
                        pe.wait_ge(dense_free, T_OUT[1])
                j = 2 * (NT * c + t)
                last = mm(PS[:, XSS_BANK[l], j:j + 2], X_SQ[l][c][:, t * P:(t + 1) * P], half_sel)
                if c == 1 and t == NT - 1:
                    last.then_inc(xq_ss, 1)

            fill = [T_XA, T_XA + 1] + [T_O + c for c in range(MC)]
            for h in range(MH):
                def in_first(k):
                    if h == MH - 1 and 3 <= k < 3 + NT:
                        cross_ss(0, 0, k - 3)
                        cross_ss(0, 1, k - 3)

                def in_second(k):
                    if k >= KD - NT:
                        head_turn(h, k - (KD - NT))

                head_scores(h)
                h_tile(fill[2 * h], after=in_first)
                head_pv(h)
                h_tile(fill[2 * h + 1], after=in_second)

            def cross_s(l, c, after=None):
                for b in range(4):
                    r = 64 * (b // 2)
                    for a in range(2):
                        t = 2 * (b % 2) + a
                        last = mm(PS[:, X_BANK[c] + b, a * MEM:(a + 1) * MEM], (xqA, xqB)[l][r:r + 64, c, t * P:(t + 1) * P],
                                  xk[r:r + 64, l, c])
                    last.then_inc(xs_done, 1)
                    if after:
                        after(b)

            def cross_t(l, c):
                i = 2 * l + c
                for b in range(4):
                    hd, mt = b // 2, b % 2
                    pe.wait_ge(xp_second if hd else xp_ready, 4 * i + 4)
                    for t in range(NT):
                        last = nc.tensor.transpose(PS[:, X_BANK[c] + b, t * P:(t + 1) * P],
                                                   X_P[l][c][4 * hd + t][:, mt * P:(mt + 1) * P], ident)
                    last.then_inc(xpt_done, 1)

            def cross_pv(l, c):
                i = 2 * l + c
                for hd in range(2):
                    for mt in range(MT_TILES):
                        pe.wait_ge(xpt_ready, 4 * i + 2 * hd + mt + 1)
                        last = mm(PS[64 * hd:64 * hd + 64, X_BANK[c]], xv[:, l, mt, (2 * c + hd) * 64:(2 * c + hd + 1) * 64],
                                  X_PT[l][c][2 * hd + mt], start=mt == 0, stop=mt == 1)
                last.then_inc(xo_done, 1)

            pe.wait_ge(dense_free, T_OUT[0])
            pe.wait_ge(xq_std, 1)
            pe.wait_ge(p_ready, NT * MH)
            cross_s(0, 0)
            pe.wait_ge(hn_low, 2 * MH)
            pe.wait_ge(hn_high, 2 * MH)
            pe.wait_ge(hout, 2 * MH)
            cross_s(0, 1)
            cross_t(0, 0)
            cross_t(0, 1)
            cross_pv(0, 0)
            cross_pv(0, 1)

            def out_proj(l, ready):
                a_tile(T_OUT[l], ready=ready)
                a_tile(T_OUT[l] + 1)
                with pe.Fori(1, KD // 2) as i:
                    a_tile(T_OUT[l], i)
                    a_tile(T_OUT[l] + 1, i)

            pe.wait_ge(xo_ready, 1)
            out_proj(0, lambda k: [(mix_lo, k + 1)] if k < MC else [(xo_ready, k - MC + 1)])

            def out_t(k, t):
                if t == 0:
                    pe.wait_ge(dense_free, seg_base(1, 2) + 2 * SEG[2][1] + k + 1)
                    if k >= 2:
                        pe.wait_ge(ot_out, k - 1)
                last = nc.tensor.transpose(PS[:, 2 + k % 2, t * P:(t + 1) * P], xT[:, k, t * P:(t + 1) * P], ident)
                if t == NT - 1:
                    last.then_inc(ot_done, 1)

            def ffn(l):
                n0 = l * HC
                for s, (h0, nh) in enumerate(SEG):
                    base = seg_base(l, s)
                    if s == 0:
                        h_tile(base, ready=lambda k: [(h_ready, KD * (2 * l + 1) + k + 1)])
                        x_ss(2 * l + 1)
                        h_tile(base + 1)
                    with pe.Fori(1 if s == 0 else 0, nh) as i:
                        h_tile(base, i)
                        h_tile(base + 1, i)
                    down = base + 2 * nh
                    a_tile(down, nk=nh, ready=lambda k: [(f_ready, n0 + h0 + k + 1)])
                    a_tile(down + 1, nk=nh)
                    if l == 1 and s == len(SEG) - 1:
                        for j in range(2, KD):
                            a_tile(down + j, nk=nh, after=lambda k: out_t(j - 2, k - 1) if 1 <= k <= NT else None)
                        break
                    with pe.Fori(1, KD // 2) as i:
                        a_tile(down, i, nk=nh)
                        a_tile(down + 1, i, nk=nh)

            ffn(0)

            h_tile(T_B, ready=lambda k: [(h_ready, 2 * KD + k + 1)])
            x_ss(2)
            h_tile(T_B + 1)
            h_tile(T_B + 2)

            def b_ss(c, a, t):
                if a == 0 and t == 0:
                    pe.wait_ge(bsq, c + 1)
                    if c >= 1:
                        pe.wait_ge(bexp, 8 * c)
                j = 2 * (NT * a + t)
                last = mm(PS[:, 6, j:j + 2], QS[:, a, t * P:(t + 1) * P], half_sel)
                if a == 1 and t == NT - 1:
                    last.then_inc(bss, 1)

            def b_kbc(c, t):
                if t == 0:
                    pe.wait_ge(bn_ready, c + 1)
                last = nc.tensor.transpose(PS[:, 7, t * P:(t + 1) * P], t512[4][:, t * P:(t + 1) * P], ident)
                if t == NT - 1:
                    last.then_inc(bk_bc, 1)

            def b_oturn(c, t):
                if t == 0:
                    pe.wait_ge(bo_norm, c + 1)
                last = nc.tensor.transpose(PS[:, 5, t * P:(t + 1) * P], t512[5][:, t * P:(t + 1) * P], ident)
                if t == NT - 1:
                    last.then_inc(bo_turn, 1)

            def b_vt(c, t):
                if t == 0:
                    pe.wait_ge(dense_free, T_B + 3 * c + 3)
                    if c >= 1:
                        pe.wait_ge(bat_ready, 4 * c)
                last = nc.tensor.transpose(PS[:, 2, t * P:(t + 1) * P], t512[2 + c % 2][:, t * P:(t + 1) * P], ident)
                if t == NT - 1:
                    last.then_inc(bvt_done, 1)

            def b_s(c, u):
                t, b = NT - 1 - u, 6 - 2 * (u % 2)
                if u == 0:
                    pe.wait_ge(bkr, c + 1)
                if u == 1 and c >= 1:
                    pe.wait_ge(bmix_lo, c)
                if u >= 2:
                    pe.wait_ge(bexp, 2 * (4 * c + u - 2) + 2)
                for hd in range(2):
                    r = 64 * hd
                    last = mm(PS[:, b + hd, 0:(t + 1) * P], QR[r:r + 64, 0, t * P:(t + 1) * P], QR[r:r + 64, 1, 0:(t + 1) * P])
                last.then_inc(bs_done, 1)

            def b_t(c, u):
                t = NT - 1 - u
                pe.wait_ge(ba_ready, 4 * c + u + 1)
                if u == 0:
                    pe.wait_ge(bv_ready, c + 1)
                if u >= 2:
                    pe.wait_ge(bat_ready, 4 * c + u - 1)
                for k in range(t + 1):
                    last = nc.tensor.transpose(PS[:, 2 + u % 2, k * P:(k + 1) * P], PB[:, 0, W_OFF[u] + k * P:W_OFF[u] + (k + 1) * P], ident)
                last.then_inc(bt_done, 1)

            def b_pv(c):
                pe.wait_ge(bat_ready, 4 * c + 4)
                for t in range(NT):
                    for k in range(t + 1):
                        last = mm(PS[:, 4, t * P:(t + 1) * P], ATB[:, k, t * P:(t + 1) * P], VB[:, c % 2, k], start=k == 0, stop=k == t)
                last.then_inc(bpv, 1)

            for c in range(MC):
                n = T_B + 3 * (c + 1)

                def in_q(k):
                    if c >= 1 and k < 2:
                        b_t(c - 1, 2 + k)
                    if k < NT:
                        b_ss(c, 0, k)
                        b_ss(c, 1, k)
                    if c >= 1 and k == 3:
                        b_pv(c - 1)

                def in_k(k):
                    if k < 2:
                        b_kbc(c, 2 * k)
                        b_kbc(c, 2 * k + 1)
                    if c >= 1 and k in (2, 3):
                        b_oturn(c - 1, 2 * (k - 2))
                        b_oturn(c - 1, 2 * (k - 2) + 1)
                    if k == 4:
                        b_s(c, 0)
                    if k in (5, 6):
                        b_vt(c, 2 * (k - 5))
                        b_vt(c, 2 * (k - 5) + 1)
                    if k == 7:
                        b_s(c, 1)

                def in_v(k):
                    if k in (0, 2):
                        b_s(c, 2 + k // 2)
                    if k in (5, 6):
                        b_t(c, k - 5)

                h_tile(n, after=in_q)
                h_tile(n + 1, after=in_k)
                if c + 1 < MC:
                    h_tile(n + 2, after=in_v)
                else:
                    for t in range(NT):
                        cross_ss(1, 0, t)
                    b_s(c, 2)
                    b_s(c, 3)
                    b_t(c, 0)
                    b_t(c, 1)
                    for t in range(NT):
                        cross_ss(1, 1, t)
                    b_t(c, 2)
                    b_t(c, 3)

            b_pv(MC - 1)

            def last_turn(b):
                for t in range(NT):
                    if b == 1:
                        b_oturn(MC - 1, t)

            pe.wait_ge(bat_ready, 4 * MC)
            pe.wait_ge(xq_std, 2)
            cross_s(1, 0, after=last_turn)
            pe.wait_ge(bmix_lo, MC)
            cross_s(1, 1)
            cross_t(1, 0)
            cross_t(1, 1)
            cross_pv(1, 0)
            cross_pv(1, 1)
            pe.wait_ge(xo_ready, 3)
            out_proj(1, lambda k: [(bmix_lo, k + 1)] if k < MC else [(xo_ready, k - MC + 3)])
            ffn(1)
            for k in range(KD - 2, KD):
                for t in range(NT):
                    out_t(k, t)


_INS = ['x', 'mem', 'positions', 'w_out', 'w_mem_kv', 'w_gate_up', 'w_down', 'a_w_in', 'a_gate_b', 'b_w_in',
        'b_lambda']
_ROWS = ['norm1', 'norm2', 'mem_norm', 'a_conv_w', 'a_conv_b', 'a_head_norm', 'b_subln']
_HALF_ROWS = ['xq_norm', 'xk_norm', 'b_q_norm', 'b_k_norm']
_OUTS = [((1, SEQ, D), 'float32')]


def kernel(**inputs):
    import numpy as _np
    import concourse.bacc as _bacc
    from concourse import mybir as _mybir
    from concourse.bass_utils import run_bass_kernel_spmd as _run

    nc = _bacc.Bacc("TRN2", target_bir_lowering=False, num_devices=1)
    arrays, args = {}, []
    for name in _INS:
        a = _np.ascontiguousarray(inputs[name])
        arrays[f"in_{name}_dram"] = a
        args.append(nc.dram_tensor(f"in_{name}_dram", a.shape, _mybir.dt.from_np(a.dtype), kind="ExternalInput").ap())
    rows = [_np.asarray(inputs[name]).reshape(-1, P) for name in _ROWS]
    rows += [_np.concatenate([_np.asarray(inputs[name])] * 2, axis=1) for name in _HALF_ROWS]
    for name, a in (("rows", _np.ascontiguousarray(_np.concatenate(rows))), ("constants", constants())):
        arrays[f"in_{name}_dram"] = a
        args.append(nc.dram_tensor(f"in_{name}_dram", a.shape, _mybir.dt.from_np(a.dtype), kind="ExternalInput").ap())
    for i, (shape, dtype) in enumerate(_OUTS):
        dt = _mybir.dt.from_np(_np.dtype(dtype))
        args.append(nc.dram_tensor(f"out_{i}_dram", shape, dt, kind="ExternalOutput").ap())
    hybrid_trunk(nc, *args)
    r = _run(nc, [arrays], core_ids=[0])
    return r.results[0]["out_0_dram"]
```
